# Optimizing a Trainium2 kernel written in Bass

```python
import math
import jax, jax.numpy as jnp
from jax import lax
import numpy as np

D_MODEL = 1024
BATCH = 1
SEQ = 2048
DEPTH = 1

BRANCH_WIDTH = D_MODEL // 2
N_BRANCHES = 3
GDN_HEAD_DIM = 128
GDN_HEADS = BRANCH_WIDTH // GDN_HEAD_DIM
GDN_CONV = 4
GDN_CHUNK = 64
DIFF_V_DIM = 128
DIFF_QK_DIM = DIFF_V_DIM // 2
DIFF_HEADS = BRANCH_WIDTH // DIFF_V_DIM
Q_BLOCK = 128
SC_CONV = 3
NORM_EPS = 1e-6
NEG_INF = -1e30
SPLIT_SIZES = (3 * BRANCH_WIDTH, BRANCH_WIDTH, GDN_HEADS, GDN_HEADS,
               BRANCH_WIDTH, BRANCH_WIDTH, BRANCH_WIDTH, BRANCH_WIDTH,
               BRANCH_WIDTH, BRANCH_WIDTH, BRANCH_WIDTH, BRANCH_WIDTH,
               N_BRANCHES * D_MODEL)
N_IN = sum(SPLIT_SIZES)

kernel_name = 'hybrid_gdn_diffattn_shortconv_block'

def rms_norm(x, w, eps=NORM_EPS):
    x32 = x.astype(jnp.float32)
    y = x32 * lax.rsqrt(jnp.mean(x32 * x32, axis=-1, keepdims=True) + eps)
    return (y * w.astype(jnp.float32)).astype(x.dtype)

def l2_normalize(x, eps=1e-6):
    return x * lax.rsqrt(jnp.sum(x * x, axis=-1, keepdims=True) + eps)

def causal_dwconv(x, w):
    k_width, channels = w.shape
    return lax.conv_general_dilated(
        x, w[:, None, :].astype(x.dtype), window_strides=(1,),
        padding=[(k_width - 1, 0)], dimension_numbers=('NWC', 'WIO', 'NWC'),
        feature_group_count=channels)

def alibi_slopes(n_heads):
    return 2.0 ** (-8.0 * jnp.arange(1, n_heads + 1, dtype=jnp.float32) / n_heads)

def chunk_gated_delta_rule(q, k, v, g, beta):
    bsz, seq, n_h, dk = q.shape
    dv = v.shape[-1]
    n_chunks = seq // GDN_CHUNK

    def to_chunks(t):
        t = jnp.moveaxis(t, 2, 1)
        return t.reshape(t.shape[:2] + (n_chunks, GDN_CHUNK) + t.shape[3:])

    q = to_chunks(q * dk ** -0.5)
    k = to_chunks(k)
    v = to_chunks(v)
    beta = to_chunks(beta)
    g = jnp.cumsum(to_chunks(g), axis=-1)
    k_beta = k * beta[..., None]
    v_beta = v * beta[..., None]
    tril = jnp.tril(jnp.ones((GDN_CHUNK, GDN_CHUNK), bool))
    strict = jnp.tril(jnp.ones((GDN_CHUNK, GDN_CHUNK), bool), k=-1)
    decay = jnp.exp(jnp.where(tril, g[..., :, None] - g[..., None, :], -jnp.inf))
    lower = jnp.where(strict, jnp.einsum('bhncd,bhnsd->bhncs', k_beta, k) * decay, 0.0)
    unit_lower = lower + jnp.eye(GDN_CHUNK, dtype=lower.dtype)
    rhs = jnp.concatenate([v_beta, k_beta * jnp.exp(g)[..., None]], axis=-1)
    sol = lax.linalg.triangular_solve(unit_lower, rhs, left_side=True, lower=True,
                                      unit_diagonal=True)
    u, w = sol[..., :dv], sol[..., dv:]
    qk = jnp.where(tril, jnp.einsum('bhncd,bhnsd->bhncs', q, k) * decay, 0.0)
    q_dec = q * jnp.exp(g)[..., None]
    k_dec = k * jnp.exp(g[..., -1:] - g)[..., None]
    g_last = jnp.exp(g[..., -1])

    def step(state, inp):
        u_c, w_c, qk_c, q_dec_c, k_dec_c, g_last_c = inp
        v_new = u_c - w_c @ state
        o_c = q_dec_c @ state + qk_c @ v_new
        state = state * g_last_c[..., None, None] + jnp.einsum('bhcd,bhce->bhde', k_dec_c, v_new)
        return state, o_c

    xs = [jnp.moveaxis(t, 2, 0) for t in (u, w, qk, q_dec, k_dec, g_last)]
    state0 = jnp.zeros((bsz, n_h, dk, dv), jnp.float32)
    _, o = lax.scan(step, state0, tuple(xs))
    o = jnp.moveaxis(o, 0, 2).reshape(bsz, n_h, seq, dv)
    return jnp.moveaxis(o, 1, 2)

def gdn_branch(qkv_pre, z, b, a, conv_w, a_log, dt_bias, norm_w):
    bsz, seq, _ = qkv_pre.shape
    qkv = jax.nn.silu(causal_dwconv(qkv_pre, conv_w)).astype(jnp.float32)
    q, k, v = jnp.split(qkv, 3, axis=-1)
    shp = (bsz, seq, GDN_HEADS, GDN_HEAD_DIM)
    q = l2_normalize(q.reshape(shp))
    k = l2_normalize(k.reshape(shp))
    v = v.reshape(shp)
    beta = jax.nn.sigmoid(b.astype(jnp.float32))
    g = -jnp.exp(a_log.astype(jnp.float32)) * jax.nn.softplus(
        a.astype(jnp.float32) + dt_bias.astype(jnp.float32))
    o = chunk_gated_delta_rule(q, k, v, g, beta)
    o = rms_norm(o.astype(z.dtype), norm_w).reshape(bsz, seq, BRANCH_WIDTH)
    return o * jax.nn.silu(z)

def diff_attn_branch(q, k, v, z, lam_vecs, lam_init, norm_w):
    bsz, seq, _ = q.shape
    q = (q * DIFF_QK_DIM ** -0.5).reshape(bsz, seq, DIFF_HEADS, 2, DIFF_QK_DIM)
    k = k.reshape(bsz, seq, DIFF_HEADS, 2, DIFF_QK_DIM)
    v = v.reshape(bsz, seq, DIFF_HEADS, DIFF_V_DIM)
    lv = lam_vecs.astype(jnp.float32)
    lam = jnp.exp(jnp.sum(lv[0] * lv[1])) - jnp.exp(jnp.sum(lv[2] * lv[3])) + lam_init
    slopes = alibi_slopes(DIFF_HEADS)
    n_blk = seq // Q_BLOCK
    q_blocks = jnp.moveaxis(q.reshape(bsz, n_blk, Q_BLOCK, DIFF_HEADS, 2, DIFF_QK_DIM), 1, 0)
    k_pos = jnp.arange(seq)

    def attend(args):
        q_blk, blk = args
        s = jnp.einsum('bqhmd,bkhmd->bhmqk', q_blk, k).astype(jnp.float32)
        dist = (blk * Q_BLOCK + jnp.arange(Q_BLOCK))[:, None] - k_pos[None, :]
        s = jnp.where(dist >= 0, s - slopes[:, None, None, None] * dist.astype(jnp.float32), NEG_INF)
        p = jax.nn.softmax(s, axis=-1)
        p = p[:, :, 0] - lam * p[:, :, 1]
        return jnp.einsum('bhqk,bkhe->bqhe', p.astype(v.dtype), v)

    o = lax.map(attend, (q_blocks, jnp.arange(n_blk)))
    o = jnp.moveaxis(o, 0, 1).reshape(bsz, seq, DIFF_HEADS, DIFF_V_DIM)
    o = (rms_norm(o, norm_w) * (1.0 - lam_init)).reshape(bsz, seq, BRANCH_WIDTH)
    return o * jax.nn.silu(z)

def short_conv_branch(b, c, x_in, z, conv_w):
    y = b * causal_dwconv(c * x_in, conv_w)
    return y * jax.nn.silu(z)

def setup_inputs(seed: int = 0) -> dict:
    key = jax.random.key(seed)
    ks = jax.random.split(key, 14)
    f32 = jnp.float32
    nrm = jax.random.normal
    x = nrm(ks[0], (BATCH, SEQ, D_MODEL), f32)
    norm_pre = 1.0 + 0.1 * nrm(ks[1], (DEPTH, D_MODEL), f32)
    norm_post = 1.0 + 0.1 * nrm(ks[2], (DEPTH, D_MODEL), f32)
    w_in = nrm(ks[3], (DEPTH, D_MODEL, N_IN), f32) * D_MODEL ** -0.5
    gdn_conv_w = nrm(ks[4], (DEPTH, GDN_CONV, 3 * BRANCH_WIDTH), f32) * GDN_CONV ** -0.5
    gdn_a_log = jnp.log(jax.random.uniform(ks[5], (DEPTH, GDN_HEADS), f32, 1.0, 16.0))
    dt = jnp.exp(jax.random.uniform(ks[6], (DEPTH, GDN_HEADS), f32, math.log(1e-3), math.log(1e-1)))
    gdn_dt_bias = dt + jnp.log(-jnp.expm1(-dt))
    gdn_norm_w = 1.0 + 0.1 * nrm(ks[7], (DEPTH, GDN_HEAD_DIM), f32)
    diff_lambda = 0.1 * nrm(ks[8], (DEPTH, 4, DIFF_QK_DIM), f32)
    diff_norm_w = 1.0 + 0.1 * nrm(ks[9], (DEPTH, DIFF_V_DIM), f32)
    sc_conv_w = nrm(ks[10], (DEPTH, SC_CONV, BRANCH_WIDTH), f32) * SC_CONV ** -0.5
    w_branch = nrm(ks[11], (DEPTH, N_BRANCHES, BRANCH_WIDTH, D_MODEL), f32) * BRANCH_WIDTH ** -0.5
    w_out = nrm(ks[12], (DEPTH, D_MODEL, D_MODEL), f32) * D_MODEL ** -0.5
    return {'x': x, 'norm_pre': norm_pre, 'norm_post': norm_post, 'w_in': w_in,
            'gdn_conv_w': gdn_conv_w, 'gdn_a_log': gdn_a_log, 'gdn_dt_bias': gdn_dt_bias,
            'gdn_norm_w': gdn_norm_w, 'diff_lambda': diff_lambda, 'diff_norm_w': diff_norm_w,
            'sc_conv_w': sc_conv_w, 'w_branch': w_branch, 'w_out': w_out}

def reference(x, norm_pre, norm_post, w_in, gdn_conv_w, gdn_a_log, gdn_dt_bias, gdn_norm_w,
              diff_lambda, diff_norm_w, sc_conv_w, w_branch, w_out):
    bsz, seq, _ = x.shape
    split_at = [int(i) for i in np.cumsum(SPLIT_SIZES)[:-1]]
    for l in range(DEPTH):
        h = rms_norm(x, norm_pre[l])
        proj = jnp.einsum('bld,dn->bln', h, w_in[l])
        (gdn_qkv, gdn_z, gdn_b, gdn_a, d_q, d_k, d_v, d_z,
         s_b, s_c, s_x, s_z, merge_logits) = jnp.split(proj, split_at, axis=-1)
        lam_init = 0.8 - 0.6 * math.exp(-0.3 * l)
        y_a = gdn_branch(gdn_qkv, gdn_z, gdn_b, gdn_a, gdn_conv_w[l], gdn_a_log[l],
                         gdn_dt_bias[l], gdn_norm_w[l])
        y_b = diff_attn_branch(d_q, d_k, d_v, d_z, diff_lambda[l], lam_init, diff_norm_w[l])
        y_c = short_conv_branch(s_b, s_c, s_x, s_z, sc_conv_w[l])
        branches = jnp.stack([y_a, y_b, y_c], axis=2)
        branch_out = jnp.einsum('blkw,kwd->blkd', branches, w_branch[l])
        gates = jax.nn.sigmoid(merge_logits.reshape(bsz, seq, N_BRANCHES, D_MODEL))
        merged = jnp.sum(gates * branch_out, axis=2)
        out = jnp.einsum('bld,de->ble', merged, w_out[l])
        x = x + rms_norm(out, norm_post[l])
    return x


_drawn_inputs = setup_inputs


def setup_inputs(seed=0):
    import zlib

    import numpy as np

    out = dict(_drawn_inputs(seed))
    spreads = {}
    factors = {}
    for name, (base, spread) in spreads.items():
        noise = np.random.default_rng([zlib.crc32(name.encode()), seed]).standard_normal(out[name].shape)
        drawn = base * np.exp(spread * noise) if base else spread * noise
        out[name] = __import__('jax').numpy.asarray(drawn.astype(out[name].dtype))
    for name, factor in factors.items():
        out[name] = (out[name] * factor).astype(out[name].dtype)
    return out
```

```python
from contextlib import ExitStack
import math

import concourse.bass as bass
from concourse import mybir

F32 = mybir.dt.float32
F32R = mybir.dt.float32r
ALU = mybir.AluOpType
ACT = mybir.ActivationFunctionType
AX = mybir.AxisListType
ds = bass.ds

P = 128
SEQ = 2048
D = 1024
KT = D // P
BW = D // 2
H = BW // P
N_IN = 9224
RB = 4
R = SEQ // RB
TILES = SEQ // P
GDN_CONV = 4
SC_CONV = 3
EPS = 1e-6
NEG = -1e30
LAM_INIT = 0.8 - 0.6 * math.exp(-0.3 * 0)
MAPS = 2
QK_DIM = P // MAPS
AHEAD = 4
LEVELS = 7
SLOPE = 2.0 ** (-8.0 / H)
UNITS = 72
CONSTS = 34
TURNS = RB + sum(b // RB + 1 for b in range(TILES))
SCORES = MAPS * sum(b // RB + 1 for b in range(TILES))

COL_B = 4 * BW
COL_ATT = COL_B + 2 * H
COL_SC = COL_ATT + 4 * BW
COL_MERGE = COL_SC + 4 * BW
U_GDN, U_ZA, U_Q, U_K, U_V, U_ZB = 0, 12, 16, 20, 24, 28
U_SAVED = 32
VEC_CONV, VEC_SC = 0, GDN_CONV * 12
VEC_GDN = VEC_SC + SC_CONV * H
VEC_DIFF = VEC_GDN + 1
VECS = VEC_DIFF + 1


def hybrid_block(nc, x, norm_pre, norm_post, w_in, gdn_conv_w, gdn_a_log, gdn_dt_bias, gdn_norm_w,
                 diff_lambda, diff_norm_w, sc_conv_w, w_branch, w_out, out):
    with ExitStack() as ctx:
        def sem(name):
            return ctx.enter_context(nc.semaphore(name))

        counted = []

        def counter(name):
            counted.append(sem(name))
            return counted[-1]

        def counters(name, n):
            return [counter(f"{name}{i}") for i in range(n)]

        def past(n):
            return n + 1

        BASE = (nc.sbuf_base + 63) // 64 * 64
        LIMIT = nc.sbuf_usable_end

        class Room:

            def __init__(self, at):
                self.at = at

            def __call__(self, name, shape, dt=F32):
                n = 4
                for s in shape[1:]:
                    n *= s
                t = nc.alloc_sbuf_tensor_at(name, shape, dt, offset=self.at)
                self.at += (n + 63) // 64 * 64
                assert self.at <= LIMIT, (name, self.at, LIMIT)
                return t

        keep = Room(BASE)
        ident = keep("ident", [P, P])
        ones = keep("ones", [P, P])
        triu = keep("triu", [P, P])
        mask_lo = keep("mask_lo", [P, P])
        mask_up = keep("mask_up", [P, P])
        pair_t = keep("pair_t", [P, LEVELS, P])
        pair1 = keep("pair1", [P, P])
        eps = keep("eps", [P, 1])
        vec_rows = keep("vec_rows", [VECS, P])
        vec = keep("vec", [P, VECS])
        diff_w = keep("diff_w", [P, 1])
        lam_in = keep("lam_in", [P, 4, QK_DIM])
        lam_s = keep("lam_s", [P, 4])
        neg_lam = keep("neg_lam", [P, 1])
        head_in = keep("head_in", [P, 2, H])
        tab = {n: keep("tab_" + n, [P, TILES * H]) for n in
               ("g", "cum", "beta", "beta_ecum", "k_decay", "e_last", "t0", "t1")}
        ROOM = keep.at

        room = Room(ROOM)
        hT_hi = room("hT_hi", [P, KT, SEQ], F32R)
        hT_lo = room("hT_lo", [P, KT, SEQ], F32R)
        w_hi = [room(f"w_hi{p}", [P, KT, P], F32R) for p in range(2)]
        w_lo = [room(f"w_lo{p}", [P, KT, P], F32R) for p in range(2)]
        w_raw = [room(f"w_raw{p}", [P, KT, P]) for p in range(2)]
        AFTER_W = room.at
        stage = [room(f"stage{p}", [P, SEQ]) for p in range(2)]
        raw = [room(f"raw{p}", [P, GDN_CONV - 1 + SEQ]) for p in range(2)]
        conv = room("conv", [P, SEQ])
        abT = raw[0]
        room = Room(AFTER_W)
        x_in = [room(f"x_in{q}", [P, D]) for q in range(4)]
        x_junk = room("x_junk", [P, D])
        pre_w = room("pre_w", [P, D])
        x_stat = room("x_stat", [P, 4, 3])

        room = Room(ROOM)
        qkv_in = [room(f"qkv_in{p}", [P, 3 * H, P]) for p in range(2)]
        za_in = [room(f"za_in{p}", [P, H, P]) for p in range(2)]
        sq_qk = room("sq_qk", [P, 2 * H, P])
        rs_qk = room("rs_qk", [P, 2 * H, P])
        qkn = room("qkn", [P, 2 * H, P])
        g_tri = room("g_tri", [P, H, P])
        dec = room("dec", [P, 2, H, P])
        e_cum = room("e_cum", [P, H, P])
        q_dec = room("q_dec", [P, H, P])
        low = room("low", [P, H, P])
        lowT = room("lowT", [P, H, P])
        pairM = room("pairM", [P, LEVELS, H, P])
        T = room("T", [P, H, P])
        Tt = room("Tt", [P, H, P])
        X = room("X", [P, H, P])
        qk_m = room("qk_m", [P, H, P])
        k_beta = room("k_beta", [P, H, P])
        k_dec = room("k_dec", [P, H, P])
        v_beta = room("v_beta", [P, H, P])
        U = room("U", [P, H, P])
        WT = room("WT", [P, H, P])
        v_new = room("v_new", [P, H, P])
        state = room("state", [P, H, P])
        state_d = room("state_d", [P, H, P])
        sq_o = room("sq_o", [P, H, P])
        rs_o = room("rs_o", [P, H, P])
        y_a = room("y_a", [P, H, P])

        room = Room(ROOM)
        q_in = [room(f"q_in{p}", [P, SEQ]) for p in range(2)]
        k_in = [room(f"k_in{p}", [P, SEQ]) for p in range(2)]
        v_in = [room(f"v_in{p}", [P, SEQ]) for p in range(2)]
        zb_in = [room(f"zb_in{p}", [P, SEQ]) for p in range(2)]
        v_rows = room("v_rows", [P, TILES, P])
        REACH = SEQ
        dist = room("dist", [P, REACH])
        bias = [room(f"bias{p}", [P, REACH]) for p in range(2)]
        s_buf = [room(f"s_buf{n}", [P, MAPS, SEQ]) for n in range(AHEAD)]
        probsT = [room(f"probsT{p}", [P, TILES, P]) for p in range(2)]
        top = [room(f"top{n}", [P, MAPS, RB]) for n in range(AHEAD)]
        top_all = [room(f"top_all{n}", [P, MAPS]) for n in range(AHEAD)]
        neg_top = [room(f"neg_top{n}", [P, MAPS]) for n in range(AHEAD)]
        den = [room(f"den{n}", [P, MAPS]) for n in range(AHEAD)]
        inv = [room(f"inv{n}", [P, MAPS]) for n in range(AHEAD)]
        sub_w = [room(f"sub_w{n}", [P, 1]) for n in range(AHEAD)]
        sq_b = room("sq_b", [P, R])
        rs_b = room("rs_b", [P, R])
        y_b = room("y_b", [P, R])

        room = Room(ROOM)
        wo_hi = room("wo_hi", [P, KT, D], F32R)
        wo_lo = room("wo_lo", [P, KT, D], F32R)
        y_hi = room("y_hi", [P, 3 * H, R], F32R)
        y_lo = room("y_lo", [P, 3 * H, R], F32R)
        m_hi = room("m_hi", [P, KT, R], F32R)
        m_lo = room("m_lo", [P, KT, R], F32R)
        y_in = room("y_in", [P, H, R])
        wb_in = [room(f"wb_in{p}", [P, H, P]) for p in range(2)]
        wb_hi = [room(f"wb_hi{p}", [P, H, P], F32R) for p in range(3)]
        wb_lo = [room(f"wb_lo{p}", [P, H, P], F32R) for p in range(3)]
        gate_in = [room(f"gate_in{p}", [P, R]) for p in range(3)]
        gated = [room(f"gated{p}", [P, R]) for p in range(3)]
        x_res = [room(f"x_res{p}", [P, D]) for p in range(2)]
        o_norm = room("o_norm", [P, D])
        post_w = room("post_w", [P, D])
        o_stat = room("o_stat", [P, 5])

        bank = [ctx.enter_context(nc.psum_tensor(f"bank{i}", [P, R], F32)) for i in range(8)]

        def hp(t):
            return t[:, :].rearrange("p (h c) -> p h c", h=H)

        saved = nc.dram_tensor("saved", (U_SAVED, P, SEQ), F32, kind="Internal").ap()
        gates = nc.dram_tensor("gates", (3 * KT, P, SEQ), F32, kind="Internal").ap()
        y_all = nc.dram_tensor("y_all", (3 * H, P, SEQ), F32, kind="Internal").ap()

        x_rows = x.rearrange("b (t p) d -> (b t) p d", p=P)
        out_rows = out.rearrange("b (t p) d -> (b t) p d", p=P)
        w_cols = w_in.rearrange("l (k p) n -> p (l k) n", p=P)
        wb_rows = w_branch.rearrange("l b (k p) n -> p (l b k) n", p=P)
        wo_rows = w_out.rearrange("l (k p) n -> p (l k) n", p=P)

        vec_loaded = sem("vec_loaded")
        const_step = sem("const_step")
        vec_turned = sem("vec_turned")
        vec_ready = sem("vec_ready")
        lam_step = sem("lam_step")
        x_loaded = counters("x_loaded", 4)
        x_used = counters("x_used", 4)
        x_square = counter("x_square")
        x_root = counter("x_root")
        x_inv = counter("x_inv")
        x_scaled = counter("x_scaled")
        h_hi_done = counter("h_hi_done")
        h_lo_done = counters("h_lo_done", 2)
        w_loaded = counters("w_loaded", 2)
        w_hi_done = counter("w_hi_done")
        w_ready = counter("w_ready")
        block_done = counters("block_done", 2)
        bank_free = counters("bank_free", RB)
        raw_zero = sem("raw_zero")
        conv_step = counter("conv_step")
        conv_done = counters("conv_done", 2)
        silu_done = counter("silu_done")
        stored = counters("stored", 2)
        sc_step = counter("sc_step")
        sc_conv_done = counter("sc_conv_done")
        yc_done = counter("yc_done")
        ab_turned = sem("ab_turned")
        tab_v = sem("tab_v")
        tab_a = sem("tab_a")
        tab_mm = sem("tab_mm")
        through = [sem(f"through{i}") for i in range(3)]

        phase_engines = 5

        def arrive(e, phase):
            e.drain().then_inc(through[phase], 1)
            e.wait_ge(through[phase], phase_engines)

        pool_waited = sem("pool_waited")
        dve_waited = sem("dve_waited")

        def wait_apart(e, waited):
            e.sem_inc(waited, 1)

        qkv_loaded = counters("qkv_loaded", 2)
        G = {n: counter("g_" + n) for n in (
            "sq", "ss", "rs_ln", "rs", "tri", "cumb", "qkn", "mask", "ecum", "diff", "decay", "decay_b",
            "qdec", "kk", "turn", "masked", "rows", "lowt", "lowt_sb", "t0", "pair",
            "T", "x_mm", "x_sb", "y_mm", "t_new", "u_mm", "uw_sb", "ws", "vnew", "o_mm", "s_mm", "sdec",
            "state", "zero")}
        N = {n: counter("n_" + n) for n in ("sqo", "sso", "rso_ln", "rso", "on", "y_stored")}
        g_y = counters("g_y", 2)
        A = {n: counter("a_" + n) for n in (
            "dist", "score", "top", "negtop", "exp", "inv", "subw",
            "sub", "probs", "turn")}
        a_pv = counters("a_pv", AHEAD)
        a_y = counters("a_y", 2)
        head_loaded = counters("head_loaded", 2)
        score_free = counters("score_free", 4)
        turn_free = counters("turn_free", 2)
        M = {n: counter("m_" + n) for n in (
            "wo_loaded", "wo_hi", "wo_lo", "post", "y_loaded", "y_hi", "y_lo", "wb_hi",
            "sum1", "sum2", "hi", "lo", "out_mm", "sq", "ss", "root", "inv", "normed", "done")}
        wb_free = counters("m_wb_free", 2)
        mm_done = counters("m_mm_done", 3)
        gated_done = counters("m_gated_done", 6)
        wb_loaded = counters("m_wb_loaded", 2)
        gate_loaded = counters("m_gate_loaded", 3)
        x_res_loaded = counters("m_x_loaded", 2)
        out_stored = counters("m_out_stored", 2)

        block = ctx.enter_context(nc.Block())

        @block.sync
        def _(sp):
            for s in counted:
                sp.sem_inc(s, 1)
            sp.dma_start(vec_rows[VEC_CONV:VEC_SC, :],
                         gdn_conv_w.rearrange("l k (t c) -> (l k t) c", c=P)).then_inc(vec_loaded, 16)
            sp.dma_start(vec_rows[VEC_SC:VEC_GDN, :],
                         sc_conv_w.rearrange("l k (t c) -> (l k t) c", c=P)).then_inc(vec_loaded, 16)
            sp.dma_start(vec_rows[VEC_GDN:VEC_DIFF, :], gdn_norm_w).then_inc(vec_loaded, 16)
            sp.dma_start(vec_rows[VEC_DIFF:VECS, :], diff_norm_w).then_inc(vec_loaded, 16)
            sp.dma_start(pre_w[:, :], norm_pre[0].partition_broadcast(P)).then_inc(vec_loaded, 16)
            sp.dma_start(lam_in[:, :, :], diff_lambda[0].partition_broadcast(P)).then_inc(vec_loaded, 16)
            sp.dma_start(head_in[:, 0, :], gdn_a_log[0].partition_broadcast(P)).then_inc(vec_loaded, 16)
            sp.dma_start(head_in[:, 1, :], gdn_dt_bias[0].partition_broadcast(P)).then_inc(vec_loaded, 16)
            with sp.Fori(0, TILES // 4) as i:
                for q in range(4):
                    sp.wait_ge(x_used[q], past(i))
                    sp.dma_start(x_in[q][:, :], x_rows[ds(4 * i + q, 1), :, :].rearrange("o p d -> p (o d)")
                                 ).then_inc(x_loaded[q], 16)

            def load_w(p, nth, col):
                sp.wait_ge(w_ready, past(nth))
                sp.dma_start(w_raw[p][:, :, :], w_cols[:, :, col]).then_inc(w_loaded[p], 16)

            load_w(0, 0, slice(0, P))
            load_w(1, 0, slice(P, 2 * P))
            with sp.Fori(1, U_Q // 2) as i:
                for p in range(2):
                    load_w(p, 2 * i + p - 1, ds(i * (2 * P) + p * P, P))
            with sp.Fori(U_Q // 2, U_SAVED // 2) as i:
                for p in range(2):
                    load_w(p, 2 * i + p - 1, ds(i * (2 * P) + (p * P + 2 * H), P))
            with sp.Fori(0, H) as j:
                for n, part in enumerate((1, 2, 0, 3)):
                    load_w(n % 2, 4 * j + (U_SAVED + n - 1), ds(j * P + (COL_SC + part * BW), P))
            with sp.Fori(0, 3 * KT // 2) as i:
                for p in range(2):
                    load_w(p, 2 * i + (U_SAVED + 4 * H + p - 1), ds(i * (2 * P) + (COL_MERGE + p * P), P))
            load_w(0, U_SAVED + 4 * H + 3 * KT - 1, slice(COL_B, COL_B + P))
            arrive(sp, 0)

            with sp.Fori(0, TILES // 2) as i:
                for p in range(2):
                    sp.wait_ge(g_y[p], past(i))
                    rows = ds(i * (2 * P) + p * P, P)
                    sp.dma_start(qkv_in[p][:, :, :], saved[U_GDN:U_ZA, :, rows].rearrange("u p r -> p u r")
                                 ).then_inc(qkv_loaded[p], 16)
                    sp.dma_start(za_in[p][:, :, :], saved[U_ZA:U_Q, :, rows].rearrange("u p r -> p u r")
                                 ).then_inc(qkv_loaded[p], 16)
            arrive(sp, 1)

            with sp.Fori(0, H // 2) as i:
                for p in range(2):
                    sp.wait_ge(a_y[p], past(RB * i))
                    for t, u in ((v_in, U_V), (q_in, U_Q), (k_in, U_K), (zb_in, U_ZB)):
                        sp.dma_start(t[p][:, :], saved[ds(2 * i + (u + p), 1), :, :].rearrange("o p r -> p (o r)")
                                     ).then_inc(head_loaded[p], 16)
            arrive(sp, 2)

            sp.dma_start(post_w[:, :], norm_post[0].partition_broadcast(P)).then_inc(M["post"], 16)

            def load_y(r, b):
                sp.wait_ge(M["y_lo"], past(3 * r + b))
                sp.dma_start(y_in[:, :, :], y_all[H * b:H * (b + 1), :, ds(r * R, R)].rearrange("u p r -> p u r")
                             ).then_inc(M["y_loaded"], 16)

            def merge_loads(r, first=False, last=False):
                rows = ds(r * R, R)
                for d in range(KT):
                    for b in range(3):
                        n = 3 * d + b
                        sp.wait_ge(wb_free[n % 2], past(12 * r + n // 2))
                        sp.dma_start(wb_in[n % 2][:, :, :], wb_rows[:, H * b:H * (b + 1), d * P:(d + 1) * P]
                                     ).then_inc(wb_loaded[n % 2], 16)
                        sp.wait_ge(gated_done[3 * ((d + 1) % 2) + b], past(RB * r + (d + 1) // 2))
                        sp.dma_start(gate_in[b][:, :], gates[b * KT + d, :, rows]).then_inc(gate_loaded[b], 16)
                    if first:
                        sp.wait_ge(M["wo_lo"], past(max(0, d - 1)))
                        sp.dma_start(x_res[d % 2][:, :], wo_rows[:, d, :]).then_inc(M["wo_loaded"], 16)
                if first:
                    sp.wait_ge(M["wo_lo"], past(KT))
                if not last:
                    load_y(r + 1, 0)
                for t in range(RB):
                    sp.wait_ge(out_stored[t % 2], past(32 * r + 16 * (t // 2)))
                    sp.dma_start(x_res[t % 2][:, :], x_rows[ds(RB * r + t, 1), :, :].rearrange("o p d -> p (o d)")
                                 ).then_inc(x_res_loaded[t % 2], 16)
                    if not last and t in (1, 2):
                        load_y(r + 1, t)

            for b in range(3):
                load_y(0, b)
            merge_loads(0, first=True)
            with sp.Fori(1, RB - 1) as r:
                merge_loads(r)
            merge_loads(RB - 1, last=True)
            for p in range(2):
                sp.wait_ge(out_stored[p], past(16 * TILES // 2))

        @block.gpsimd
        def _(pool):
            def sum_last(pool, r, d):
                pool.wait_ge(M["sum1"], past(KT * r + d + 1))
                pool.wait_ge(gated_done[3 * (d % 2) + 2], past(KT // 2 * r + d // 2 + 1))
                pool.tensor_tensor(gated[0][:, :], gated[1][:, :], gated[2][:, :], ALU.add
                                   ).then_inc(M["sum2"], 1)

            n_const = [0]

            def const(ins):
                n_const[0] += 1
                ins.then_inc(const_step, 1)
                pool.wait_ge(const_step, n_const[0])

            def select(t, op, fill, base, cm, pattern):
                const(pool.affine_select(out=t, in_=t, compare_op=op, fill=fill, base=base,
                                         channel_multiplier=cm, pattern=pattern))

            const(pool.memset(ident[:, :], 0.0))
            select(ident[:, :], ALU.not_equal, 1.0, 0, 1, [[-1, P]])
            const(pool.memset(ones[:, :], 1.0))
            const(pool.memset(eps[:, :], EPS))
            const(pool.memset(triu[:, :], 1.0))
            select(triu[:, :], ALU.is_ge, 0.0, 0, -1, [[1, P]])
            const(pool.memset(mask_lo[:, :], 0.0))
            select(mask_lo[:, :], ALU.is_ge, NEG, -1, 1, [[-1, P]])
            const(pool.memset(mask_up[:, :], 0.0))
            select(mask_up[:, :], ALU.is_ge, NEG, 0, -1, [[1, P]])
            const(pool.memset(pair_t[:, :, :], 0.0))
            for lv in range(LEVELS):
                s = 1 << lv
                odd = pair_t[:, lv, :].rearrange("p (a two s) -> p a two s", two=2, s=s)[:, :, 1, :]
                const(pool.memset(odd, 1.0))
                select(odd, ALU.is_ge, 0.0, 0, 1, [[-2 * s, P // (2 * s)], [0, s]])
                select(odd, ALU.is_ge, 0.0, s - 1, -1, [[2 * s, P // (2 * s)], [0, s]])
            const(pool.memset(pair1[:, :], 0.0))
            even = pair1[:, :].rearrange("p (a two) -> p a two", two=2)[:, :, 0]
            select(even, ALU.not_equal, 1.0, -1, 1, [[-2, P // 2]])

            assert n_const[0] == CONSTS

            def split_w(u, k, p):
                pool.wait_ge(w_loaded[p], past(16 * k + 16))
                pool.wait_ge(block_done[p], past(RB * k))
                wait_apart(pool, pool_waited)
                pool.tensor_copy(w_hi[p][:, :, :], w_raw[p][:, :, :]).then_inc(w_hi_done, 1)
                pool.wait_ge(w_hi_done, past(u + 1))
                pool.tensor_tensor(w_lo[p][:, :, :], w_raw[p][:, :, :], w_hi[p][:, :, :].bitcast(F32),
                                   ALU.subtract).then_inc(w_ready, 1)

            with pool.Fori(0, UNITS // 2) as i:
                for p in range(2):
                    split_w(2 * i + p, i, p)
            split_w(UNITS, UNITS // 2, 0)
            arrive(pool, 0)

            def bc(t, c):
                return t[:, ds(H * c, H)].rearrange("p (h o) -> p h o", o=1).to_broadcast([P, H, P])

            def per_head(m):
                return m.rearrange("p (o c) -> p o c", o=1).to_broadcast([P, H, P])

            pool.memset(state[:, :, :], 0.0).then_inc(G["zero"], 1)
            with pool.Fori(0, TILES // 2) as i:
                for p in range(2):
                    c = 2 * i + p
                    pool.wait_ge(G["cumb"], past(c))
                    pool.tensor_tensor(g_tri[:, :, :], per_head(triu[:, :]), bc(tab["g"], c), ALU.mult
                                       ).then_inc(G["tri"], 1)
                    pool.wait_ge(G["masked"], past(2 * c))
                    pool.tensor_tensor(dec[:, 0, :, :], per_head(mask_lo[:, :]), bc(tab["cum"], c), ALU.add
                                       ).then_inc(G["mask"], 1)
                    pool.tensor_tensor(dec[:, 1, :, :], per_head(mask_up[:, :]), bc(tab["cum"], c),
                                       ALU.subtract).then_inc(G["mask"], 1)
                    pool.wait_ge(G["decay"], past(c + 1))
                    pool.tensor_tensor(dec[:, 0, :, :], dec[:, 0, :, :], bc(tab["beta"], c), ALU.mult
                                       ).then_inc(G["decay_b"], 1)
                    pool.wait_ge(G["ecum"], past(c + 1))
                    pool.wait_ge(G["qkn"], past(2 * c + 1))
                    pool.wait_ge(G["o_mm"], past(c))
                    pool.tensor_tensor(q_dec[:, :, :], qkn[:, 0:H, :], e_cum[:, :, :], ALU.mult
                                       ).then_inc(G["qdec"], 1)
                    pool.wait_ge(G["masked"], past(2 * c + 1))
                    pool.wait_ge(G["uw_sb"], past(2 * c))
                    pool.tensor_tensor(T[:, :, :], low[:, :, :], per_head(pair1[:, :]), ALU.mult
                                       ).then_inc(G["t0"], 1)
                    pool.wait_ge(G["t0"], past(2 * c + 1))
                    pool.tensor_tensor(T[:, :, :], per_head(ident[:, :]), T[:, :, :], ALU.subtract
                                       ).then_inc(G["t0"], 1)
                    pool.wait_ge(G["lowt_sb"], past(c + 1))
                    for lv in range(LEVELS):
                        pool.tensor_tensor(pairM[:, lv, :, :], lowT[:, :, :], per_head(pair_t[:, lv, :]),
                                           ALU.mult).then_inc(G["pair"], 1)
                        if lv == 0:
                            pool.wait_ge(G["pair"], past(LEVELS * c + 1))
                            pool.tensor_tensor(Tt[:, :, :], per_head(ident[:, :]), pairM[:, 0, :, :],
                                               ALU.subtract).then_inc(G["T"], 1)
                    pool.wait_ge(G["state"], past(c))
                    pool.wait_ge(G["zero"], past(1))
                    pool.tensor_tensor(state_d[:, :, :], state[:, :, :], bc(tab["e_last"], c), ALU.mult
                                       ).then_inc(G["sdec"], 1)
            arrive(pool, 1)

            pool.iota(dist[:, :], [[1, SEQ]], base=P - SEQ, channel_multiplier=-1,
                      allow_small_or_imprecise_dtypes=True).then_inc(A["dist"], 1)
            pool.wait_ge(A["dist"], past(1))
            pool.affine_select(out=dist[:, :], in_=dist[:, :], compare_op=ALU.is_ge, fill=NEG, base=SEQ - P,
                               channel_multiplier=1, pattern=[[-1, SEQ]]).then_inc(A["dist"], 1)
            with pool.Fori(0, H // MAPS) as i:
                for p in range(2):
                    h = 2 * i + p
                    pool.wait_ge(A["dist"], past(2 * h + 2))
                    wait_apart(pool, pool_waited)
                    pool.tensor_scalar(dist[:, :], dist[:, :], SLOPE, 1.0, ALU.mult, ALU.mult
                                       ).then_inc(A["dist"], 1)
                    pool.wait_ge(A["dist"], past(2 * h + 3))
                    pool.wait_ge(a_y[p], past(RB * i))
                    wait_apart(pool, pool_waited)
                    pool.tensor_scalar(bias[p][:, :], dist[:, :], 1.0, 1.0, ALU.mult, ALU.mult
                                       ).then_inc(A["dist"], 1)
            arrive(pool, 2)

            with pool.Fori(0, RB) as r:
                for d in range(KT):
                    for b in range(3):
                        n = 3 * d + b
                        pool.wait_ge(M["wb_hi"], past(24 * r + n + 1))
                        pool.tensor_tensor(wb_lo[n % 3][:, :, :], wb_in[n % 2][:, :, :],
                                           wb_hi[n % 3][:, :, :].bitcast(F32), ALU.subtract
                                           ).then_inc(wb_free[n % 2], 1)
                        if b == 1 and d:
                            sum_last(pool, r, d - 1)
                sum_last(pool, r, KT - 1)

        @block.tensor
        def _(pe):
            def mm3(dst, lhs, rhs, first, last):
                pe.matmul(dst, lhs[0], rhs[0], start=first, stop=False)
                pe.matmul(dst, lhs[0], rhs[1], start=False, stop=False)
                return pe.matmul(dst, lhs[1], rhs[0], start=False, stop=last)

            pe.wait_ge(const_step, CONSTS)
            pe.wait_ge(vec_loaded, 128)
            pe.transpose(bank[0][:, 0:VECS], vec_rows[:, :], ident[0:VECS, 0:VECS]).then_inc(vec_turned, 1)
            with pe.Fori(0, TILES // 4) as i:
                for q in range(4):
                    p = q % 2
                    pe.wait_ge(x_scaled, past(4 * i + q + 1))
                    pe.wait_ge(h_lo_done[p], past(2 * (2 * i + q // 2)))
                    for k in range(KT):
                        last = pe.transpose(bank[4 + 2 * p + k // 4][:, (k % 4) * P:(k % 4 + 1) * P],
                                            x_in[q][:, k * P:(k + 1) * P], ident[:, :])
                    last.then_inc(x_used[q], 1)
            pe.wait_ge(h_lo_done[0], past(TILES))
            pe.wait_ge(h_lo_done[1], past(TILES))
            pe.wait_ge(vec_ready, 1)

            def project(u, p):
                pe.wait_ge(w_ready, past(u + 1))
                for rb in range(RB):
                    pe.wait_ge(bank_free[rb], past(u))
                    for k in range(KT):
                        cols = slice(rb * R, (rb + 1) * R)
                        last = mm3(bank[rb][:, :], (w_hi[p][:, k, :], w_lo[p][:, k, :]),
                                   (hT_hi[:, k, cols], hT_lo[:, k, cols]), k == 0, k == KT - 1)
                    last.then_inc(block_done[p], 1)

            with pe.Fori(0, UNITS // 2) as i:
                for p in range(2):
                    project(2 * i + p, p)
            project(UNITS, 0)

            pe.wait_ge(bank_free[RB - 1], past(UNITS + 1))
            for c in range(TILES):
                last = pe.transpose(bank[4][:, 2 * H * c:2 * H * (c + 1)], abT[0:2 * H, c * P:(c + 1) * P],
                                    ident[0:2 * H, 0:2 * H])
            last.then_inc(ab_turned, 1)
            pe.wait_ge(tab_v, 3)
            pe.matmul(bank[5][:, 0:TILES * H], triu[:, :], tab["g"][:, :], start=True, stop=True)
            pe.matmul(bank[5][:, TILES * H:2 * TILES * H], ones[:, :], tab["g"][:, :], start=True, stop=True
                      ).then_inc(tab_mm, 1)
            arrive(pe, 0)

            def heads(dst, lhs, rhs):
                for h in range(H):
                    last = pe.matmul(dst[:, h * P:(h + 1) * P], lhs[:, h, :], rhs[:, h, :],
                                     start=True, stop=True)
                return last

            with pe.Fori(0, TILES // 2) as i:
                for p in range(2):
                    c = 2 * i + p
                    kn = qkn[:, H:2 * H, :]
                    pe.wait_ge(G["sq"], past(c + 1))
                    pe.wait_ge(G["uw_sb"], past(2 * c))
                    pe.matmul(bank[0][:, :], ones[:, :], sq_qk[:, 0:H, :], start=True, stop=True)
                    pe.matmul(bank[1][:, :], ones[:, :], sq_qk[:, H:2 * H, :], start=True, stop=True
                              ).then_inc(G["ss"], 1)
                    pe.wait_ge(G["tri"], past(c + 1))
                    pe.wait_ge(G["vnew"], past(c))
                    pe.matmul(bank[2][:, :], ones[:, :], g_tri[:, :, :], start=True, stop=True
                              ).then_inc(G["cumb"], 1)
                    pe.wait_ge(G["state"], past(c))
                    for h in range(H):
                        last = pe.transpose(bank[4][:, h * P:(h + 1) * P], qkv_in[p][:, 2 * H + h, :],
                                            ident[:, :])
                    last.then_inc(G["turn"], 1)
                    pe.wait_ge(G["qkn"], past(2 * c + 2))
                    pe.wait_ge(N["on"], past(c))
                    for h in range(H):
                        last = pe.transpose(bank[3][:, h * P:(h + 1) * P], kn[:, h, :], ident[:, :])
                    last.then_inc(G["turn"], 1)
                    heads(bank[0], kn, kn).then_inc(G["kk"], 1)
                    pe.wait_ge(G["qkn"], past(2 * c + 1))
                    heads(bank[1], kn, qkn[:, 0:H, :]).then_inc(G["kk"], 1)
                    pe.wait_ge(G["masked"], past(2 * c + 1))
                    for h in range(H):
                        last = pe.transpose(bank[0][:, h * P:(h + 1) * P], low[:, h, :], ident[:, :])
                    last.then_inc(G["lowt"], 1)
                    for lv in range(1, LEVELS):
                        n = (LEVELS - 1) * c + lv
                        pe.wait_ge(G["pair"], past(LEVELS * c + lv + 1))
                        if lv == 1:
                            pe.wait_ge(G["t0"], past(2 * c + 2))
                            pe.wait_ge(G["T"], past(c + 1))
                            pe.wait_ge(G["decay"], past(c + 1))
                            pe.wait_ge(G["rows"], past(3 * c + 3))
                            pe.wait_ge(G["rows"], past(3 * c + 1))
                        else:
                            pe.wait_ge(G["t_new"], past(n - 1))
                        heads(bank[2], pairM[:, lv, :, :], T).then_inc(G["x_mm"], 1)
                        pe.wait_ge(G["x_sb"], past(n))
                        heads(bank[3], X, Tt).then_inc(G["y_mm"], 1)
                        if lv < LEVELS - 1:
                            heads(bank[4], Tt, X).then_inc(G["y_mm"], 1)
                    pe.wait_ge(G["t_new"], past((LEVELS - 1) * (c + 1)))
                    pe.wait_ge(G["lowt_sb"], past(c + 1))
                    heads(bank[0], Tt, v_beta).then_inc(G["u_mm"], 1)
                    pe.wait_ge(G["masked"], past(2 * c + 2))
                    pe.wait_ge(G["rows"], past(3 * c + 2))
                    heads(bank[1], k_beta, Tt).then_inc(G["u_mm"], 1)
                    pe.wait_ge(G["uw_sb"], past(2 * c + 2))
                    pe.wait_ge(G["state"], past(c))
                    pe.wait_ge(G["zero"], past(1))
                    heads(bank[2], WT, state).then_inc(G["ws"], 1)
                    pe.wait_ge(G["qdec"], past(c + 1))
                    pe.wait_ge(G["vnew"], past(c + 1))
                    for h in range(H):
                        cols = slice(h * P, (h + 1) * P)
                        pe.matmul(bank[3][:, cols], state[:, h, :], q_dec[:, h, :], start=True, stop=False)
                        last = pe.matmul(bank[3][:, cols], v_new[:, h, :], qk_m[:, h, :],
                                         start=False, stop=True)
                    last.then_inc(G["o_mm"], 1)
                    heads(bank[4], k_dec, v_new).then_inc(G["s_mm"], 1)
                    pe.wait_ge(N["sqo"], past(c + 1))
                    pe.wait_ge(N["rso_ln"], past(c))
                    pe.matmul(bank[5][:, :], ones[:, :], sq_o[:, :, :], start=True, stop=True
                              ).then_inc(N["sso"], 1)
            arrive(pe, 1)

            with pe.Fori(0, H // MAPS) as i:
                for p in range(2):
                    h = 2 * i + p
                    turns = [0]
                    scored = [0]

                    def turn_bank():
                        n = turns[0]
                        turns[0] += 1
                        pe.wait_ge(turn_free[n % 2], past(TURNS // 2 * h + n // 2))
                        return bank[4 + n % 2]

                    def scores(b):
                        for m in range(MAPS):
                            part = slice(m * QK_DIM, (m + 1) * QK_DIM)
                            for g in range(b // RB + 1):
                                n = scored[0]
                                scored[0] += 1
                                w = min(R, (b + 1) * P - g * R)
                                pe.wait_ge(score_free[n % 4], past(SCORES // 4 * h + n // 4))
                                pe.matmul(bank[n % 4][:, 0:w], q_in[p][part, b * P:(b + 1) * P],
                                          k_in[p][part, g * R:g * R + w], start=True, stop=True
                                          ).then_inc(A["score"], 1)

                    def square_sum(sb):
                        pe.wait_ge(N["sqo"], past(TILES + RB * h + sb + 1))
                        pe.wait_ge(N["rso_ln"], past(TILES + RB * h + sb))
                        pe.matmul(bank[7][:, :], ones[:, :], sq_b[:, :], start=True, stop=True
                                  ).then_inc(N["sso"], 1)

                    pe.wait_ge(head_loaded[p], past(64 * i + 64))
                    scores(0)
                    scores(1)
                    for g in range(RB):
                        dst = turn_bank()
                        for k in range(RB):
                            last = pe.transpose(dst[:, k * P:(k + 1) * P],
                                                v_in[p][:, (g * RB + k) * P:(g * RB + k + 1) * P], ident[:, :])
                        last.then_inc(A["turn"], 1)
                    for b in range(TILES):
                        if b + 2 < TILES:
                            scores(b + 2)
                        if b and b % RB == 0:
                            square_sum(b // RB - 1)
                        pe.wait_ge(A["probs"], past(TILES * h + b + 1))
                        for g in range(b // RB + 1):
                            dst = turn_bank()
                            for k in range(min(RB, b + 1 - g * RB)):
                                kb = g * RB + k
                                last = pe.transpose(dst[:, k * P:(k + 1) * P],
                                                    s_buf[b % AHEAD][:, 0, kb * P:(kb + 1) * P], ident[:, :])
                            last.then_inc(A["turn"], 1)
                        n = turns[0] - 1
                        pe.wait_ge(turn_free[n % 2], past(TURNS // 2 * h + n // 2 + 1))
                        pe.wait_ge(turn_free[(n + 1) % 2], past(TURNS // 2 * h + (n - 1) // 2 + 1))
                        if b % RB == 0:
                            pe.wait_ge(N["on"], past(TILES + RB * h + b // RB))
                        for kb in range(b + 1):
                            last = pe.matmul(bank[6][:, (b % RB) * P:(b % RB + 1) * P], v_rows[:, kb, :],
                                             probsT[b % 2][:, kb, :], start=(kb == 0), stop=(kb == b))
                        last.then_inc(a_pv[b % AHEAD], 1)
                    square_sum(RB - 1)
                    assert turns[0] == TURNS and scored[0] == SCORES
            arrive(pe, 2)

            with pe.Fori(0, RB) as r:
                pe.wait_ge(M["y_lo"], past(3 * r + 3))
                for d in range(KT):
                    for b in range(3):
                        n = 3 * d + b
                        half = KT // 2
                        pe.wait_ge(wb_free[n % 2], past(12 * r + n // 2 + 1))
                        pe.wait_ge(gated_done[n % 6], past(half * r + n // 6))
                        if n < 2:
                            pe.wait_ge(M["normed"], past(RB * r))
                        for k in range(H):
                            last = mm3(bank[n % 6][:, :], (wb_hi[n % 3][:, k, :], wb_lo[n % 3][:, k, :]),
                                       (y_hi[:, H * b + k, :], y_lo[:, H * b + k, :]), k == 0, k == H - 1)
                        last.then_inc(mm_done[n % 3], 1)
                pe.wait_ge(M["lo"], past(KT * r + KT))
                pe.wait_ge(M["wo_lo"], past(KT))
                for t in range(RB):
                    pe.wait_ge(M["normed"], past(RB * r + max(0, t - 1)))
                    for nb in range(2):
                        dst = bank[(6, 0)[t % 2] + nb]
                        for d in range(KT):
                            rows = slice(t * P, (t + 1) * P)
                            cols = slice(nb * R, (nb + 1) * R)
                            last = mm3(dst[:, :], (m_hi[:, d, rows], m_lo[:, d, rows]),
                                       (wo_hi[:, d, cols], wo_lo[:, d, cols]), d == 0, d == KT - 1)
                        last.then_inc(M["out_mm"], 1)

        @block.scalar
        def _(act):
            def f(out_, in_, func, **kw):
                return act.activation(out_, in_, func, **kw)

            def row_scale(i, q):
                t = 4 * i + q
                act.wait_ge(x_loaded[q], past(16 * i + 16))
                f(x_junk[:, :], x_in[q][:, :], ACT.Square, accum_out=x_stat[:, q, 0:1]).then_inc(x_square, 1)
                act.wait_ge(x_square, past(t + 1))
                f(x_stat[:, q, 1:2], x_stat[:, q, 0:1], ACT.Sqrt, scale=1.0 / D, bias=eps[:, 0:1]
                  ).then_inc(x_root, 1)

            def take_hi(i, q):
                t = 4 * i + q
                act.wait_ge(x_used[q], past(i + 1))
                for n in range(2):
                    f(hT_hi[:, 4 * n:4 * n + 4, ds(t * P, P)], hp(bank[4 + 2 * (q % 2) + n]), ACT.Copy
                      ).then_inc(h_hi_done, 1)

            act.wait_ge(const_step, CONSTS)
            row_scale(0, 0)
            row_scale(0, 1)
            with act.Fori(0, TILES // 4 - 1) as i:
                for q in range(4):
                    take_hi(i, q)
                    row_scale(i + (q + 2) // 4, (q + 2) % 4)
            last_i = TILES // 4 - 1
            for q in range(4):
                take_hi(last_i, q)
                if q < 2:
                    row_scale(last_i, q + 2)
            act.wait_ge(vec_loaded, 128)
            act.wait_ge(lam_step, 2)
            f(lam_s[:, 2:4], lam_s[:, 0:2], ACT.Exp).then_inc(lam_step, 1)

            def store(dst, p, sp_sem, value):
                act.wait_ge(sp_sem, past(value))
                act.dma_start(dst, stage[p][:, :]).then_inc(stored[p], 16)

            def one(t, u):
                return t[ds(u, 1), :, :].rearrange("o p r -> p (o r)")

            act.wait_ge(h_lo_done[1], past(TILES))
            act.wait_ge(raw_zero, 1)
            with act.Fori(0, U_ZA // 2) as i:
                for p in range(2):
                    u = 2 * i + p
                    act.wait_ge(conv_done[p], past(i))
                    for rb in range(RB):
                        act.wait_ge(block_done[p], past(RB * i + rb + 1))
                        f(raw[p][:, GDN_CONV - 1 + rb * R:GDN_CONV - 1 + (rb + 1) * R], bank[rb][:, :], ACT.Copy
                          ).then_inc(bank_free[rb], 1)
                    act.wait_ge(conv_done[p], past(i + 1))
                    f(stage[p][:, :], stage[p][:, :], ACT.Silu).then_inc(silu_done, 1)
                    store(one(saved, u), p, silu_done, u + 1)

            def direct(first, count, func, dst, dst_first, stored_before, **kw):
                with act.Fori(0, count // 2) as i:
                    for p in range(2):
                        k = i + first // 2
                        act.wait_ge(stored[p], past(16 * (i + stored_before[p])))
                        for rb in range(RB):
                            act.wait_ge(block_done[p], past(RB * k + rb + 1))
                            f(stage[p][:, rb * R:(rb + 1) * R], bank[rb][:, :], func, **kw
                              ).then_inc(bank_free[rb], 1)
                        store(one(dst, 2 * i + (dst_first + p)), p, bank_free[RB - 1], 2 * i + (first + p + 1))

            for first, count, func, kw in ((U_ZA, 4, ACT.Silu, {}), (U_Q, 4, ACT.Copy, {"scale": QK_DIM ** -0.5}),
                                           (U_K, 8, ACT.Copy, {}), (U_ZB, 4, ACT.Silu, {})):
                direct(first, count, func, saved, first, (first // 2, first // 2), **kw)
            with act.Fori(0, H) as j:
                k = 2 * j + U_SAVED // 2
                act.wait_ge(sc_conv_done, past(j))
                for rb in range(RB):
                    act.wait_ge(block_done[0], past(RB * k + rb + 1))
                    f(raw[0][:, GDN_CONV - 1 + rb * R:GDN_CONV - 1 + (rb + 1) * R], bank[rb][:, :], ACT.Copy
                      ).then_inc(bank_free[rb], 1)
                act.wait_ge(yc_done, past(j))
                act.wait_ge(stored[1], past(16 * (U_SAVED // 2)))
                for rb in range(RB):
                    act.wait_ge(block_done[1], past(RB * k + (RB + rb + 1)))
                    f(stage[1][:, rb * R:(rb + 1) * R], bank[rb][:, :], ACT.Silu).then_inc(bank_free[rb], 1)
                act.wait_ge(yc_done, past(j + 1))
                act.dma_start(one(y_all, j + 2 * H), stage[0][:, :]).then_inc(stored[0], 16)
            direct(U_SAVED + 4 * H, 3 * KT, ACT.Sigmoid, gates, 0, (U_SAVED // 2 + H, U_SAVED // 2))
            for rb in range(RB):
                act.wait_ge(block_done[0], past(RB * (UNITS // 2) + rb + 1))
                f(abT[0:2 * H, rb * R:(rb + 1) * R], bank[rb][0:2 * H, :], ACT.Copy).then_inc(bank_free[rb], 1)

            ab = bank[4][:, 0:TILES * 2 * H].rearrange("p (c e) -> p c e", e=2 * H)
            act.wait_ge(tab_v, 1)
            f(tab["beta"][:, :].rearrange("p (c h) -> p c h", h=H), ab[:, :, 0:H], ACT.Sigmoid).then_inc(tab_a, 1)
            f(tab["t1"][:, :], tab["t0"][:, :], ACT.Abs).then_inc(tab_a, 1)
            act.wait_ge(tab_a, 2)
            f(tab["t1"][:, :], tab["t1"][:, :], ACT.Exp, scale=-1.0).then_inc(tab_a, 1)
            f(head_in[:, 0, :], head_in[:, 0, :], ACT.Exp).then_inc(tab_a, 1)
            act.wait_ge(tab_a, 4)
            f(tab["t1"][:, :], tab["t1"][:, :], ACT.Ln, bias=ones[:, 0:1]).then_inc(tab_a, 1)
            act.wait_ge(tab_v, 5)
            f(tab["k_decay"][:, :], tab["t0"][:, :], ACT.Exp).then_inc(tab_a, 1)
            f(tab["e_last"][:, :], bank[5][:, TILES * H:2 * TILES * H], ACT.Exp).then_inc(tab_a, 1)
            f(tab["t1"][:, :], tab["cum"][:, :], ACT.Exp).then_inc(tab_a, 1)
            act.wait_ge(stored[0], past(16 * (U_SAVED // 2 + H + 3 * KT // 2)))
            act.wait_ge(stored[1], past(16 * (U_SAVED // 2 + 3 * KT // 2)))
            arrive(act, 0)

            with act.Fori(0, TILES // 2) as i:
                for p in range(2):
                    c = 2 * i + p
                    act.wait_ge(qkv_loaded[p], past(32 * i + 32))
                    act.wait_ge(G["ss"], past(c))
                    f(sq_qk[:, :, :], qkv_in[p][:, 0:2 * H, :], ACT.Square).then_inc(G["sq"], 1)
                    act.wait_ge(G["ss"], past(c + 1))
                    act.wait_ge(G["qkn"], past(2 * c))
                    for n in range(2):
                        f(rs_qk[:, n * H:(n + 1) * H, :], hp(bank[n]), ACT.Ln, bias=eps[:, 0:1]
                          ).then_inc(G["rs_ln"], 1)
                    act.wait_ge(G["rs_ln"], past(2 * c + 2))
                    f(rs_qk[:, :, :], rs_qk[:, :, :], ACT.Exp, scale=-0.5).then_inc(G["rs"], 1)
                    act.wait_ge(G["cumb"], past(c + 1))
                    act.wait_ge(G["qdec"], past(c))
                    f(e_cum[:, :, :], hp(bank[2]), ACT.Exp).then_inc(G["ecum"], 1)
                    act.wait_ge(G["diff"], past(2 * c + 2))
                    f(dec[:, :, :, :], dec[:, :, :, :], ACT.Exp).then_inc(G["decay"], 1)
                    act.wait_ge(G["lowt"], past(c + 1))
                    act.wait_ge(G["pair"], past(LEVELS * c))
                    f(lowT[:, :, :], hp(bank[0]), ACT.Copy).then_inc(G["lowt_sb"], 1)
                    for lv in range(1, LEVELS):
                        n = (LEVELS - 1) * c + lv
                        act.wait_ge(G["x_mm"], past(n))
                        f(X[:, :, :], hp(bank[2]), ACT.Copy).then_inc(G["x_sb"], 1)
                    act.wait_ge(G["u_mm"], past(2 * c + 1))
                    act.wait_ge(G["vnew"], past(c))
                    f(U[:, :, :], hp(bank[0]), ACT.Copy).then_inc(G["uw_sb"], 1)
                    act.wait_ge(G["u_mm"], past(2 * c + 2))
                    f(WT[:, :, :], hp(bank[1]), ACT.Copy).then_inc(G["uw_sb"], 1)
                    act.wait_ge(G["o_mm"], past(c + 1))
                    f(sq_o[:, :, :], hp(bank[3]), ACT.Square).then_inc(N["sqo"], 1)
                    act.wait_ge(N["sso"], past(c + 1))
                    act.wait_ge(N["on"], past(c))
                    f(rs_o[:, :, :], hp(bank[5]), ACT.Ln, scale=1.0 / P, bias=eps[:, 0:1]).then_inc(N["rso_ln"], 1)
                    act.wait_ge(N["rso_ln"], past(c + 1))
                    f(rs_o[:, :, :], rs_o[:, :, :], ACT.Exp, scale=-0.5).then_inc(N["rso"], 1)
                    act.wait_ge(g_y[p], past(i + 1))
                    act.dma_start(y_all[0:H, :, ds(c * P, P)].rearrange("h p r -> p h r"), y_a[:, :, :]
                                  ).then_inc(N["y_stored"], 16)
            act.wait_ge(N["y_stored"], past(16 * TILES))
            arrive(act, 1)

            with act.Fori(0, H // MAPS) as i:
                for p in range(2):
                    h = 2 * i + p
                    turns = [0]

                    def turned(dst):
                        n = turns[0]
                        turns[0] += 1
                        act.wait_ge(A["turn"], past(TURNS * h + n + 1))
                        w = dst.shape[1]
                        f(dst, bank[4 + n % 2][:, 0:w * P].rearrange("p (k c) -> p k c", c=P), ACT.Copy
                          ).then_inc(turn_free[n % 2], 1)

                    def exps(b):
                        act.wait_ge(A["negtop"], past(TILES * h + b + 1))
                        for m in range(MAPS):
                            n = b % AHEAD
                            s = s_buf[n][:, m, 0:(b + 1) * P]
                            f(s, s, ACT.Exp, bias=neg_top[n][:, m:m + 1], accum_out=den[n][:, m:m + 1]
                              ).then_inc(A["exp"], 1)

                    def out_norm(sb):
                        n = RB * h + sb
                        act.wait_ge(a_pv[AHEAD - 1], past(RB * h + sb + 1))
                        act.wait_ge(N["sso"], past(TILES + n))
                        f(sq_b[:, :], bank[6][:, :], ACT.Square).then_inc(N["sqo"], 1)
                        act.wait_ge(N["sso"], past(TILES + n + 1))
                        act.wait_ge(N["on"], past(TILES + n))
                        f(rs_b[:, :], bank[7][:, :], ACT.Ln, scale=1.0 / P, bias=eps[:, 0:1]
                          ).then_inc(N["rso_ln"], 1)
                        act.wait_ge(N["rso_ln"], past(TILES + n + 1))
                        f(rs_b[:, :], rs_b[:, :], ACT.Exp, scale=-0.5).then_inc(N["rso"], 1)

                    def save(sb):
                        act.wait_ge(a_y[p], past(RB * i + sb + 1))
                        act.dma_start(y_all[ds(h + H, 1), :, sb * R:(sb + 1) * R].rearrange("o p r -> p (o r)"),
                                      y_b[:, :]).then_inc(N["y_stored"], 16)

                    act.wait_ge(a_pv[AHEAD - 1], past(RB * h))
                    exps(0)
                    exps(1)
                    for g in range(RB):
                        turned(v_rows[:, g * RB:(g + 1) * RB, :])
                    for b in range(TILES):
                        if b and b % RB == 0:
                            out_norm(b // RB - 1)
                        act.wait_ge(a_pv[(b - 2) % AHEAD], past(RB * h + (b + 2) // AHEAD))
                        for g in range(b // RB + 1):
                            turned(probsT[b % 2][:, g * RB:min((g + 1) * RB, b + 1), :])
                        if b + 2 < TILES:
                            exps(b + 2)
                        if b and b % RB == 0:
                            save(b // RB - 1)
                    out_norm(RB - 1)
                    save(RB - 1)
            act.wait_ge(N["y_stored"], past(16 * TILES + 16 * RB * H))
            arrive(act, 2)

            def wb_split(r, n):
                act.wait_ge(wb_loaded[n % 2], past(192 * r + 16 * (n // 2) + 16))
                act.wait_ge(mm_done[n % 3], past(KT * r + n // 3))
                f(wb_hi[n % 3][:, :, :], wb_in[n % 2][:, :, :], ACT.Copy).then_inc(M["wb_hi"], 1)

            def y_split(r, b):
                act.wait_ge(M["y_loaded"], past(48 * r + 16 * b + 16))
                act.wait_ge(mm_done[2], past(KT * r))
                f(y_hi[:, H * b:H * (b + 1), :], y_in[:, :, :], ACT.Copy).then_inc(M["y_hi"], 1)

            def m_split(r, d):
                act.wait_ge(M["sum2"], past(KT * r + d + 1))
                if d == 0:
                    act.wait_ge(M["out_mm"], past(2 * RB * r))
                f(m_hi[:, d, :], gated[0][:, :], ACT.Copy).then_inc(M["hi"], 1)

            def merge(r, first=False, last=False):
                for d in range(KT):
                    for b in range(3):
                        wb_split(r, 3 * d + b)
                        if b == 1 and d:
                            m_split(r, d - 1)
                    if first:
                        act.wait_ge(M["wo_loaded"], past(16 * d + 16))
                        f(wo_hi[:, d, :], x_res[d % 2][:, :], ACT.Copy).then_inc(M["wo_hi"], 1)
                m_split(r, KT - 1)
                for t in range(RB):
                    n = RB * r + t
                    if not last and t:
                        y_split(r + 1, t - 1)
                    act.wait_ge(M["done"], past(n))
                    for nb in range(2):
                        act.wait_ge(M["out_mm"], past(2 * n + nb + 1))
                        f(o_norm[:, nb * R:(nb + 1) * R], bank[(6, 0)[t % 2] + nb][:, :], ACT.Square,
                          accum_out=o_stat[:, nb:nb + 1]).then_inc(M["sq"], 1)
                    act.wait_ge(M["ss"], past(n + 1))
                    f(o_stat[:, 3:4], o_stat[:, 2:3], ACT.Sqrt, scale=1.0 / D, bias=eps[:, 0:1]
                      ).then_inc(M["root"], 1)
                    act.wait_ge(M["done"], past(n + 1))
                    act.dma_start(out_rows[ds(n, 1), :, :].rearrange("o p d -> p (o d)"), x_res[t % 2][:, :]
                                  ).then_inc(out_stored[t % 2], 16)

            for b in range(3):
                y_split(0, b)
            merge(0, first=True)
            with act.Fori(1, RB - 1) as r:
                merge(r)
            merge(RB - 1, last=True)

        @block.vector
        def _(dve):
            def stt(out_, a, s, b, op0, op1):
                return dve.scalar_tensor_tensor(out_, a, s, b, op0, op1)

            def tt(out_, a, b, op):
                return dve.tensor_tensor(out_, a, b, op)

            dve.wait_ge(vec_turned, 1)
            dve.tensor_copy(vec[:, :], bank[0][:, 0:VECS]).then_inc(vec_ready, 1)
            dve.wait_ge(vec_ready, 1)
            dve.tensor_scalar(diff_w[:, :], vec[:, VEC_DIFF:VEC_DIFF + 1], 1.0 - LAM_INIT, None, ALU.mult
                              ).then_inc(vec_ready, 1)
            for m in range(2):
                dve.tensor_tensor_reduce(lam_in[:, 2 * m, :], lam_in[:, 2 * m, :], lam_in[:, 2 * m + 1, :], 1.0, 0.0,
                                         ALU.mult, ALU.add, lam_s[:, m:m + 1]).then_inc(lam_step, 1)

            def scale_rows(i, q):
                t = 4 * i + q
                dve.wait_ge(x_root, past(t + 1))
                dve.reciprocal(x_stat[:, q, 2:3], x_stat[:, q, 1:2]).then_inc(x_inv, 1)
                dve.wait_ge(x_inv, past(t + 1))
                stt(x_in[q][:, :], x_in[q][:, :], x_stat[:, q, 2:3], pre_w[:, :], ALU.mult, ALU.mult
                    ).then_inc(x_scaled, 1)

            def take_lo(i, q):
                t = 4 * i + q
                for n in range(2):
                    dve.wait_ge(h_hi_done, past(2 * t + n + 1))
                    part = slice(4 * n, 4 * n + 4)
                    tt(hT_lo[:, part, ds(t * P, P)], hp(bank[4 + 2 * (q % 2) + n]),
                       hT_hi[:, part, ds(t * P, P)].bitcast(F32), ALU.subtract).then_inc(h_lo_done[q % 2], 1)

            scale_rows(0, 0)
            scale_rows(0, 1)
            with dve.Fori(0, TILES // 4 - 1) as i:
                for q in range(4):
                    take_lo(i, q)
                    scale_rows(i + (q + 2) // 4, (q + 2) % 4)
            last_i = TILES // 4 - 1
            for q in range(4):
                take_lo(last_i, q)
                if q < 2:
                    scale_rows(last_i, q + 2)
            dve.wait_ge(x_scaled, past(TILES))
            for p in range(2):
                dve.memset(raw[p][:, 0:GDN_CONV - 1], 0.0).then_inc(raw_zero, 1)
            dve.wait_ge(lam_step, 3)
            tt(neg_lam[:, :], lam_s[:, 3:4], lam_s[:, 2:3], ALU.subtract).then_inc(lam_step, 1)
            dve.wait_ge(lam_step, 4)
            dve.tensor_scalar(neg_lam[:, :], neg_lam[:, :], -LAM_INIT, None, ALU.add).then_inc(lam_step, 1)

            dve.wait_ge(raw_zero, 2)
            dve.wait_ge(vec_ready, 2)
            with dve.Fori(0, U_ZA // 2) as i:
                for p in range(2):
                    u = 2 * i + p
                    dve.wait_ge(bank_free[RB - 1], past(u + 1))
                    dve.wait_ge(stored[p], past(16 * i))
                    dve.tensor_scalar(stage[p][:, :], raw[p][:, 0:SEQ], vec[:, ds(u, 1)], None, ALU.mult
                                      ).then_inc(conv_step, 1)
                    for tap in range(1, GDN_CONV):
                        dve.wait_ge(conv_step, past((GDN_CONV - 1) * u + tap))
                        last = stt(stage[p][:, :], raw[p][:, tap:tap + SEQ], vec[:, ds(u + 12 * tap, 1)],
                                   stage[p][:, :], ALU.mult, ALU.add)
                        if tap < GDN_CONV - 1:
                            last.then_inc(conv_step, 1)
                    last.then_inc(conv_done[p], 1)

            with dve.Fori(0, H) as j:
                k = 2 * j + U_SAVED // 2
                u = 4 * j + U_SAVED
                for rb in range(RB):
                    dve.wait_ge(block_done[1], past(RB * k + rb + 1))
                    dve.wait_ge(bank_free[rb], past(u + 1))
                    part = raw[0][:, GDN_CONV - 1 + rb * R:GDN_CONV - 1 + (rb + 1) * R]
                    tt(part, part, bank[rb][:, :], ALU.mult).then_inc(bank_free[rb], 1)
                dve.wait_ge(bank_free[RB - 1], past(u + 2))
                for tap in range(SC_CONV):
                    src = raw[0][:, GDN_CONV - SC_CONV + tap:GDN_CONV - SC_CONV + tap + SEQ]
                    w = vec[:, ds(j + (VEC_SC + H * tap), 1)]
                    if tap == 0:
                        dve.tensor_scalar(conv[:, :], src, w, None, ALU.mult).then_inc(sc_step, 1)
                        continue
                    dve.wait_ge(sc_step, past((SC_CONV - 1) * j + tap))
                    last = stt(conv[:, :], src, w, conv[:, :], ALU.mult, ALU.add)
                    last.then_inc(sc_step if tap < SC_CONV - 1 else sc_conv_done, 1)
                dve.wait_ge(sc_conv_done, past(j + 1))
                for rb in range(RB):
                    dve.wait_ge(block_done[0], past(RB * k + (RB + rb + 1)))
                    part = conv[:, rb * R:(rb + 1) * R]
                    tt(part, part, bank[rb][:, :], ALU.mult).then_inc(bank_free[rb], 1)
                dve.wait_ge(bank_free[RB - 1], past(u + 4))
                dve.wait_ge(stored[0], past(16 * (j + U_SAVED // 2)))
                tt(stage[0][:, :], conv[:, :], stage[1][:, :], ALU.mult).then_inc(yc_done, 1)

            def by_chunk(t):
                return t[:, :].rearrange("p (c h) -> p c h", h=H)

            ab = bank[4][:, 0:TILES * 2 * H].rearrange("p (c e) -> p c e", e=2 * H)
            dve.wait_ge(ab_turned, 1)
            tt(by_chunk(tab["t0"]), ab[:, :, H:2 * H], head_in[:, 1:2, :].to_broadcast([P, TILES, H]), ALU.add
               ).then_inc(tab_v, 1)
            dve.wait_ge(tab_a, 5)
            stt(tab["t0"][:, :], tab["t0"][:, :], 0.0, tab["t1"][:, :], ALU.max, ALU.add).then_inc(tab_v, 1)
            dve.wait_ge(tab_v, 2)
            stt(by_chunk(tab["g"]), by_chunk(tab["t0"]), -1.0, head_in[:, 0:1, :].to_broadcast([P, TILES, H]),
                ALU.mult, ALU.mult).then_inc(tab_v, 1)
            dve.wait_ge(tab_mm, 1)
            dve.tensor_copy(tab["cum"][:, :], bank[5][:, 0:TILES * H]).then_inc(tab_v, 1)
            dve.wait_ge(tab_v, 4)
            tt(tab["t0"][:, :], bank[5][:, TILES * H:2 * TILES * H], tab["cum"][:, :], ALU.subtract
               ).then_inc(tab_v, 1)
            dve.wait_ge(tab_a, 8)
            tt(tab["beta_ecum"][:, :], tab["beta"][:, :], tab["t1"][:, :], ALU.mult).then_inc(tab_v, 1)
            arrive(dve, 0)

            def bc(t, c):
                return t[:, ds(H * c, H)].rearrange("p (h o) -> p h o", o=1).to_broadcast([P, H, P])

            with dve.Fori(0, TILES // 2) as i:
                for p in range(2):
                    c = 2 * i + p
                    dve.wait_ge(G["rs"], past(c + 1))
                    dve.wait_ge(qkv_loaded[p], past(32 * i + 32))
                    dve.wait_ge(G["kk"], past(2 * c))
                    dve.wait_ge(G["qdec"], past(c))
                    stt(qkn[:, 0:H, :], qkv_in[p][:, 0:H, :], P ** -0.5, rs_qk[:, 0:H, :], ALU.mult, ALU.mult
                        ).then_inc(G["qkn"], 1)
                    tt(qkn[:, H:2 * H, :], qkv_in[p][:, H:2 * H, :], rs_qk[:, H:2 * H, :], ALU.mult
                       ).then_inc(G["qkn"], 1)
                    dve.wait_ge(G["mask"], past(2 * c + 2))
                    dve.wait_ge(G["ecum"], past(c + 1))
                    tt(dec[:, 0, :, :], dec[:, 0, :, :], hp(bank[2]), ALU.subtract).then_inc(G["diff"], 1)
                    tt(dec[:, 1, :, :], dec[:, 1, :, :], hp(bank[2]), ALU.add).then_inc(G["diff"], 1)
                    dve.wait_ge(G["turn"], past(2 * c + 1))
                    dve.wait_ge(G["u_mm"], past(2 * c))
                    tt(v_beta[:, :, :], hp(bank[4]), bc(tab["beta"], c), ALU.mult).then_inc(G["rows"], 1)
                    dve.wait_ge(G["turn"], past(2 * c + 2))
                    tt(k_beta[:, :, :], hp(bank[3]), bc(tab["beta_ecum"], c), ALU.mult).then_inc(G["rows"], 1)
                    dve.wait_ge(G["s_mm"], past(c))
                    tt(k_dec[:, :, :], hp(bank[3]), bc(tab["k_decay"], c), ALU.mult).then_inc(G["rows"], 1)
                    dve.wait_ge(G["kk"], past(2 * c + 1))
                    dve.wait_ge(G["decay_b"], past(c + 1))
                    dve.wait_ge(G["lowt"], past(c))
                    dve.wait_ge(G["t0"], past(2 * c))
                    tt(low[:, :, :], hp(bank[0]), dec[:, 0, :, :], ALU.mult).then_inc(G["masked"], 1)
                    dve.wait_ge(G["kk"], past(2 * c + 2))
                    dve.wait_ge(G["o_mm"], past(c))
                    tt(qk_m[:, :, :], hp(bank[1]), dec[:, 1, :, :], ALU.mult).then_inc(G["masked"], 1)
                    for lv in range(1, LEVELS):
                        n = (LEVELS - 1) * c + lv
                        m = (2 * (LEVELS - 1) - 1) * c + 2 * lv
                        dve.wait_ge(G["y_mm"], past(m if lv < LEVELS - 1 else m - 1))
                        last = tt(Tt[:, :, :], Tt[:, :, :], hp(bank[3]), ALU.subtract)
                        if lv < LEVELS - 1:
                            last = tt(T[:, :, :], T[:, :, :], hp(bank[4]), ALU.subtract)
                        last.then_inc(G["t_new"], 1)
                    dve.wait_ge(G["ws"], past(c + 1))
                    dve.wait_ge(G["uw_sb"], past(2 * c + 1))
                    dve.wait_ge(G["s_mm"], past(c))
                    tt(v_new[:, :, :], U[:, :, :], hp(bank[2]), ALU.subtract).then_inc(G["vnew"], 1)
                    dve.wait_ge(G["s_mm"], past(c + 1))
                    dve.wait_ge(G["sdec"], past(c + 1))
                    tt(state[:, :, :], state_d[:, :, :], hp(bank[4]), ALU.add).then_inc(G["state"], 1)
                    dve.wait_ge(N["rso"], past(c + 1))
                    dve.wait_ge(N["y_stored"], past(16 * c))
                    tt(y_a[:, :, :], hp(bank[3]), rs_o[:, :, :], ALU.mult).then_inc(N["on"], 1)
                    dve.wait_ge(N["on"], past(c + 1))
                    stt(y_a[:, :, :], y_a[:, :, :], vec[:, VEC_GDN:VEC_GDN + 1], za_in[p][:, :, :],
                        ALU.mult, ALU.mult).then_inc(g_y[p], 1)
            arrive(dve, 1)

            with dve.Fori(0, H // MAPS) as i:
                for p in range(2):
                    h = 2 * i + p
                    scored = [0]

                    def biased(b):
                        bp = b % AHEAD
                        groups = b // RB + 1
                        dve.wait_ge(a_pv[bp], past(RB * h + b // AHEAD))
                        for m in range(MAPS):
                            for g in range(groups):
                                n = scored[0]
                                scored[0] += 1
                                w = min(R, (b + 1) * P - g * R)
                                at = SEQ - P - b * P + g * R
                                dve.wait_ge(A["score"], past(SCORES * h + n + 1))
                                wait_apart(dve, dve_waited)
                                dve.tensor_tensor_reduce(
                                    s_buf[bp][:, m, g * R:g * R + w], bank[n % 4][:, 0:w], bias[p][:, at:at + w],
                                    1.0, -3e38, ALU.add, ALU.max, top[bp][:, m, g:g + 1]
                                ).then_inc(score_free[n % 4], 1)
                        n = scored[0] - 1
                        dve.wait_ge(score_free[n % 4], past(SCORES // 4 * h + n // 4 + 1))
                        dve.tensor_reduce(top_all[bp][:, :], top[bp][:, :, 0:groups], AX.X, ALU.max
                                          ).then_inc(A["top"], 1)
                        dve.wait_ge(A["top"], past(TILES * h + b + 1))
                        dve.tensor_scalar(neg_top[bp][:, :], top_all[bp][:, :], -1.0, None, ALU.mult
                                          ).then_inc(A["negtop"], 1)

                    def combine(b):
                        bp = b % AHEAD
                        n = TILES * h + b
                        dve.wait_ge(A["exp"], past(2 * n + 2))
                        dve.reciprocal(inv[bp][:, :], den[bp][:, :]).then_inc(A["inv"], 1)
                        dve.wait_ge(A["inv"], past(n + 1))
                        tt(sub_w[bp][:, :], inv[bp][:, 1:2], neg_lam[:, :], ALU.mult).then_inc(A["subw"], 1)
                        w = (b + 1) * P
                        s0, s1 = s_buf[bp][:, 0, 0:w], s_buf[bp][:, 1, 0:w]
                        dve.wait_ge(A["subw"], past(n + 1))
                        dve.tensor_scalar(s1, s1, sub_w[bp][:, 0:1], None, ALU.mult).then_inc(A["sub"], 1)
                        dve.wait_ge(A["sub"], past(n + 1))
                        stt(s0, s0, inv[bp][:, 0:1], s1, ALU.mult, ALU.add).then_inc(A["probs"], 1)

                    def finish(sb):
                        n = RB * h + sb
                        dve.wait_ge(N["rso"], past(TILES + n + 1))
                        dve.wait_ge(N["y_stored"], past(16 * TILES + 16 * n))
                        tt(y_b[:, :], bank[6][:, :], rs_b[:, :], ALU.mult).then_inc(N["on"], 1)
                        dve.wait_ge(N["on"], past(TILES + n + 1))
                        stt(y_b[:, :], y_b[:, :], diff_w[:, 0:1], zb_in[p][:, sb * R:(sb + 1) * R],
                            ALU.mult, ALU.mult).then_inc(a_y[p], 1)

                    dve.wait_ge(head_loaded[p], past(64 * i + 64))
                    dve.wait_ge(A["dist"], past(2 * h + 4))
                    biased(0)
                    biased(1)
                    for b in range(TILES):
                        combine(b)
                        if b + 2 < TILES:
                            biased(b + 2)
                        if b and b % RB == 0:
                            finish(b // RB - 1)
                    finish(RB - 1)
            arrive(dve, 2)

            dve.wait_ge(M["post"], past(16))

            def y_split(r, b):
                dve.wait_ge(M["y_hi"], past(3 * r + b + 1))
                tt(y_lo[:, H * b:H * (b + 1), :], y_in[:, :, :],
                   y_hi[:, H * b:H * (b + 1), :].bitcast(F32), ALU.subtract).then_inc(M["y_lo"], 1)

            def merge(r, first=False, last=False):
                for d in range(KT):
                    for b in range(3):
                        n = 3 * d + b
                        dve.wait_ge(mm_done[b], past(KT * r + d + 1))
                        dve.wait_ge(gate_loaded[b], past(128 * r + 16 * d + 16))
                        dve.wait_ge(M["lo"], past(KT * r + d))
                        tt(gated[b][:, :], bank[n % 6][:, :], gate_in[b][:, :], ALU.mult
                           ).then_inc(gated_done[n % 6], 1)
                        if b == 1:
                            dve.wait_ge(gated_done[n % 6], past(KT // 2 * r + d // 2 + 1))
                            tt(gated[1][:, :], gated[0][:, :], gated[1][:, :], ALU.add).then_inc(M["sum1"], 1)
                    if first:
                        dve.wait_ge(M["wo_hi"], past(d + 1))
                        tt(wo_lo[:, d, :], x_res[d % 2][:, :], wo_hi[:, d, :].bitcast(F32), ALU.subtract
                           ).then_inc(M["wo_lo"], 1)
                    dve.wait_ge(M["hi"], past(KT * r + d + 1))
                    tt(m_lo[:, d, :], gated[0][:, :], m_hi[:, d, :].bitcast(F32), ALU.subtract).then_inc(M["lo"], 1)
                for t in range(RB):
                    n = RB * r + t
                    if not last and t:
                        y_split(r + 1, t - 1)
                    dve.wait_ge(M["sq"], past(2 * n + 2))
                    tt(o_stat[:, 2:3], o_stat[:, 0:1], o_stat[:, 1:2], ALU.add).then_inc(M["ss"], 1)
                    dve.wait_ge(M["root"], past(n + 1))
                    dve.reciprocal(o_stat[:, 4:5], o_stat[:, 3:4]).then_inc(M["inv"], 1)
                    dve.wait_ge(M["inv"], past(n + 1))
                    for nb in range(2):
                        cols = slice(nb * R, (nb + 1) * R)
                        last_op = stt(o_norm[:, cols], bank[(6, 0)[t % 2] + nb][:, :], o_stat[:, 4:5],
                                      post_w[:, cols], ALU.mult, ALU.mult)
                    last_op.then_inc(M["normed"], 1)
                    dve.wait_ge(M["normed"], past(n + 1))
                    dve.wait_ge(x_res_loaded[t % 2], past(32 * r + 16 * (t // 2) + 16))
                    tt(x_res[t % 2][:, :], x_res[t % 2][:, :], o_norm[:, :], ALU.add).then_inc(M["done"], 1)

            for b in range(3):
                y_split(0, b)
            merge(0, first=True)
            with dve.Fori(1, RB - 1) as r:
                merge(r)
            merge(RB - 1, last=True)


_INS = ["x", "norm_pre", "norm_post", "w_in", "gdn_conv_w", "gdn_a_log", "gdn_dt_bias", "gdn_norm_w",
        "diff_lambda", "diff_norm_w", "sc_conv_w", "w_branch", "w_out"]


def kernel(**inputs):
    import numpy as np
    import concourse.bacc as bacc
    from concourse.bass_utils import run_bass_kernel_spmd

    nc = bacc.Bacc("TRN2", target_bir_lowering=False, num_devices=1)
    arrays, args = {}, []
    for name in _INS:
        a = np.ascontiguousarray(inputs[name])
        arrays[f"in_{name}"] = a
        args.append(nc.dram_tensor(f"in_{name}", a.shape, mybir.dt.from_np(a.dtype), kind="ExternalInput").ap())
    out = nc.dram_tensor("out_x", (1, SEQ, D), F32, kind="ExternalOutput").ap()
    hybrid_block(nc, *args, out)
    r = run_bass_kernel_spmd(nc, [arrays], core_ids=[0])
    return r.results[0]["out_x"]
```

```python
from contextlib import ExitStack
import math

import concourse.bass as bass
from concourse import mybir

F32 = mybir.dt.float32
F32R = mybir.dt.float32r
ALU = mybir.AluOpType
ACT = mybir.ActivationFunctionType
AX = mybir.AxisListType
ds = bass.ds

P = 128
SEQ = 2048
D = 1024
KT = D // P
BW = D // 2
H = BW // P
N_IN = 9224
RB = 4
R = SEQ // RB
TILES = SEQ // P
GDN_CONV = 4
SC_CONV = 3
EPS = 1e-6
NEG = -1e30
LAM_INIT = 0.8 - 0.6 * math.exp(-0.3 * 0)
MAPS = 2
QK_DIM = P // MAPS
AHEAD = 4
LEVELS = 7
SLOPE = 2.0 ** (-8.0 / H)
UNITS = 72
CONSTS = 34
TURNS = RB + sum(b // RB + 1 for b in range(TILES))
SCORES = MAPS * sum(b // RB + 1 for b in range(TILES))

COL_B = 4 * BW
COL_ATT = COL_B + 2 * H
COL_SC = COL_ATT + 4 * BW
COL_MERGE = COL_SC + 4 * BW
U_GDN, U_ZA, U_Q, U_K, U_V, U_ZB = 0, 12, 16, 20, 24, 28
U_SAVED = 32
VEC_CONV, VEC_SC = 0, GDN_CONV * 12
VEC_GDN = VEC_SC + SC_CONV * H
VEC_DIFF = VEC_GDN + 1
VECS = VEC_DIFF + 1


def hybrid_block(nc, x, norm_pre, norm_post, w_in, gdn_conv_w, gdn_a_log, gdn_dt_bias, gdn_norm_w,
                 diff_lambda, diff_norm_w, sc_conv_w, w_branch, w_out, out):
    with ExitStack() as ctx:
        def sem(name):
            return ctx.enter_context(nc.semaphore(name))

        counted = []

        def counter(name):
            counted.append(sem(name))
            return counted[-1]

        def counters(name, n):
            return [counter(f"{name}{i}") for i in range(n)]

        def past(n):
            return n + 1

        BASE = (nc.sbuf_base + 63) // 64 * 64
        LIMIT = nc.sbuf_usable_end

        class Room:

            def __init__(self, at):
                self.at = at

            def __call__(self, name, shape, dt=F32):
                n = 4
                for s in shape[1:]:
                    n *= s
                t = nc.alloc_sbuf_tensor_at(name, shape, dt, offset=self.at)
                self.at += (n + 63) // 64 * 64
                assert self.at <= LIMIT, (name, self.at, LIMIT)
                return t

        keep = Room(BASE)
        ident = keep("ident", [P, P])
        ones = keep("ones", [P, P])
        triu = keep("triu", [P, P])
        mask_lo = keep("mask_lo", [P, P])
        mask_up = keep("mask_up", [P, P])
        pair_t = keep("pair_t", [P, LEVELS, P])
        pair1 = keep("pair1", [P, P])
        eps = keep("eps", [P, 1])
        vec_rows = keep("vec_rows", [VECS, P])
        vec = keep("vec", [P, VECS])
        diff_w = keep("diff_w", [P, 1])
        lam_in = keep("lam_in", [P, 4, QK_DIM])
        lam_s = keep("lam_s", [P, 4])
        neg_lam = keep("neg_lam", [P, 1])
        head_in = keep("head_in", [P, 2, H])
        tab = {n: keep("tab_" + n, [P, TILES * H]) for n in
               ("g", "cum", "beta", "beta_ecum", "k_decay", "e_last", "t0", "t1")}
        ROOM = keep.at

        room = Room(ROOM)
        hT_hi = room("hT_hi", [P, KT, SEQ], F32R)
        hT_lo = room("hT_lo", [P, KT, SEQ], F32R)
        w_hi = [room(f"w_hi{p}", [P, KT, P], F32R) for p in range(2)]
        w_lo = [room(f"w_lo{p}", [P, KT, P], F32R) for p in range(2)]
        w_raw = [room(f"w_raw{p}", [P, KT, P]) for p in range(2)]
        AFTER_W = room.at
        stage = [room(f"stage{p}", [P, SEQ]) for p in range(2)]
        raw = [room(f"raw{p}", [P, GDN_CONV - 1 + SEQ]) for p in range(2)]
        conv = room("conv", [P, SEQ])
        abT = raw[0]
        room = Room(AFTER_W)
        x_in = [room(f"x_in{q}", [P, D]) for q in range(4)]
        x_junk = room("x_junk", [P, D])
        pre_w = room("pre_w", [P, D])
        x_stat = room("x_stat", [P, 4, 3])

        room = Room(ROOM)

        def tiles(name, copies, *extra):
            return [room(f"{name}{p}", [P, *extra, H, P]) for p in range(copies)]

        qkv_in = [room(f"qkv_in{p}", [P, 3 * H, P]) for p in range(2)]
        sq_qk = [room(f"sq_qk{p}", [P, 2 * H, P]) for p in range(2)]
        rs_qk = [room(f"rs_qk{p}", [P, 2 * H, P]) for p in range(2)]
        qkn = [room(f"qkn{p}", [P, 2 * H, P]) for p in range(2)]
        g_tri = tiles("g_tri", 2)
        dec = tiles("dec", 2, 2)
        e_cum = tiles("e_cum", 2)
        low = tiles("low", 2)
        lowT = tiles("lowT", 2)
        pairM = tiles("pairM", 2, LEVELS)
        T = tiles("T", 2)
        Tt = tiles("Tt", 2)
        X = tiles("X", 2)
        k_beta = tiles("k_beta", 2)
        v_beta = tiles("v_beta", 2)
        U = tiles("U", 2)
        WT = tiles("WT", 2)
        q_dec = tiles("q_dec", 4)
        qk_m = tiles("qk_m", 4)
        k_dec = tiles("k_dec", 4)
        za_in = tiles("za_in", 4)
        state = tiles("state", 2)
        v_new = room("v_new", [P, H, P])
        state_d = room("state_d", [P, H, P])
        sq_o = room("sq_o", [P, H, P])
        rs_o = room("rs_o", [P, H, P])
        y_a = room("y_a", [P, H, P])

        room = Room(ROOM)
        q_in = [room(f"q_in{p}", [P, SEQ]) for p in range(2)]
        k_in = [room(f"k_in{p}", [P, SEQ]) for p in range(2)]
        v_in = [room(f"v_in{p}", [P, SEQ]) for p in range(2)]
        zb_in = [room(f"zb_in{p}", [P, SEQ]) for p in range(2)]
        v_rows = room("v_rows", [P, TILES, P])
        REACH = SEQ
        dist = room("dist", [P, REACH])
        bias = [room(f"bias{p}", [P, REACH]) for p in range(2)]
        s_buf = [room(f"s_buf{n}", [P, MAPS, SEQ]) for n in range(AHEAD)]
        probsT = [room(f"probsT{p}", [P, TILES, P]) for p in range(2)]
        top = [room(f"top{n}", [P, MAPS, RB]) for n in range(AHEAD)]
        top_all = [room(f"top_all{n}", [P, MAPS]) for n in range(AHEAD)]
        neg_top = [room(f"neg_top{n}", [P, MAPS]) for n in range(AHEAD)]
        den = [room(f"den{n}", [P, MAPS]) for n in range(AHEAD)]
        inv = [room(f"inv{n}", [P, MAPS]) for n in range(AHEAD)]
        sub_w = [room(f"sub_w{n}", [P, 1]) for n in range(AHEAD)]
        sq_b = room("sq_b", [P, R])
        rs_b = room("rs_b", [P, R])
        y_b = room("y_b", [P, R])

        room = Room(ROOM)
        wo_hi = room("wo_hi", [P, KT, D], F32R)
        wo_lo = room("wo_lo", [P, KT, D], F32R)
        y_hi = room("y_hi", [P, 3 * H, R], F32R)
        y_lo = room("y_lo", [P, 3 * H, R], F32R)
        m_hi = room("m_hi", [P, KT, R], F32R)
        m_lo = room("m_lo", [P, KT, R], F32R)
        y_in = room("y_in", [P, H, R])
        wb_in = [room(f"wb_in{p}", [P, H, P]) for p in range(2)]
        wb_hi = [room(f"wb_hi{p}", [P, H, P], F32R) for p in range(3)]
        wb_lo = [room(f"wb_lo{p}", [P, H, P], F32R) for p in range(3)]
        gate_in = [room(f"gate_in{p}", [P, R]) for p in range(3)]
        gated = [room(f"gated{p}", [P, R]) for p in range(3)]
        x_res = [room(f"x_res{p}", [P, D]) for p in range(2)]
        o_norm = room("o_norm", [P, D])
        post_w = room("post_w", [P, D])
        o_stat = room("o_stat", [P, 5])

        bank = [ctx.enter_context(nc.psum_tensor(f"bank{i}", [P, R], F32)) for i in range(8)]

        def hp(t):
            return t[:, :].rearrange("p (h c) -> p h c", h=H)

        saved = nc.dram_tensor("saved", (U_SAVED, P, SEQ), F32, kind="Internal").ap()
        gates = nc.dram_tensor("gates", (3 * KT, P, SEQ), F32, kind="Internal").ap()
        y_all = nc.dram_tensor("y_all", (3 * H, P, SEQ), F32, kind="Internal").ap()

        x_rows = x.rearrange("b (t p) d -> (b t) p d", p=P)
        out_rows = out.rearrange("b (t p) d -> (b t) p d", p=P)
        w_cols = w_in.rearrange("l (k p) n -> p (l k) n", p=P)
        wb_rows = w_branch.rearrange("l b (k p) n -> p (l b k) n", p=P)
        wo_rows = w_out.rearrange("l (k p) n -> p (l k) n", p=P)

        vec_loaded = sem("vec_loaded")
        const_step = sem("const_step")
        vec_turned = sem("vec_turned")
        vec_ready = sem("vec_ready")
        lam_step = sem("lam_step")
        x_loaded = counters("x_loaded", 4)
        x_used = counters("x_used", 4)
        x_square = counter("x_square")
        x_root = counter("x_root")
        x_inv = counter("x_inv")
        x_scaled = counter("x_scaled")
        h_hi_done = counter("h_hi_done")
        h_lo_done = counters("h_lo_done", 2)
        w_loaded = counters("w_loaded", 2)
        w_hi_done = counter("w_hi_done")
        w_ready = counter("w_ready")
        block_done = counters("block_done", 2)
        bank_free = counters("bank_free", RB)
        raw_zero = sem("raw_zero")
        conv_step = counter("conv_step")
        conv_done = counters("conv_done", 2)
        silu_done = counter("silu_done")
        stored = counters("stored", 2)
        sc_step = counter("sc_step")
        sc_conv_done = counter("sc_conv_done")
        yc_done = counter("yc_done")
        ab_turned = sem("ab_turned")
        tab_v = sem("tab_v")
        tab_a = sem("tab_a")
        tab_mm = sem("tab_mm")
        through = sem("through")
        ENGINES = 5

        def arrive(e, phase):
            e.drain().then_inc(through, 1)
            e.wait_ge(through, ENGINES * (phase + 1))

        pool_waited = sem("pool_waited")
        dve_waited = sem("dve_waited")

        def wait_apart(e, waited):
            e.sem_inc(waited, 1)

        qkv_loaded = counters("qkv_loaded", 2)
        G = {n: counter("g_" + n) for n in (
            "sq", "ss", "rs_ln", "rs", "tri", "cumb", "qkn", "mask", "ecum", "diff", "decay", "decay_b",
            "qdec", "kk", "turn", "masked", "rows", "lowt", "lowt_sb", "t0", "pair",
            "T", "x_mm", "x_sb", "y_mm", "t_new", "u_mm", "uw_sb", "ws", "vnew", "o_mm", "s_mm", "sdec",
            "state", "zero")}
        N = {n: counter("n_" + n) for n in ("sqo", "sso", "rso_ln", "rso", "on", "y_stored")}
        g_y = counters("g_y", 2)
        za_loaded = counters("za_loaded", 2)

        def level(k, lv, p):
            return 2 * (LEVELS - 1) * k + (2 * (lv - 1) + p + 1)

        def level_y(k, lv, p, which):
            return (4 * LEVELS - 6) * k + (4 * (lv - 1) + (2 * p + which + 1 if lv < LEVELS - 1 else p + 1))

        def pairs(e, body, tail):
            body(0, 0, first=True)
            with e.Fori(0, TILES // 4 - 1) as i:
                body(2 * i + 1, 1)
                body(2 * i + 2, 0)
            body(TILES // 2 - 1, 1, last=True)
            tail()
        A = {n: counter("a_" + n) for n in (
            "dist", "score", "top", "negtop", "exp", "inv", "subw",
            "sub", "probs", "turn")}
        a_pv = counters("a_pv", AHEAD)
        a_y = counters("a_y", 2)
        head_loaded = counters("head_loaded", 2)
        score_free = counters("score_free", 4)
        turn_free = counters("turn_free", 2)
        M = {n: counter("m_" + n) for n in (
            "wo_loaded", "wo_hi", "wo_lo", "post", "y_loaded", "y_hi", "y_lo", "wb_hi",
            "sum1", "sum2", "hi", "lo", "out_mm", "sq", "ss", "root", "inv", "normed", "done")}
        wb_free = counters("m_wb_free", 2)
        mm_done = counters("m_mm_done", 3)
        gated_done = counters("m_gated_done", 6)
        wb_loaded = counters("m_wb_loaded", 2)
        gate_loaded = counters("m_gate_loaded", 3)
        x_res_loaded = counters("m_x_loaded", 2)
        out_stored = counters("m_out_stored", 2)

        block = ctx.enter_context(nc.Block())

        @block.sync
        def _(sp):
            for s in counted:
                sp.sem_inc(s, 1)
            sp.dma_start(vec_rows[VEC_CONV:VEC_SC, :],
                         gdn_conv_w.rearrange("l k (t c) -> (l k t) c", c=P)).then_inc(vec_loaded, 16)
            sp.dma_start(vec_rows[VEC_SC:VEC_GDN, :],
                         sc_conv_w.rearrange("l k (t c) -> (l k t) c", c=P)).then_inc(vec_loaded, 16)
            sp.dma_start(vec_rows[VEC_GDN:VEC_DIFF, :], gdn_norm_w).then_inc(vec_loaded, 16)
            sp.dma_start(vec_rows[VEC_DIFF:VECS, :], diff_norm_w).then_inc(vec_loaded, 16)
            sp.dma_start(pre_w[:, :], norm_pre[0].partition_broadcast(P)).then_inc(vec_loaded, 16)
            sp.dma_start(lam_in[:, :, :], diff_lambda[0].partition_broadcast(P)).then_inc(vec_loaded, 16)
            sp.dma_start(head_in[:, 0, :], gdn_a_log[0].partition_broadcast(P)).then_inc(vec_loaded, 16)
            sp.dma_start(head_in[:, 1, :], gdn_dt_bias[0].partition_broadcast(P)).then_inc(vec_loaded, 16)
            with sp.Fori(0, TILES // 4) as i:
                for q in range(4):
                    sp.wait_ge(x_used[q], past(i))
                    sp.dma_start(x_in[q][:, :], x_rows[ds(4 * i + q, 1), :, :].rearrange("o p d -> p (o d)")
                                 ).then_inc(x_loaded[q], 16)

            def load_w(p, nth, col):
                sp.wait_ge(w_ready, past(nth))
                sp.dma_start(w_raw[p][:, :, :], w_cols[:, :, col]).then_inc(w_loaded[p], 16)

            load_w(0, 0, slice(0, P))
            load_w(1, 0, slice(P, 2 * P))
            with sp.Fori(1, U_Q // 2) as i:
                for p in range(2):
                    load_w(p, 2 * i + p - 1, ds(i * (2 * P) + p * P, P))
            with sp.Fori(U_Q // 2, U_SAVED // 2) as i:
                for p in range(2):
                    load_w(p, 2 * i + p - 1, ds(i * (2 * P) + (p * P + 2 * H), P))
            with sp.Fori(0, H) as j:
                for n, part in enumerate((1, 2, 0, 3)):
                    load_w(n % 2, 4 * j + (U_SAVED + n - 1), ds(j * P + (COL_SC + part * BW), P))
            with sp.Fori(0, 3 * KT // 2) as i:
                for p in range(2):
                    load_w(p, 2 * i + (U_SAVED + 4 * H + p - 1), ds(i * (2 * P) + (COL_MERGE + p * P), P))
            load_w(0, U_SAVED + 4 * H + 3 * KT - 1, slice(COL_B, COL_B + P))
            arrive(sp, 0)

            def chunk_loads(k, kp, first=False, last=False):
                for p in range(2):
                    rows = ds(k * (2 * P) + p * P, P)
                    sp.wait_ge(G["qkn"], past(4 * k))
                    sp.wait_ge(G["turn"], past(4 * k))
                    sp.dma_start(qkv_in[p][:, :, :], saved[U_GDN:U_ZA, :, rows].rearrange("u p r -> p u r")
                                 ).then_inc(qkv_loaded[p], 16)
                for p in range(2):
                    rows = ds(k * (2 * P) + p * P, P)
                    if not first:
                        sp.wait_ge(g_y[p], past(k - 1))
                    sp.dma_start(za_in[2 * kp + p][:, :, :], saved[U_ZA:U_Q, :, rows].rearrange("u p r -> p u r")
                                 ).then_inc(za_loaded[kp], 16)

            pairs(sp, chunk_loads, lambda: None)
            arrive(sp, 1)

            with sp.Fori(0, H // 2) as i:
                for p in range(2):
                    sp.wait_ge(a_y[p], past(RB * i))
                    for t, u in ((v_in, U_V), (q_in, U_Q), (k_in, U_K), (zb_in, U_ZB)):
                        sp.dma_start(t[p][:, :], saved[ds(2 * i + (u + p), 1), :, :].rearrange("o p r -> p (o r)")
                                     ).then_inc(head_loaded[p], 16)
            arrive(sp, 2)

            sp.dma_start(post_w[:, :], norm_post[0].partition_broadcast(P)).then_inc(M["post"], 16)

            def load_y(r, b):
                sp.wait_ge(M["y_lo"], past(3 * r + b))
                sp.dma_start(y_in[:, :, :], y_all[H * b:H * (b + 1), :, ds(r * R, R)].rearrange("u p r -> p u r")
                             ).then_inc(M["y_loaded"], 16)

            def merge_loads(r, first=False, last=False):
                rows = ds(r * R, R)
                for d in range(KT):
                    for b in range(3):
                        n = 3 * d + b
                        sp.wait_ge(wb_free[n % 2], past(12 * r + n // 2))
                        sp.dma_start(wb_in[n % 2][:, :, :], wb_rows[:, H * b:H * (b + 1), d * P:(d + 1) * P]
                                     ).then_inc(wb_loaded[n % 2], 16)
                        sp.wait_ge(gated_done[3 * ((d + 1) % 2) + b], past(RB * r + (d + 1) // 2))
                        sp.dma_start(gate_in[b][:, :], gates[b * KT + d, :, rows]).then_inc(gate_loaded[b], 16)
                    if first:
                        sp.wait_ge(M["wo_lo"], past(max(0, d - 1)))
                        sp.dma_start(x_res[d % 2][:, :], wo_rows[:, d, :]).then_inc(M["wo_loaded"], 16)
                if first:
                    sp.wait_ge(M["wo_lo"], past(KT))
                if not last:
                    load_y(r + 1, 0)
                for t in range(RB):
                    sp.wait_ge(out_stored[t % 2], past(32 * r + 16 * (t // 2)))
                    sp.dma_start(x_res[t % 2][:, :], x_rows[ds(RB * r + t, 1), :, :].rearrange("o p d -> p (o d)")
                                 ).then_inc(x_res_loaded[t % 2], 16)
                    if not last and t in (1, 2):
                        load_y(r + 1, t)

            for b in range(3):
                load_y(0, b)
            merge_loads(0, first=True)
            with sp.Fori(1, RB - 1) as r:
                merge_loads(r)
            merge_loads(RB - 1, last=True)
            for p in range(2):
                sp.wait_ge(out_stored[p], past(16 * TILES // 2))

        @block.gpsimd
        def _(pool):
            def sum_last(pool, r, d):
                pool.wait_ge(M["sum1"], past(KT * r + d + 1))
                pool.wait_ge(gated_done[3 * (d % 2) + 2], past(KT // 2 * r + d // 2 + 1))
                pool.tensor_tensor(gated[0][:, :], gated[1][:, :], gated[2][:, :], ALU.add
                                   ).then_inc(M["sum2"], 1)

            n_const = [0]

            def const(ins):
                n_const[0] += 1
                ins.then_inc(const_step, 1)
                pool.wait_ge(const_step, n_const[0])

            def select(t, op, fill, base, cm, pattern):
                const(pool.affine_select(out=t, in_=t, compare_op=op, fill=fill, base=base,
                                         channel_multiplier=cm, pattern=pattern))

            const(pool.memset(ident[:, :], 0.0))
            select(ident[:, :], ALU.not_equal, 1.0, 0, 1, [[-1, P]])
            const(pool.memset(ones[:, :], 1.0))
            const(pool.memset(eps[:, :], EPS))
            const(pool.memset(triu[:, :], 1.0))
            select(triu[:, :], ALU.is_ge, 0.0, 0, -1, [[1, P]])
            const(pool.memset(mask_lo[:, :], 0.0))
            select(mask_lo[:, :], ALU.is_ge, NEG, -1, 1, [[-1, P]])
            const(pool.memset(mask_up[:, :], 0.0))
            select(mask_up[:, :], ALU.is_ge, NEG, 0, -1, [[1, P]])
            const(pool.memset(pair_t[:, :, :], 0.0))
            for lv in range(LEVELS):
                s = 1 << lv
                odd = pair_t[:, lv, :].rearrange("p (a two s) -> p a two s", two=2, s=s)[:, :, 1, :]
                const(pool.memset(odd, 1.0))
                select(odd, ALU.is_ge, 0.0, 0, 1, [[-2 * s, P // (2 * s)], [0, s]])
                select(odd, ALU.is_ge, 0.0, s - 1, -1, [[2 * s, P // (2 * s)], [0, s]])
            const(pool.memset(pair1[:, :], 0.0))
            even = pair1[:, :].rearrange("p (a two) -> p a two", two=2)[:, :, 0]
            select(even, ALU.not_equal, 1.0, -1, 1, [[-2, P // 2]])

            assert n_const[0] == CONSTS

            def split_w(u, k, p):
                pool.wait_ge(w_loaded[p], past(16 * k + 16))
                pool.wait_ge(block_done[p], past(RB * k))
                wait_apart(pool, pool_waited)
                pool.tensor_copy(w_hi[p][:, :, :], w_raw[p][:, :, :]).then_inc(w_hi_done, 1)
                pool.wait_ge(w_hi_done, past(u + 1))
                pool.tensor_tensor(w_lo[p][:, :, :], w_raw[p][:, :, :], w_hi[p][:, :, :].bitcast(F32),
                                   ALU.subtract).then_inc(w_ready, 1)

            with pool.Fori(0, UNITS // 2) as i:
                for p in range(2):
                    split_w(2 * i + p, i, p)
            split_w(UNITS, UNITS // 2, 0)
            arrive(pool, 0)

            def bc(t, c):
                return t[:, ds(H * c, H)].rearrange("p (h o) -> p h o", o=1).to_broadcast([P, H, P])

            def per_head(m):
                return m.rearrange("p (o c) -> p o c", o=1).to_broadcast([P, H, P])

            def chunk_pair(k, kp, first=False, last=False):
                if not first:
                    decay(2 * k - 2, 0)
                for p in range(2):
                    c = 2 * k + p
                    pool.wait_ge(G["cumb"], past(2 * k))
                    pool.tensor_tensor(g_tri[p][:, :, :], per_head(triu[:, :]), bc(tab["g"], c), ALU.mult
                                       ).then_inc(G["tri"], 1)
                for p in range(2):
                    c = 2 * k + p
                    pool.wait_ge(G["masked"], past(4 * k))
                    pool.tensor_tensor(dec[p][:, 0, :, :], per_head(mask_lo[:, :]), bc(tab["cum"], c), ALU.add
                                       ).then_inc(G["mask"], 1)
                    pool.tensor_tensor(dec[p][:, 1, :, :], per_head(mask_up[:, :]), bc(tab["cum"], c),
                                       ALU.subtract).then_inc(G["mask"], 1)
                for p in range(2):
                    c = 2 * k + p
                    pool.wait_ge(G["decay"], past(c + 1))
                    pool.tensor_tensor(dec[p][:, 0, :, :], dec[p][:, 0, :, :], bc(tab["beta"], c), ALU.mult
                                       ).then_inc(G["decay_b"], 1)
                for p in range(2):
                    pool.wait_ge(G["lowt_sb"], past(2 * k + p + 1))
                    pool.wait_ge(G["u_mm"], past(4 * k))
                    for lv in range(2):
                        pool.tensor_tensor(pairM[p][:, lv, :, :], lowT[p][:, :, :], per_head(pair_t[:, lv, :]),
                                           ALU.mult).then_inc(G["pair"], 1)
                        if lv == 0:
                            pool.wait_ge(G["pair"], past(2 * LEVELS * k + 2 * p + 1))
                            pool.tensor_tensor(Tt[p][:, :, :], per_head(ident[:, :]), pairM[p][:, 0, :, :],
                                               ALU.subtract).then_inc(G["T"], 1)
                for lv in range(2, LEVELS):
                    for p in range(2):
                        pool.tensor_tensor(pairM[p][:, lv, :, :], lowT[p][:, :, :], per_head(pair_t[:, lv, :]),
                                           ALU.mult).then_inc(G["pair"], 1)
                    if lv == 2 and not first:
                        decay(2 * k - 1, 1)
                for p in range(2):
                    q = 2 * kp + p
                    pool.wait_ge(G["ecum"], past(2 * k + p + 1))
                    pool.wait_ge(G["qkn"], past(4 * k + 2 * p + 2))
                    if not first:
                        pool.wait_ge(G["o_mm"], past(2 * k - 2))
                    pool.tensor_tensor(q_dec[q][:, :, :], qkn[p][:, 0:H, :], e_cum[p][:, :, :], ALU.mult
                                       ).then_inc(G["qdec"], 1)

            def decay(c, p):
                pool.wait_ge(G["state"], past(c))
                pool.tensor_tensor(state_d[:, :, :], state[p][:, :, :], bc(tab["e_last"], c), ALU.mult
                                   ).then_inc(G["sdec"], 1)

            pool.memset(state[0][:, :, :], 0.0).then_inc(G["zero"], 1)
            pool.wait_ge(G["zero"], past(1))
            pairs(pool, chunk_pair, lambda: (decay(TILES - 2, 0), decay(TILES - 1, 1)))
            arrive(pool, 1)

            pool.iota(dist[:, :], [[1, SEQ]], base=P - SEQ, channel_multiplier=-1,
                      allow_small_or_imprecise_dtypes=True).then_inc(A["dist"], 1)
            pool.wait_ge(A["dist"], past(1))
            pool.affine_select(out=dist[:, :], in_=dist[:, :], compare_op=ALU.is_ge, fill=NEG, base=SEQ - P,
                               channel_multiplier=1, pattern=[[-1, SEQ]]).then_inc(A["dist"], 1)
            with pool.Fori(0, H // MAPS) as i:
                for p in range(2):
                    h = 2 * i + p
                    pool.wait_ge(A["dist"], past(2 * h + 2))
                    wait_apart(pool, pool_waited)
                    pool.tensor_scalar(dist[:, :], dist[:, :], SLOPE, 1.0, ALU.mult, ALU.mult
                                       ).then_inc(A["dist"], 1)
                    pool.wait_ge(A["dist"], past(2 * h + 3))
                    pool.wait_ge(a_y[p], past(RB * i))
                    wait_apart(pool, pool_waited)
                    pool.tensor_scalar(bias[p][:, :], dist[:, :], 1.0, 1.0, ALU.mult, ALU.mult
                                       ).then_inc(A["dist"], 1)
            arrive(pool, 2)

            with pool.Fori(0, RB) as r:
                for d in range(KT):
                    for b in range(3):
                        n = 3 * d + b
                        pool.wait_ge(M["wb_hi"], past(24 * r + n + 1))
                        pool.tensor_tensor(wb_lo[n % 3][:, :, :], wb_in[n % 2][:, :, :],
                                           wb_hi[n % 3][:, :, :].bitcast(F32), ALU.subtract
                                           ).then_inc(wb_free[n % 2], 1)
                        if b == 1 and d:
                            sum_last(pool, r, d - 1)
                sum_last(pool, r, KT - 1)

        @block.tensor
        def _(pe):
            def mm3(dst, lhs, rhs, first, last):
                pe.matmul(dst, lhs[0], rhs[0], start=first, stop=False)
                pe.matmul(dst, lhs[0], rhs[1], start=False, stop=False)
                return pe.matmul(dst, lhs[1], rhs[0], start=False, stop=last)

            pe.wait_ge(const_step, CONSTS)
            pe.wait_ge(vec_loaded, 128)
            pe.transpose(bank[0][:, 0:VECS], vec_rows[:, :], ident[0:VECS, 0:VECS]).then_inc(vec_turned, 1)
            with pe.Fori(0, TILES // 4) as i:
                for q in range(4):
                    p = q % 2
                    pe.wait_ge(x_scaled, past(4 * i + q + 1))
                    pe.wait_ge(h_lo_done[p], past(2 * (2 * i + q // 2)))
                    for k in range(KT):
                        last = pe.transpose(bank[4 + 2 * p + k // 4][:, (k % 4) * P:(k % 4 + 1) * P],
                                            x_in[q][:, k * P:(k + 1) * P], ident[:, :])
                    last.then_inc(x_used[q], 1)
            pe.wait_ge(h_lo_done[0], past(TILES))
            pe.wait_ge(h_lo_done[1], past(TILES))
            pe.wait_ge(vec_ready, 1)

            def project(u, p):
                pe.wait_ge(w_ready, past(u + 1))
                for rb in range(RB):
                    pe.wait_ge(bank_free[rb], past(u))
                    for k in range(KT):
                        cols = slice(rb * R, (rb + 1) * R)
                        last = mm3(bank[rb][:, :], (w_hi[p][:, k, :], w_lo[p][:, k, :]),
                                   (hT_hi[:, k, cols], hT_lo[:, k, cols]), k == 0, k == KT - 1)
                    last.then_inc(block_done[p], 1)

            with pe.Fori(0, UNITS // 2) as i:
                for p in range(2):
                    project(2 * i + p, p)
            project(UNITS, 0)

            pe.wait_ge(bank_free[RB - 1], past(UNITS + 1))
            for c in range(TILES):
                last = pe.transpose(bank[4][:, 2 * H * c:2 * H * (c + 1)], abT[0:2 * H, c * P:(c + 1) * P],
                                    ident[0:2 * H, 0:2 * H])
            last.then_inc(ab_turned, 1)
            pe.wait_ge(tab_v, 3)
            pe.matmul(bank[5][:, 0:TILES * H], triu[:, :], tab["g"][:, :], start=True, stop=True)
            pe.matmul(bank[5][:, TILES * H:2 * TILES * H], ones[:, :], tab["g"][:, :], start=True, stop=True
                      ).then_inc(tab_mm, 1)
            arrive(pe, 0)

            def heads(dst, lhs, rhs):
                for h in range(H):
                    last = pe.matmul(dst[:, h * P:(h + 1) * P], lhs[:, h, :], rhs[:, h, :],
                                     start=True, stop=True)
                return last

            def against_state(c, q):
                pe.wait_ge(G["uw_sb"], past(2 * c + 2))
                pe.wait_ge(G["state"], past(c))
                pe.wait_ge(G["zero"], past(1))
                pe.wait_ge(N["on"], past(c))
                heads(bank[6], WT[q % 2], state[q % 2]).then_inc(G["ws"], 1)

            def new_state(c, q):
                pe.wait_ge(G["vnew"], past(c + 1))
                pe.wait_ge(N["rso_ln"], past(c))
                heads(bank[7], k_dec[q], v_new).then_inc(G["s_mm"], 1)
                pe.wait_ge(G["qdec"], past(c + 1))
                for h in range(H):
                    cols = slice(h * P, (h + 1) * P)
                    pe.matmul(bank[6][:, cols], state[q % 2][:, h, :], q_dec[q][:, h, :], start=True, stop=False)
                    last = pe.matmul(bank[6][:, cols], v_new[:, h, :], qk_m[q][:, h, :],
                                     start=False, stop=True)
                last.then_inc(G["o_mm"], 1)

            def out_squares(c):
                pe.wait_ge(N["sqo"], past(c + 1))
                pe.wait_ge(G["state"], past(c + 1))
                pe.matmul(bank[7][:, :], ones[:, :], sq_o[:, :, :], start=True, stop=True
                          ).then_inc(N["sso"], 1)

            def chunk_pair(k, kp, first=False, last=False):
                c0 = 2 * k
                old, old_q = c0 - 2, 2 * (1 - kp)
                pe.wait_ge(G["uw_sb"], past(4 * k))
                for p in range(2):
                    pe.wait_ge(G["sq"], past(c0 + p + 1))
                    pe.matmul(bank[3 * p][:, :], ones[:, :], sq_qk[p][:, 0:H, :], start=True, stop=True)
                    pe.matmul(bank[3 * p + 1][:, :], ones[:, :], sq_qk[p][:, H:2 * H, :], start=True, stop=True
                              ).then_inc(G["ss"], 1)
                if not first:
                    against_state(old, old_q)
                for p in range(2):
                    pe.wait_ge(G["tri"], past(c0 + p + 1))
                    pe.matmul(bank[3 * p + 2][:, :], ones[:, :], g_tri[p][:, :, :], start=True, stop=True
                              ).then_inc(G["cumb"], 1)
                for p in range(2):
                    pe.wait_ge(G["rs_ln"], past(2 * c0 + 2 * p + 1))
                    for h in range(H):
                        end = pe.transpose(bank[3 * p][:, h * P:(h + 1) * P], qkv_in[p][:, 2 * H + h, :],
                                           ident[:, :])
                    end.then_inc(G["turn"], 1)
                if not first:
                    new_state(old, old_q)
                for p in range(2):
                    kn = qkn[p][:, H:2 * H, :]
                    pe.wait_ge(G["qkn"], past(2 * c0 + 2 * p + 1))
                    for h in range(H):
                        end = pe.transpose(bank[3 * p + 1][:, h * P:(h + 1) * P], kn[:, h, :], ident[:, :])
                    end.then_inc(G["turn"], 1)
                    pe.wait_ge(G["diff"], past(2 * c0 + 2 * p + 2))
                    heads(bank[3 * p + 2], kn, kn).then_inc(G["kk"], 1)
                for p in range(2):
                    pe.wait_ge(G["qkn"], past(2 * c0 + 2 * p + 2))
                    pe.wait_ge(G["rows"], past(6 * k + p + 1))
                    heads(bank[3 * p], qkn[p][:, H:2 * H, :], qkn[p][:, 0:H, :]).then_inc(G["kk"], 1)
                for p in range(2):
                    pe.wait_ge(G["masked"], past(4 * k + p + 1))
                    for h in range(H):
                        end = pe.transpose(bank[3 * p + 2][:, h * P:(h + 1) * P], low[p][:, h, :], ident[:, :])
                    end.then_inc(G["lowt"], 1)
                if not first:
                    out_squares(old)
                for lv in range(1, LEVELS):
                    for p in range(2):
                        pe.wait_ge(G["pair"], past(2 * LEVELS * k + (2 * p + 2 if lv == 1 else 2 * lv + p + 1)))
                        if lv == 1:
                            pe.wait_ge(G["t0"], past(2 * c0 + 2 * p + 2))
                            pe.wait_ge(G["masked"], past(4 * k + p + 3))
                        else:
                            pe.wait_ge(G["t_new"], past(level(k, lv - 1, p)))
                        heads(bank[3 * p], pairM[p][:, lv, :, :], T[p]).then_inc(G["x_mm"], 1)
                    if not first and lv == 2:
                        against_state(old + 1, old_q + 1)
                    if not first and lv == 3:
                        new_state(old + 1, old_q + 1)
                    if not first and lv == 5:
                        out_squares(old + 1)
                    for p in range(2):
                        if lv == 1:
                            pe.wait_ge(G["T"], past(c0 + p + 1))
                            pe.wait_ge(G["rows"], past(6 * k + 2 * p + 4))
                        pe.wait_ge(G["x_sb"], past(level(k, lv, p)))
                        if lv < LEVELS - 1:
                            heads(bank[3 * p + 2], Tt[p], X[p]).then_inc(G["y_mm"], 1)
                        heads(bank[3 * p + 1], X[p], Tt[p]).then_inc(G["y_mm"], 1)
                for p in range(2):
                    pe.wait_ge(G["t_new"], past(level(k, LEVELS - 1, p)))
                    heads(bank[3 * p], Tt[p], v_beta[p]).then_inc(G["u_mm"], 1)
                    heads(bank[3 * p + 2], k_beta[p], Tt[p]).then_inc(G["u_mm"], 1)

            def last_states():
                for p in range(2):
                    c = TILES - 2 + p
                    against_state(c, 2 + p)
                    new_state(c, 2 + p)
                    out_squares(c)

            pairs(pe, chunk_pair, last_states)
            arrive(pe, 1)

            with pe.Fori(0, H // MAPS) as i:
                for p in range(2):
                    h = 2 * i + p
                    turns = [0]
                    scored = [0]

                    def turn_bank():
                        n = turns[0]
                        turns[0] += 1
                        pe.wait_ge(turn_free[n % 2], past(TURNS // 2 * h + n // 2))
                        return bank[4 + n % 2]

                    def scores(b):
                        for m in range(MAPS):
                            part = slice(m * QK_DIM, (m + 1) * QK_DIM)
                            for g in range(b // RB + 1):
                                n = scored[0]
                                scored[0] += 1
                                w = min(R, (b + 1) * P - g * R)
                                pe.wait_ge(score_free[n % 4], past(SCORES // 4 * h + n // 4))
                                pe.matmul(bank[n % 4][:, 0:w], q_in[p][part, b * P:(b + 1) * P],
                                          k_in[p][part, g * R:g * R + w], start=True, stop=True
                                          ).then_inc(A["score"], 1)

                    def square_sum(sb):
                        pe.wait_ge(N["sqo"], past(TILES + RB * h + sb + 1))
                        pe.wait_ge(N["rso_ln"], past(TILES + RB * h + sb))
                        pe.matmul(bank[7][:, :], ones[:, :], sq_b[:, :], start=True, stop=True
                                  ).then_inc(N["sso"], 1)

                    pe.wait_ge(head_loaded[p], past(64 * i + 64))
                    scores(0)
                    scores(1)
                    for g in range(RB):
                        dst = turn_bank()
                        for k in range(RB):
                            last = pe.transpose(dst[:, k * P:(k + 1) * P],
                                                v_in[p][:, (g * RB + k) * P:(g * RB + k + 1) * P], ident[:, :])
                        last.then_inc(A["turn"], 1)
                    for b in range(TILES):
                        if b + 2 < TILES:
                            scores(b + 2)
                        if b and b % RB == 0:
                            square_sum(b // RB - 1)
                        pe.wait_ge(A["probs"], past(TILES * h + b + 1))
                        for g in range(b // RB + 1):
                            dst = turn_bank()
                            for k in range(min(RB, b + 1 - g * RB)):
                                kb = g * RB + k
                                last = pe.transpose(dst[:, k * P:(k + 1) * P],
                                                    s_buf[b % AHEAD][:, 0, kb * P:(kb + 1) * P], ident[:, :])
                            last.then_inc(A["turn"], 1)
                        n = turns[0] - 1
                        pe.wait_ge(turn_free[n % 2], past(TURNS // 2 * h + n // 2 + 1))
                        pe.wait_ge(turn_free[(n + 1) % 2], past(TURNS // 2 * h + (n - 1) // 2 + 1))
                        if b % RB == 0:
                            pe.wait_ge(N["on"], past(TILES + RB * h + b // RB))
                        for kb in range(b + 1):
                            last = pe.matmul(bank[6][:, (b % RB) * P:(b % RB + 1) * P], v_rows[:, kb, :],
                                             probsT[b % 2][:, kb, :], start=(kb == 0), stop=(kb == b))
                        last.then_inc(a_pv[b % AHEAD], 1)
                    square_sum(RB - 1)
                    assert turns[0] == TURNS and scored[0] == SCORES
            arrive(pe, 2)

            with pe.Fori(0, RB) as r:
                pe.wait_ge(M["y_lo"], past(3 * r + 3))
                for d in range(KT):
                    for b in range(3):
                        n = 3 * d + b
                        half = KT // 2
                        pe.wait_ge(wb_free[n % 2], past(12 * r + n // 2 + 1))
                        pe.wait_ge(gated_done[n % 6], past(half * r + n // 6))
                        if n < 2:
                            pe.wait_ge(M["normed"], past(RB * r))
                        for k in range(H):
                            last = mm3(bank[n % 6][:, :], (wb_hi[n % 3][:, k, :], wb_lo[n % 3][:, k, :]),
                                       (y_hi[:, H * b + k, :], y_lo[:, H * b + k, :]), k == 0, k == H - 1)
                        last.then_inc(mm_done[n % 3], 1)
                pe.wait_ge(M["lo"], past(KT * r + KT))
                pe.wait_ge(M["wo_lo"], past(KT))
                for t in range(RB):
                    pe.wait_ge(M["normed"], past(RB * r + max(0, t - 1)))
                    for nb in range(2):
                        dst = bank[(6, 0)[t % 2] + nb]
                        for d in range(KT):
                            rows = slice(t * P, (t + 1) * P)
                            cols = slice(nb * R, (nb + 1) * R)
                            last = mm3(dst[:, :], (m_hi[:, d, rows], m_lo[:, d, rows]),
                                       (wo_hi[:, d, cols], wo_lo[:, d, cols]), d == 0, d == KT - 1)
                        last.then_inc(M["out_mm"], 1)

        @block.scalar
        def _(act):
            def f(out_, in_, func, **kw):
                return act.activation(out_, in_, func, **kw)

            def row_scale(i, q):
                t = 4 * i + q
                act.wait_ge(x_loaded[q], past(16 * i + 16))
                f(x_junk[:, :], x_in[q][:, :], ACT.Square, accum_out=x_stat[:, q, 0:1]).then_inc(x_square, 1)
                act.wait_ge(x_square, past(t + 1))
                f(x_stat[:, q, 1:2], x_stat[:, q, 0:1], ACT.Sqrt, scale=1.0 / D, bias=eps[:, 0:1]
                  ).then_inc(x_root, 1)

            def take_hi(i, q):
                t = 4 * i + q
                act.wait_ge(x_used[q], past(i + 1))
                for n in range(2):
                    f(hT_hi[:, 4 * n:4 * n + 4, ds(t * P, P)], hp(bank[4 + 2 * (q % 2) + n]), ACT.Copy
                      ).then_inc(h_hi_done, 1)

            act.wait_ge(const_step, CONSTS)
            row_scale(0, 0)
            row_scale(0, 1)
            with act.Fori(0, TILES // 4 - 1) as i:
                for q in range(4):
                    take_hi(i, q)
                    row_scale(i + (q + 2) // 4, (q + 2) % 4)
            last_i = TILES // 4 - 1
            for q in range(4):
                take_hi(last_i, q)
                if q < 2:
                    row_scale(last_i, q + 2)
            act.wait_ge(vec_loaded, 128)
            act.wait_ge(lam_step, 2)
            f(lam_s[:, 2:4], lam_s[:, 0:2], ACT.Exp).then_inc(lam_step, 1)

            def store(dst, p, sp_sem, value):
                act.wait_ge(sp_sem, past(value))
                act.dma_start(dst, stage[p][:, :]).then_inc(stored[p], 16)

            def one(t, u):
                return t[ds(u, 1), :, :].rearrange("o p r -> p (o r)")

            act.wait_ge(h_lo_done[1], past(TILES))
            act.wait_ge(raw_zero, 1)
            with act.Fori(0, U_ZA // 2) as i:
                for p in range(2):
                    u = 2 * i + p
                    act.wait_ge(conv_done[p], past(i))
                    for rb in range(RB):
                        act.wait_ge(block_done[p], past(RB * i + rb + 1))
                        f(raw[p][:, GDN_CONV - 1 + rb * R:GDN_CONV - 1 + (rb + 1) * R], bank[rb][:, :], ACT.Copy
                          ).then_inc(bank_free[rb], 1)
                    act.wait_ge(conv_done[p], past(i + 1))
                    f(stage[p][:, :], stage[p][:, :], ACT.Silu).then_inc(silu_done, 1)
                    store(one(saved, u), p, silu_done, u + 1)

            def direct(first, count, func, dst, dst_first, stored_before, **kw):
                with act.Fori(0, count // 2) as i:
                    for p in range(2):
                        k = i + first // 2
                        act.wait_ge(stored[p], past(16 * (i + stored_before[p])))
                        for rb in range(RB):
                            act.wait_ge(block_done[p], past(RB * k + rb + 1))
                            f(stage[p][:, rb * R:(rb + 1) * R], bank[rb][:, :], func, **kw
                              ).then_inc(bank_free[rb], 1)
                        store(one(dst, 2 * i + (dst_first + p)), p, bank_free[RB - 1], 2 * i + (first + p + 1))

            for first, count, func, kw in ((U_ZA, 4, ACT.Silu, {}), (U_Q, 4, ACT.Copy, {"scale": QK_DIM ** -0.5}),
                                           (U_K, 8, ACT.Copy, {}), (U_ZB, 4, ACT.Silu, {})):
                direct(first, count, func, saved, first, (first // 2, first // 2), **kw)
            with act.Fori(0, H) as j:
                k = 2 * j + U_SAVED // 2
                act.wait_ge(sc_conv_done, past(j))
                for rb in range(RB):
                    act.wait_ge(block_done[0], past(RB * k + rb + 1))
                    f(raw[0][:, GDN_CONV - 1 + rb * R:GDN_CONV - 1 + (rb + 1) * R], bank[rb][:, :], ACT.Copy
                      ).then_inc(bank_free[rb], 1)
                act.wait_ge(yc_done, past(j))
                act.wait_ge(stored[1], past(16 * (U_SAVED // 2)))
                for rb in range(RB):
                    act.wait_ge(block_done[1], past(RB * k + (RB + rb + 1)))
                    f(stage[1][:, rb * R:(rb + 1) * R], bank[rb][:, :], ACT.Silu).then_inc(bank_free[rb], 1)
                act.wait_ge(yc_done, past(j + 1))
                act.dma_start(one(y_all, j + 2 * H), stage[0][:, :]).then_inc(stored[0], 16)
            direct(U_SAVED + 4 * H, 3 * KT, ACT.Sigmoid, gates, 0, (U_SAVED // 2 + H, U_SAVED // 2))
            for rb in range(RB):
                act.wait_ge(block_done[0], past(RB * (UNITS // 2) + rb + 1))
                f(abT[0:2 * H, rb * R:(rb + 1) * R], bank[rb][0:2 * H, :], ACT.Copy).then_inc(bank_free[rb], 1)

            ab = bank[4][:, 0:TILES * 2 * H].rearrange("p (c e) -> p c e", e=2 * H)
            act.wait_ge(tab_v, 1)
            f(tab["beta"][:, :].rearrange("p (c h) -> p c h", h=H), ab[:, :, 0:H], ACT.Sigmoid).then_inc(tab_a, 1)
            f(tab["t1"][:, :], tab["t0"][:, :], ACT.Abs).then_inc(tab_a, 1)
            act.wait_ge(tab_a, 2)
            f(tab["t1"][:, :], tab["t1"][:, :], ACT.Exp, scale=-1.0).then_inc(tab_a, 1)
            f(head_in[:, 0, :], head_in[:, 0, :], ACT.Exp).then_inc(tab_a, 1)
            act.wait_ge(tab_a, 4)
            f(tab["t1"][:, :], tab["t1"][:, :], ACT.Ln, bias=ones[:, 0:1]).then_inc(tab_a, 1)
            act.wait_ge(tab_v, 5)
            f(tab["k_decay"][:, :], tab["t0"][:, :], ACT.Exp).then_inc(tab_a, 1)
            f(tab["e_last"][:, :], bank[5][:, TILES * H:2 * TILES * H], ACT.Exp).then_inc(tab_a, 1)
            f(tab["t1"][:, :], tab["cum"][:, :], ACT.Exp).then_inc(tab_a, 1)
            act.wait_ge(stored[0], past(16 * (U_SAVED // 2 + H + 3 * KT // 2)))
            act.wait_ge(stored[1], past(16 * (U_SAVED // 2 + 3 * KT // 2)))
            arrive(act, 0)

            def squares(k):
                for p in range(2):
                    act.wait_ge(qkv_loaded[p], past(16 * k + 16))
                    act.wait_ge(G["ss"], past(2 * k))
                    f(sq_qk[p][:, :, :], qkv_in[p][:, 0:2 * H, :], ACT.Square).then_inc(G["sq"], 1)

            def out_squares(c):
                act.wait_ge(G["o_mm"], past(c + 1))
                act.wait_ge(N["sso"], past(c))
                f(sq_o[:, :, :], hp(bank[6]), ACT.Square).then_inc(N["sqo"], 1)

            def out_scale(c):
                act.wait_ge(N["sso"], past(c + 1))
                act.wait_ge(N["on"], past(c))
                f(rs_o[:, :, :], hp(bank[7]), ACT.Ln, scale=1.0 / P, bias=eps[:, 0:1]).then_inc(N["rso_ln"], 1)
                act.wait_ge(N["rso_ln"], past(c + 1))
                f(rs_o[:, :, :], rs_o[:, :, :], ACT.Exp, scale=-0.5).then_inc(N["rso"], 1)

            def save_out(c, k, p):
                act.wait_ge(g_y[p], past(k + 1))
                act.dma_start(y_all[0:H, :, ds(c * P, P)].rearrange("h p r -> p h r"), y_a[:, :, :]
                              ).then_inc(N["y_stored"], 16)

            def chunk_pair(k, kp, first=False, last=False):
                c0 = 2 * k
                for p in range(2):
                    act.wait_ge(G["ss"], past(c0 + p + 1))
                    act.wait_ge(G["qkn"], past(4 * k))
                    for n in range(2):
                        f(rs_qk[p][:, n * H:(n + 1) * H, :], hp(bank[3 * p + n]), ACT.Ln, bias=eps[:, 0:1]
                          ).then_inc(G["rs_ln"], 1)
                    act.wait_ge(G["rs_ln"], past(2 * c0 + 2 * p + 2))
                    f(rs_qk[p][:, :, :], rs_qk[p][:, :, :], ACT.Exp, scale=-0.5).then_inc(G["rs"], 1)
                for p in range(2):
                    act.wait_ge(G["cumb"], past(c0 + p + 1))
                    act.wait_ge(G["qdec"], past(c0))
                    f(e_cum[p][:, :, :], hp(bank[3 * p + 2]), ACT.Exp).then_inc(G["ecum"], 1)
                for p in range(2):
                    act.wait_ge(G["diff"], past(2 * c0 + 2 * p + 2))
                    f(dec[p][:, :, :, :], dec[p][:, :, :, :], ACT.Exp).then_inc(G["decay"], 1)
                if not first:
                    out_squares(c0 - 2)
                for p in range(2):
                    act.wait_ge(G["lowt"], past(c0 + p + 1))
                    act.wait_ge(G["pair"], past(2 * LEVELS * k))
                    f(lowT[p][:, :, :], hp(bank[3 * p + 2]), ACT.Copy).then_inc(G["lowt_sb"], 1)
                if not first:
                    out_scale(c0 - 2)
                for lv in range(1, LEVELS):
                    for p in range(2):
                        act.wait_ge(G["x_mm"], past(level(k, lv, p)))
                        f(X[p][:, :, :], hp(bank[3 * p]), ACT.Copy).then_inc(G["x_sb"], 1)
                    if not first and lv == 2:
                        save_out(c0 - 2, k - 1, 0)
                    if not first and lv == 4:
                        out_squares(c0 - 1)
                    if not first and lv == 5:
                        out_scale(c0 - 1)
                if not last:
                    squares(k + 1)
                if not first:
                    save_out(c0 - 1, k - 1, 1)
                for p in range(2):
                    act.wait_ge(G["vnew"], past(c0))
                    act.wait_ge(G["u_mm"], past(2 * c0 + 2 * p + 1))
                    f(U[p][:, :, :], hp(bank[3 * p]), ACT.Copy).then_inc(G["uw_sb"], 1)
                    act.wait_ge(G["u_mm"], past(2 * c0 + 2 * p + 2))
                    f(WT[p][:, :, :], hp(bank[3 * p + 2]), ACT.Copy).then_inc(G["uw_sb"], 1)

            def last_outs():
                for p in range(2):
                    out_squares(TILES - 2 + p)
                    out_scale(TILES - 2 + p)
                    save_out(TILES - 2 + p, TILES // 2 - 1, p)

            squares(0)
            pairs(act, chunk_pair, last_outs)
            act.wait_ge(N["y_stored"], past(16 * TILES))
            arrive(act, 1)

            with act.Fori(0, H // MAPS) as i:
                for p in range(2):
                    h = 2 * i + p
                    turns = [0]

                    def turned(dst):
                        n = turns[0]
                        turns[0] += 1
                        act.wait_ge(A["turn"], past(TURNS * h + n + 1))
                        w = dst.shape[1]
                        f(dst, bank[4 + n % 2][:, 0:w * P].rearrange("p (k c) -> p k c", c=P), ACT.Copy
                          ).then_inc(turn_free[n % 2], 1)

                    def exps(b):
                        act.wait_ge(A["negtop"], past(TILES * h + b + 1))
                        for m in range(MAPS):
                            n = b % AHEAD
                            s = s_buf[n][:, m, 0:(b + 1) * P]
                            f(s, s, ACT.Exp, bias=neg_top[n][:, m:m + 1], accum_out=den[n][:, m:m + 1]
                              ).then_inc(A["exp"], 1)

                    def out_norm(sb):
                        n = RB * h + sb
                        act.wait_ge(a_pv[AHEAD - 1], past(RB * h + sb + 1))
                        act.wait_ge(N["sso"], past(TILES + n))
                        f(sq_b[:, :], bank[6][:, :], ACT.Square).then_inc(N["sqo"], 1)
                        act.wait_ge(N["sso"], past(TILES + n + 1))
                        act.wait_ge(N["on"], past(TILES + n))
                        f(rs_b[:, :], bank[7][:, :], ACT.Ln, scale=1.0 / P, bias=eps[:, 0:1]
                          ).then_inc(N["rso_ln"], 1)
                        act.wait_ge(N["rso_ln"], past(TILES + n + 1))
                        f(rs_b[:, :], rs_b[:, :], ACT.Exp, scale=-0.5).then_inc(N["rso"], 1)

                    def save(sb):
                        act.wait_ge(a_y[p], past(RB * i + sb + 1))
                        act.dma_start(y_all[ds(h + H, 1), :, sb * R:(sb + 1) * R].rearrange("o p r -> p (o r)"),
                                      y_b[:, :]).then_inc(N["y_stored"], 16)

                    act.wait_ge(a_pv[AHEAD - 1], past(RB * h))
                    exps(0)
                    exps(1)
                    for g in range(RB):
                        turned(v_rows[:, g * RB:(g + 1) * RB, :])
                    for b in range(TILES):
                        if b and b % RB == 0:
                            out_norm(b // RB - 1)
                        act.wait_ge(a_pv[(b - 2) % AHEAD], past(RB * h + (b + 2) // AHEAD))
                        for g in range(b // RB + 1):
                            turned(probsT[b % 2][:, g * RB:min((g + 1) * RB, b + 1), :])
                        if b + 2 < TILES:
                            exps(b + 2)
                        if b and b % RB == 0:
                            save(b // RB - 1)
                    out_norm(RB - 1)
                    save(RB - 1)
            act.wait_ge(N["y_stored"], past(16 * TILES + 16 * RB * H))
            arrive(act, 2)

            def wb_split(r, n):
                act.wait_ge(wb_loaded[n % 2], past(192 * r + 16 * (n // 2) + 16))
                act.wait_ge(mm_done[n % 3], past(KT * r + n // 3))
                f(wb_hi[n % 3][:, :, :], wb_in[n % 2][:, :, :], ACT.Copy).then_inc(M["wb_hi"], 1)

            def y_split(r, b):
                act.wait_ge(M["y_loaded"], past(48 * r + 16 * b + 16))
                act.wait_ge(mm_done[2], past(KT * r))
                f(y_hi[:, H * b:H * (b + 1), :], y_in[:, :, :], ACT.Copy).then_inc(M["y_hi"], 1)

            def m_split(r, d):
                act.wait_ge(M["sum2"], past(KT * r + d + 1))
                if d == 0:
                    act.wait_ge(M["out_mm"], past(2 * RB * r))
                f(m_hi[:, d, :], gated[0][:, :], ACT.Copy).then_inc(M["hi"], 1)

            def merge(r, first=False, last=False):
                for d in range(KT):
                    for b in range(3):
                        wb_split(r, 3 * d + b)
                        if b == 1 and d:
                            m_split(r, d - 1)
                    if first:
                        act.wait_ge(M["wo_loaded"], past(16 * d + 16))
                        f(wo_hi[:, d, :], x_res[d % 2][:, :], ACT.Copy).then_inc(M["wo_hi"], 1)
                m_split(r, KT - 1)
                for t in range(RB):
                    n = RB * r + t
                    if not last and t:
                        y_split(r + 1, t - 1)
                    act.wait_ge(M["done"], past(n))
                    for nb in range(2):
                        act.wait_ge(M["out_mm"], past(2 * n + nb + 1))
                        f(o_norm[:, nb * R:(nb + 1) * R], bank[(6, 0)[t % 2] + nb][:, :], ACT.Square,
                          accum_out=o_stat[:, nb:nb + 1]).then_inc(M["sq"], 1)
                    act.wait_ge(M["ss"], past(n + 1))
                    f(o_stat[:, 3:4], o_stat[:, 2:3], ACT.Sqrt, scale=1.0 / D, bias=eps[:, 0:1]
                      ).then_inc(M["root"], 1)
                    act.wait_ge(M["done"], past(n + 1))
                    act.dma_start(out_rows[ds(n, 1), :, :].rearrange("o p d -> p (o d)"), x_res[t % 2][:, :]
                                  ).then_inc(out_stored[t % 2], 16)

            for b in range(3):
                y_split(0, b)
            merge(0, first=True)
            with act.Fori(1, RB - 1) as r:
                merge(r)
            merge(RB - 1, last=True)

        @block.vector
        def _(dve):
            def stt(out_, a, s, b, op0, op1):
                return dve.scalar_tensor_tensor(out_, a, s, b, op0, op1)

            def tt(out_, a, b, op):
                return dve.tensor_tensor(out_, a, b, op)

            dve.wait_ge(vec_turned, 1)
            dve.tensor_copy(vec[:, :], bank[0][:, 0:VECS]).then_inc(vec_ready, 1)
            dve.wait_ge(vec_ready, 1)
            dve.tensor_scalar(diff_w[:, :], vec[:, VEC_DIFF:VEC_DIFF + 1], 1.0 - LAM_INIT, None, ALU.mult
                              ).then_inc(vec_ready, 1)
            for m in range(2):
                dve.tensor_tensor_reduce(lam_in[:, 2 * m, :], lam_in[:, 2 * m, :], lam_in[:, 2 * m + 1, :], 1.0, 0.0,
                                         ALU.mult, ALU.add, lam_s[:, m:m + 1]).then_inc(lam_step, 1)

            def scale_rows(i, q):
                t = 4 * i + q
                dve.wait_ge(x_root, past(t + 1))
                dve.reciprocal(x_stat[:, q, 2:3], x_stat[:, q, 1:2]).then_inc(x_inv, 1)
                dve.wait_ge(x_inv, past(t + 1))
                stt(x_in[q][:, :], x_in[q][:, :], x_stat[:, q, 2:3], pre_w[:, :], ALU.mult, ALU.mult
                    ).then_inc(x_scaled, 1)

            def take_lo(i, q):
                t = 4 * i + q
                for n in range(2):
                    dve.wait_ge(h_hi_done, past(2 * t + n + 1))
                    part = slice(4 * n, 4 * n + 4)
                    tt(hT_lo[:, part, ds(t * P, P)], hp(bank[4 + 2 * (q % 2) + n]),
                       hT_hi[:, part, ds(t * P, P)].bitcast(F32), ALU.subtract).then_inc(h_lo_done[q % 2], 1)

            scale_rows(0, 0)
            scale_rows(0, 1)
            with dve.Fori(0, TILES // 4 - 1) as i:
                for q in range(4):
                    take_lo(i, q)
                    scale_rows(i + (q + 2) // 4, (q + 2) % 4)
            last_i = TILES // 4 - 1
            for q in range(4):
                take_lo(last_i, q)
                if q < 2:
                    scale_rows(last_i, q + 2)
            dve.wait_ge(x_scaled, past(TILES))
            for p in range(2):
                dve.memset(raw[p][:, 0:GDN_CONV - 1], 0.0).then_inc(raw_zero, 1)
            dve.wait_ge(lam_step, 3)
            tt(neg_lam[:, :], lam_s[:, 3:4], lam_s[:, 2:3], ALU.subtract).then_inc(lam_step, 1)
            dve.wait_ge(lam_step, 4)
            dve.tensor_scalar(neg_lam[:, :], neg_lam[:, :], -LAM_INIT, None, ALU.add).then_inc(lam_step, 1)

            dve.wait_ge(raw_zero, 2)
            dve.wait_ge(vec_ready, 2)
            with dve.Fori(0, U_ZA // 2) as i:
                for p in range(2):
                    u = 2 * i + p
                    dve.wait_ge(bank_free[RB - 1], past(u + 1))
                    dve.wait_ge(stored[p], past(16 * i))
                    dve.tensor_scalar(stage[p][:, :], raw[p][:, 0:SEQ], vec[:, ds(u, 1)], None, ALU.mult
                                      ).then_inc(conv_step, 1)
                    for tap in range(1, GDN_CONV):
                        dve.wait_ge(conv_step, past((GDN_CONV - 1) * u + tap))
                        last = stt(stage[p][:, :], raw[p][:, tap:tap + SEQ], vec[:, ds(u + 12 * tap, 1)],
                                   stage[p][:, :], ALU.mult, ALU.add)
                        if tap < GDN_CONV - 1:
                            last.then_inc(conv_step, 1)
                    last.then_inc(conv_done[p], 1)

            with dve.Fori(0, H) as j:
                k = 2 * j + U_SAVED // 2
                u = 4 * j + U_SAVED
                for rb in range(RB):
                    dve.wait_ge(block_done[1], past(RB * k + rb + 1))
                    dve.wait_ge(bank_free[rb], past(u + 1))
                    part = raw[0][:, GDN_CONV - 1 + rb * R:GDN_CONV - 1 + (rb + 1) * R]
                    tt(part, part, bank[rb][:, :], ALU.mult).then_inc(bank_free[rb], 1)
                dve.wait_ge(bank_free[RB - 1], past(u + 2))
                for tap in range(SC_CONV):
                    src = raw[0][:, GDN_CONV - SC_CONV + tap:GDN_CONV - SC_CONV + tap + SEQ]
                    w = vec[:, ds(j + (VEC_SC + H * tap), 1)]
                    if tap == 0:
                        dve.tensor_scalar(conv[:, :], src, w, None, ALU.mult).then_inc(sc_step, 1)
                        continue
                    dve.wait_ge(sc_step, past((SC_CONV - 1) * j + tap))
                    last = stt(conv[:, :], src, w, conv[:, :], ALU.mult, ALU.add)
                    last.then_inc(sc_step if tap < SC_CONV - 1 else sc_conv_done, 1)
                dve.wait_ge(sc_conv_done, past(j + 1))
                for rb in range(RB):
                    dve.wait_ge(block_done[0], past(RB * k + (RB + rb + 1)))
                    part = conv[:, rb * R:(rb + 1) * R]
                    tt(part, part, bank[rb][:, :], ALU.mult).then_inc(bank_free[rb], 1)
                dve.wait_ge(bank_free[RB - 1], past(u + 4))
                dve.wait_ge(stored[0], past(16 * (j + U_SAVED // 2)))
                tt(stage[0][:, :], conv[:, :], stage[1][:, :], ALU.mult).then_inc(yc_done, 1)

            def by_chunk(t):
                return t[:, :].rearrange("p (c h) -> p c h", h=H)

            ab = bank[4][:, 0:TILES * 2 * H].rearrange("p (c e) -> p c e", e=2 * H)
            dve.wait_ge(ab_turned, 1)
            tt(by_chunk(tab["t0"]), ab[:, :, H:2 * H], head_in[:, 1:2, :].to_broadcast([P, TILES, H]), ALU.add
               ).then_inc(tab_v, 1)
            dve.wait_ge(tab_a, 5)
            stt(tab["t0"][:, :], tab["t0"][:, :], 0.0, tab["t1"][:, :], ALU.max, ALU.add).then_inc(tab_v, 1)
            dve.wait_ge(tab_v, 2)
            stt(by_chunk(tab["g"]), by_chunk(tab["t0"]), -1.0, head_in[:, 0:1, :].to_broadcast([P, TILES, H]),
                ALU.mult, ALU.mult).then_inc(tab_v, 1)
            dve.wait_ge(tab_mm, 1)
            dve.tensor_copy(tab["cum"][:, :], bank[5][:, 0:TILES * H]).then_inc(tab_v, 1)
            dve.wait_ge(tab_v, 4)
            tt(tab["t0"][:, :], bank[5][:, TILES * H:2 * TILES * H], tab["cum"][:, :], ALU.subtract
               ).then_inc(tab_v, 1)
            dve.wait_ge(tab_a, 8)
            tt(tab["beta_ecum"][:, :], tab["beta"][:, :], tab["t1"][:, :], ALU.mult).then_inc(tab_v, 1)
            arrive(dve, 0)

            def bc(t, c):
                return t[:, ds(H * c, H)].rearrange("p (h o) -> p h o", o=1).to_broadcast([P, H, P])

            def per_head(m):
                return m.rearrange("p (o c) -> p o c", o=1).to_broadcast([P, H, P])

            def new_v(c, p):
                dve.wait_ge(G["ws"], past(c + 1))
                dve.wait_ge(G["o_mm"], past(c))
                tt(v_new[:, :, :], U[p][:, :, :], hp(bank[6]), ALU.subtract).then_inc(G["vnew"], 1)

            def new_state(c, p):
                dve.wait_ge(G["s_mm"], past(c + 1))
                dve.wait_ge(G["sdec"], past(c + 1))
                tt(state[1 - p][:, :, :], state_d[:, :, :], hp(bank[7]), ALU.add).then_inc(G["state"], 1)

            def norm_out(c, q):
                dve.wait_ge(N["rso"], past(c + 1))
                dve.wait_ge(N["y_stored"], past(16 * c))
                tt(y_a[:, :, :], hp(bank[6]), rs_o[:, :, :], ALU.mult).then_inc(N["on"], 1)
                dve.wait_ge(N["on"], past(c + 1))
                stt(y_a[:, :, :], y_a[:, :, :], vec[:, VEC_GDN:VEC_GDN + 1], za_in[q][:, :, :],
                    ALU.mult, ALU.mult).then_inc(g_y[q % 2], 1)

            def chunk_pair(k, kp, first=False, last=False):
                c0 = 2 * k
                old, old_q = c0 - 2, 2 * (1 - kp)
                if not first:
                    new_v(old, 0)
                for p in range(2):
                    dve.wait_ge(G["rs"], past(c0 + p + 1))
                    dve.wait_ge(qkv_loaded[p], past(16 * k + 16))
                    dve.wait_ge(G["kk"], past(4 * k))
                    dve.wait_ge(G["qdec"], past(c0))
                    tt(qkn[p][:, H:2 * H, :], qkv_in[p][:, H:2 * H, :], rs_qk[p][:, H:2 * H, :], ALU.mult
                       ).then_inc(G["qkn"], 1)
                    stt(qkn[p][:, 0:H, :], qkv_in[p][:, 0:H, :], P ** -0.5, rs_qk[p][:, 0:H, :], ALU.mult,
                        ALU.mult).then_inc(G["qkn"], 1)
                for p in range(2):
                    dve.wait_ge(G["mask"], past(2 * c0 + 2 * p + 2))
                    dve.wait_ge(G["ecum"], past(c0 + p + 1))
                    cum = hp(bank[3 * p + 2])
                    tt(dec[p][:, 0, :, :], dec[p][:, 0, :, :], cum, ALU.subtract).then_inc(G["diff"], 1)
                    tt(dec[p][:, 1, :, :], dec[p][:, 1, :, :], cum, ALU.add).then_inc(G["diff"], 1)
                for p in range(2):
                    dve.wait_ge(G["turn"], past(4 * k + p + 1))
                    dve.wait_ge(G["u_mm"], past(4 * k))
                    tt(v_beta[p][:, :, :], hp(bank[3 * p]), bc(tab["beta"], c0 + p), ALU.mult
                       ).then_inc(G["rows"], 1)
                if not first:
                    new_state(old, 0)
                for p in range(2):
                    dve.wait_ge(G["kk"], past(4 * k + p + 1))
                    dve.wait_ge(G["decay_b"], past(c0 + p + 1))
                    dve.wait_ge(G["lowt"], past(c0))
                    tt(low[p][:, :, :], hp(bank[3 * p + 2]), dec[p][:, 0, :, :], ALU.mult
                       ).then_inc(G["masked"], 1)
                for p in range(2):
                    dve.wait_ge(G["kk"], past(4 * k + p + 3))
                    tt(qk_m[2 * kp + p][:, :, :], hp(bank[3 * p]), dec[p][:, 1, :, :], ALU.mult
                       ).then_inc(G["masked"], 1)
                for p in range(2):
                    dve.wait_ge(G["masked"], past(4 * k + p + 1))
                    tt(T[p][:, :, :], low[p][:, :, :], per_head(pair1[:, :]), ALU.mult).then_inc(G["t0"], 1)
                    dve.wait_ge(G["t0"], past(2 * c0 + 2 * p + 1))
                    tt(T[p][:, :, :], per_head(ident[:, :]), T[p][:, :, :], ALU.subtract).then_inc(G["t0"], 1)
                for p in range(2):
                    dve.wait_ge(G["turn"], past(4 * k + p + 3))
                    tt(k_beta[p][:, :, :], hp(bank[3 * p + 1]), bc(tab["beta_ecum"], c0 + p), ALU.mult
                       ).then_inc(G["rows"], 1)
                    tt(k_dec[2 * kp + p][:, :, :], hp(bank[3 * p + 1]), bc(tab["k_decay"], c0 + p), ALU.mult
                       ).then_inc(G["rows"], 1)
                for lv in range(1, LEVELS):
                    for p in range(2):
                        if lv < LEVELS - 1:
                            dve.wait_ge(G["y_mm"], past(level_y(k, lv, p, 0)))
                            tt(T[p][:, :, :], T[p][:, :, :], hp(bank[3 * p + 2]), ALU.subtract)
                        dve.wait_ge(G["y_mm"], past(level_y(k, lv, p, 1)))
                        tt(Tt[p][:, :, :], Tt[p][:, :, :], hp(bank[3 * p + 1]), ALU.subtract
                           ).then_inc(G["t_new"], 1)
                        if p == 0 and not first:
                            if lv == 1:
                                dve.wait_ge(za_loaded[1 - kp], past(16 * (k + kp)))
                                norm_out(old, old_q)
                            if lv == 6:
                                norm_out(old + 1, old_q + 1)
                    if not first and lv == 2:
                        new_v(old + 1, 1)
                    if not first and lv == 3:
                        new_state(old + 1, 1)

            def last_chunks():
                dve.wait_ge(za_loaded[1], past(8 * TILES))
                for p in range(2):
                    c = TILES - 2 + p
                    new_v(c, p)
                    new_state(c, p)
                    norm_out(c, 2 + p)

            pairs(dve, chunk_pair, last_chunks)
            arrive(dve, 1)

            with dve.Fori(0, H // MAPS) as i:
                for p in range(2):
                    h = 2 * i + p
                    scored = [0]

                    def biased(b):
                        bp = b % AHEAD
                        groups = b // RB + 1
                        dve.wait_ge(a_pv[bp], past(RB * h + b // AHEAD))
                        for m in range(MAPS):
                            for g in range(groups):
                                n = scored[0]
                                scored[0] += 1
                                w = min(R, (b + 1) * P - g * R)
                                at = SEQ - P - b * P + g * R
                                dve.wait_ge(A["score"], past(SCORES * h + n + 1))
                                wait_apart(dve, dve_waited)
                                dve.tensor_tensor_reduce(
                                    s_buf[bp][:, m, g * R:g * R + w], bank[n % 4][:, 0:w], bias[p][:, at:at + w],
                                    1.0, -3e38, ALU.add, ALU.max, top[bp][:, m, g:g + 1]
                                ).then_inc(score_free[n % 4], 1)
                        n = scored[0] - 1
                        dve.wait_ge(score_free[n % 4], past(SCORES // 4 * h + n // 4 + 1))
                        dve.tensor_reduce(top_all[bp][:, :], top[bp][:, :, 0:groups], AX.X, ALU.max
                                          ).then_inc(A["top"], 1)
                        dve.wait_ge(A["top"], past(TILES * h + b + 1))
                        dve.tensor_scalar(neg_top[bp][:, :], top_all[bp][:, :], -1.0, None, ALU.mult
                                          ).then_inc(A["negtop"], 1)

                    def combine(b):
                        bp = b % AHEAD
                        n = TILES * h + b
                        dve.wait_ge(A["exp"], past(2 * n + 2))
                        dve.reciprocal(inv[bp][:, :], den[bp][:, :]).then_inc(A["inv"], 1)
                        dve.wait_ge(A["inv"], past(n + 1))
                        tt(sub_w[bp][:, :], inv[bp][:, 1:2], neg_lam[:, :], ALU.mult).then_inc(A["subw"], 1)
                        w = (b + 1) * P
                        s0, s1 = s_buf[bp][:, 0, 0:w], s_buf[bp][:, 1, 0:w]
                        dve.wait_ge(A["subw"], past(n + 1))
                        dve.tensor_scalar(s1, s1, sub_w[bp][:, 0:1], None, ALU.mult).then_inc(A["sub"], 1)
                        dve.wait_ge(A["sub"], past(n + 1))
                        stt(s0, s0, inv[bp][:, 0:1], s1, ALU.mult, ALU.add).then_inc(A["probs"], 1)

                    def finish(sb):
                        n = RB * h + sb
                        dve.wait_ge(N["rso"], past(TILES + n + 1))
                        dve.wait_ge(N["y_stored"], past(16 * TILES + 16 * n))
                        tt(y_b[:, :], bank[6][:, :], rs_b[:, :], ALU.mult).then_inc(N["on"], 1)
                        dve.wait_ge(N["on"], past(TILES + n + 1))
                        stt(y_b[:, :], y_b[:, :], diff_w[:, 0:1], zb_in[p][:, sb * R:(sb + 1) * R],
                            ALU.mult, ALU.mult).then_inc(a_y[p], 1)

                    dve.wait_ge(head_loaded[p], past(64 * i + 64))
                    dve.wait_ge(A["dist"], past(2 * h + 4))
                    biased(0)
                    biased(1)
                    for b in range(TILES):
                        combine(b)
                        if b + 2 < TILES:
                            biased(b + 2)
                        if b and b % RB == 0:
                            finish(b // RB - 1)
                    finish(RB - 1)
            arrive(dve, 2)

            dve.wait_ge(M["post"], past(16))

            def y_split(r, b):
                dve.wait_ge(M["y_hi"], past(3 * r + b + 1))
                tt(y_lo[:, H * b:H * (b + 1), :], y_in[:, :, :],
                   y_hi[:, H * b:H * (b + 1), :].bitcast(F32), ALU.subtract).then_inc(M["y_lo"], 1)

            def merge(r, first=False, last=False):
                for d in range(KT):
                    for b in range(3):
                        n = 3 * d + b
                        dve.wait_ge(mm_done[b], past(KT * r + d + 1))
                        dve.wait_ge(gate_loaded[b], past(128 * r + 16 * d + 16))
                        dve.wait_ge(M["lo"], past(KT * r + d))
                        tt(gated[b][:, :], bank[n % 6][:, :], gate_in[b][:, :], ALU.mult
                           ).then_inc(gated_done[n % 6], 1)
                        if b == 1:
                            dve.wait_ge(gated_done[n % 6], past(KT // 2 * r + d // 2 + 1))
                            tt(gated[1][:, :], gated[0][:, :], gated[1][:, :], ALU.add).then_inc(M["sum1"], 1)
                    if first:
                        dve.wait_ge(M["wo_hi"], past(d + 1))
                        tt(wo_lo[:, d, :], x_res[d % 2][:, :], wo_hi[:, d, :].bitcast(F32), ALU.subtract
                           ).then_inc(M["wo_lo"], 1)
                    dve.wait_ge(M["hi"], past(KT * r + d + 1))
                    tt(m_lo[:, d, :], gated[0][:, :], m_hi[:, d, :].bitcast(F32), ALU.subtract).then_inc(M["lo"], 1)
                for t in range(RB):
                    n = RB * r + t
                    if not last and t:
                        y_split(r + 1, t - 1)
                    dve.wait_ge(M["sq"], past(2 * n + 2))
                    tt(o_stat[:, 2:3], o_stat[:, 0:1], o_stat[:, 1:2], ALU.add).then_inc(M["ss"], 1)
                    dve.wait_ge(M["root"], past(n + 1))
                    dve.reciprocal(o_stat[:, 4:5], o_stat[:, 3:4]).then_inc(M["inv"], 1)
                    dve.wait_ge(M["inv"], past(n + 1))
                    for nb in range(2):
                        cols = slice(nb * R, (nb + 1) * R)
                        last_op = stt(o_norm[:, cols], bank[(6, 0)[t % 2] + nb][:, :], o_stat[:, 4:5],
                                      post_w[:, cols], ALU.mult, ALU.mult)
                    last_op.then_inc(M["normed"], 1)
                    dve.wait_ge(M["normed"], past(n + 1))
                    dve.wait_ge(x_res_loaded[t % 2], past(32 * r + 16 * (t // 2) + 16))
                    tt(x_res[t % 2][:, :], x_res[t % 2][:, :], o_norm[:, :], ALU.add).then_inc(M["done"], 1)

            for b in range(3):
                y_split(0, b)
            merge(0, first=True)
            with dve.Fori(1, RB - 1) as r:
                merge(r)
            merge(RB - 1, last=True)


_INS = ["x", "norm_pre", "norm_post", "w_in", "gdn_conv_w", "gdn_a_log", "gdn_dt_bias", "gdn_norm_w",
        "diff_lambda", "diff_norm_w", "sc_conv_w", "w_branch", "w_out"]


def kernel(**inputs):
    import numpy as np
    import concourse.bacc as bacc
    from concourse.bass_utils import run_bass_kernel_spmd

    nc = bacc.Bacc("TRN2", target_bir_lowering=False, num_devices=1)
    arrays, args = {}, []
    for name in _INS:
        a = np.ascontiguousarray(inputs[name])
        arrays[f"in_{name}"] = a
        args.append(nc.dram_tensor(f"in_{name}", a.shape, mybir.dt.from_np(a.dtype), kind="ExternalInput").ap())
    out = nc.dram_tensor("out_x", (1, SEQ, D), F32, kind="ExternalOutput").ap()
    hybrid_block(nc, *args, out)
    r = run_bass_kernel_spmd(nc, [arrays], core_ids=[0])
    return r.results[0]["out_x"]
```

```python
from contextlib import ExitStack
import math

import concourse.bass as bass
from concourse import mybir

F32 = mybir.dt.float32
F32R = mybir.dt.float32r
ALU = mybir.AluOpType
ACT = mybir.ActivationFunctionType
AX = mybir.AxisListType
ds = bass.ds

P = 128
SEQ = 2048
D = 1024
KT = D // P
BW = D // 2
H = BW // P
N_IN = 9224
RB = 4
R = SEQ // RB
TILES = SEQ // P
GDN_CONV = 4
SC_CONV = 3
EPS = 1e-6
NEG = -1e30
LAM_INIT = 0.8 - 0.6 * math.exp(-0.3 * 0)
MAPS = 2
QK_DIM = P // MAPS
SCORE_BANKS = 4
AHEAD = 4
LEVELS = 7
SLOPE = 2.0 ** (-8.0 / H)
UNITS = 72
CONSTS = 34

ORDER = list(range(TILES))
GROUPS = list(range(RB))
GROUP_END = [RB * n + RB - 1 for n in range(RB)]


def scores_before(j):
    return MAPS * sum(b // RB + 1 for b in ORDER[:j])


TURNS = 2 * RB + sum(b // RB + 1 for b in ORDER)
EXP_LN_SET = 6
SCORES = scores_before(TILES)

COL_B = 4 * BW
COL_ATT = COL_B + 2 * H
COL_SC = COL_ATT + 4 * BW
COL_MERGE = COL_SC + 4 * BW
U_GDN, U_ZA, U_Q, U_K, U_V, U_ZB = 0, 12, 16, 20, 24, 28
U_SAVED = 32
VEC_CONV, VEC_SC = 0, GDN_CONV * 12
VEC_GDN = VEC_SC + SC_CONV * H
VEC_DIFF = VEC_GDN + 1
VECS = VEC_DIFF + 1


def hybrid_block(nc, x, norm_pre, norm_post, w_in, gdn_conv_w, gdn_a_log, gdn_dt_bias, gdn_norm_w,
                 diff_lambda, diff_norm_w, sc_conv_w, w_branch, w_out, out):
    with ExitStack() as ctx:
        def sem(name):
            return ctx.enter_context(nc.semaphore(name))

        counted = []

        def counter(name):
            counted.append(sem(name))
            return counted[-1]

        def counters(name, n):
            return [counter(f"{name}{i}") for i in range(n)]

        def past(n):
            return n + 1

        EARLY = 4 * (MAPS * SEQ + MAPS * 2 * R + SEQ)
        BASE = (nc.sbuf_base + 63) // 64 * 64
        LIMIT = nc.sbuf_usable_end

        class Room:

            def __init__(self, at):
                self.at = at

            def __call__(self, name, shape, dt=F32):
                n = 4
                for s in shape[1:]:
                    n *= s
                t = nc.alloc_sbuf_tensor_at(name, shape, dt, offset=self.at)
                self.at += (n + 63) // 64 * 64
                assert self.at <= LIMIT, (name, self.at, LIMIT)
                return t

        keep = Room(BASE)
        ident = keep("ident", [P, P])
        ones = keep("ones", [P, P])
        triu = keep("triu", [P, P])
        mask_lo = keep("mask_lo", [P, P])
        mask_up = keep("mask_up", [P, P])
        pair_t = keep("pair_t", [P, LEVELS, P])
        pair1 = keep("pair1", [P, P])
        eps = keep("eps", [P, 1])
        vec_rows = keep("vec_rows", [VECS, P])
        vec = keep("vec", [P, VECS])
        diff_w = keep("diff_w", [P, 1])
        lam_in = keep("lam_in", [P, 4, QK_DIM])
        lam_s = keep("lam_s", [P, 4])
        neg_lam = keep("neg_lam", [P, 1])
        head_in = keep("head_in", [P, 2, H])
        tab = {n: keep("tab_" + n, [P, TILES * H]) for n in
               ("g", "cum", "beta", "beta_ecum", "k_decay", "e_last", "t0", "t1")}
        ROOM = keep.at

        room = Room(ROOM)
        hT_hi = room("hT_hi", [P, KT, SEQ], F32R)
        hT_lo = room("hT_lo", [P, KT, SEQ], F32R)
        w_hi = [room(f"w_hi{p}", [P, KT, P], F32R) for p in range(2)]
        w_lo = [room(f"w_lo{p}", [P, KT, P], F32R) for p in range(2)]
        w_raw = [room(f"w_raw{p}", [P, KT, P]) for p in range(2)]
        AFTER_W = room.at
        stage = [room(f"stage{p}", [P, SEQ]) for p in range(2)]
        raw = [room(f"raw{p}", [P, GDN_CONV - 1 + SEQ]) for p in range(2)]
        conv = room("conv", [P, SEQ])
        abT = raw[0]
        room = Room(AFTER_W)
        x_in = [room(f"x_in{q}", [P, D]) for q in range(4)]
        x_junk = room("x_junk", [P, D])
        pre_w = room("pre_w", [P, D])
        x_stat = room("x_stat", [P, 4, 3])

        room = Room(ROOM)

        def tiles(name, copies, *extra):
            return [room(f"{name}{p}", [P, *extra, H, P]) for p in range(copies)]

        qkv_in = [room(f"qkv_in{p}", [P, 3 * H, P]) for p in range(2)]
        sq_qk = [room(f"sq_qk{p}", [P, 2 * H, P]) for p in range(2)]
        rs_qk = [room(f"rs_qk{p}", [P, 2 * H, P]) for p in range(2)]
        qkn = [room(f"qkn{p}", [P, 2 * H, P]) for p in range(2)]
        g_tri = tiles("g_tri", 2)
        dec = tiles("dec", 2, 2)
        e_cum = tiles("e_cum", 2)
        low = tiles("low", 2)
        lowT = tiles("lowT", 2)
        pairM = tiles("pairM", 2, LEVELS)
        T = tiles("T", 2)
        Tt = tiles("Tt", 2)
        X = tiles("X", 2)
        k_beta = tiles("k_beta", 2)
        v_beta = tiles("v_beta", 2)
        U = tiles("U", 2)
        WT = tiles("WT", 2)
        q_dec = tiles("q_dec", 4)
        qk_m = tiles("qk_m", 4)
        k_dec = tiles("k_dec", 4)
        za_in = tiles("za_in", 4)
        state = tiles("state", 2)
        v_new = room("v_new", [P, H, P])
        state_d = room("state_d", [P, H, P])
        sq_o = room("sq_o", [P, H, P])
        rs_o = room("rs_o", [P, H, P])
        y_a = room("y_a", [P, H, P])
        after_delta = room.at

        early = Room(LIMIT // 64 * 64 - EARLY)
        room = Room(ROOM)
        k_in = [(early, room)[p](f"k_in{p}", [P, MAPS, SEQ]) for p in range(2)]
        q_in = [(early, room)[n](f"q_in{n}", [P, MAPS, 2, R]) for n in range(2)]
        v_in = [room(f"v_in{p}", [P, SEQ]) for p in range(2)]
        zb_in = [room(f"zb_in{p}", [P, SEQ]) for p in range(2)]
        v_rows = room("v_rows", [P, TILES, P])
        REACH = SEQ
        dist = early("dist", [P, REACH])
        bias = [room(f"bias{p}", [P, REACH]) for p in range(2)]
        s_buf = [room(f"s_buf{n}", [P, MAPS, SEQ]) for n in range(AHEAD)]
        probsT = [room(f"probsT{p}", [P, TILES, P]) for p in range(2)]
        small = [room(f"small{n}", [P, (RB + 5) * MAPS]) for n in range(AHEAD)]
        top = [t[:, 0:RB * MAPS].rearrange("p (m g) -> p m g", m=MAPS) for t in small]
        top_all, neg_top, den, inv, sub_w = [[t[:, (RB + n) * MAPS:(RB + n + 1) * MAPS] for t in small]
                                             for n in range(5)]
        sq_b = room("sq_b", [P, R])
        rs_b = sq_b
        y_b = room("y_b", [P, R])
        assert max(room.at, after_delta) <= LIMIT // 64 * 64 - EARLY

        room = Room(ROOM)
        wo_hi = room("wo_hi", [P, KT, D], F32R)
        wo_lo = room("wo_lo", [P, KT, D], F32R)
        y_hi = room("y_hi", [P, 3 * H, R], F32R)
        y_lo = room("y_lo", [P, 3 * H, R], F32R)
        m_hi = room("m_hi", [P, KT, R], F32R)
        m_lo = room("m_lo", [P, KT, R], F32R)
        y_in = room("y_in", [P, H, R])
        y_first = [y_in[:, :, :]] + [wo_lo[:, 4 + 2 * n:6 + 2 * n, :].bitcast(F32).rearrange(
            "p k (two r) -> p (k two) r", r=R) for n in range(2)]
        wb_in = [room(f"wb_in{p}", [P, H, P]) for p in range(2)]
        wb_hi = [room(f"wb_hi{p}", [P, H, P], F32R) for p in range(3)]
        wb_lo = [room(f"wb_lo{p}", [P, H, P], F32R) for p in range(3)]
        gate_in = [room(f"gate_in{p}", [P, R]) for p in range(3)]
        gated = [room(f"gated{p}", [P, R]) for p in range(3)]
        x_res = [room(f"x_res{p}", [P, D]) for p in range(2)]
        o_norm = room("o_norm", [P, D])
        post_w = room("post_w", [P, D])
        o_stat = room("o_stat", [P, 5])

        bank = [ctx.enter_context(nc.psum_tensor(f"bank{i}", [P, R], F32)) for i in range(8)]

        def hp(t):
            return t[:, :].rearrange("p (h c) -> p h c", h=H)

        saved = nc.dram_tensor("saved", (U_SAVED, P, SEQ), F32, kind="Internal").ap()
        gates = nc.dram_tensor("gates", (3 * KT, P, SEQ), F32, kind="Internal").ap()
        qk_parts = nc.dram_tensor("qk_parts", (2, 2 * H, P, SEQ), F32, kind="Internal").ap()
        y_all = nc.dram_tensor("y_all", (3 * H, P, SEQ), F32, kind="Internal").ap()

        x_rows = x.rearrange("b (t p) d -> (b t) p d", p=P)
        out_rows = out.rearrange("b (t p) d -> (b t) p d", p=P)
        w_cols = w_in.rearrange("l (k p) n -> p (l k) n", p=P)
        wb_rows = w_branch.rearrange("l b (k p) n -> p (l b k) n", p=P)
        wo_rows = w_out.rearrange("l (k p) n -> p (l k) n", p=P)

        vec_loaded = sem("vec_loaded")
        const_step = sem("const_step")
        vec_ready = sem("vec_ready")
        lam_step = sem("lam_step")
        x_loaded = counters("x_loaded", 4)
        x_used = counters("x_used", 4)
        x_square = counter("x_square")
        x_root = counter("x_root")
        x_inv = counter("x_inv")
        x_scaled = counter("x_scaled")
        h_hi_done = counter("h_hi_done")
        h_lo_done = counters("h_lo_done", 2)
        w_loaded = counters("w_loaded", 2)
        w_hi_done = counter("w_hi_done")
        w_ready = counter("w_ready")
        block_done = counters("block_done", 2)
        bank_free = counters("bank_free", RB)
        raw_zero = sem("raw_zero")
        conv_step = counter("conv_step")
        conv_done = counters("conv_done", 2)
        staged = counter("staged")
        stored = counters("stored", 2)
        sc_step = counter("sc_step")
        sc_conv_done = counter("sc_conv_done")
        yc_done = counter("yc_done")
        ab_turned = sem("ab_turned")
        tab_v = sem("tab_v")
        tab_a = sem("tab_a")
        tab_mm = sem("tab_mm")
        through = sem("through")
        ENGINES = 5

        def arrive(e, phase):
            e.drain().then_inc(through, 1)
            e.wait_ge(through, ENGINES * (phase + 1))

        waited = sem("waited")

        def wait_apart(e):
            e.sem_inc(waited, 1)

        qkv_loaded = counters("qkv_loaded", 2)
        G = {n: counter("g_" + n) for n in (
            "sq", "ss", "rs_ln", "rs", "tri", "cumb", "qkn", "mask", "ecum", "diff", "decay", "decay_b",
            "qdec", "kk", "turn", "masked", "rows", "lowt", "lowt_sb", "t0", "pair",
            "T", "x_mm", "x_sb", "y_mm", "t_new", "u_mm", "uw_sb", "ws", "vnew", "o_mm", "s_mm", "sdec",
            "state", "zero")}
        N = {n: counter("n_" + n) for n in ("sqo", "sso", "rso_ln", "rso", "on", "y_stored")}
        g_y = counters("g_y", 2)
        za_loaded = counters("za_loaded", 2)

        def level(k, lv, p):
            return 2 * (LEVELS - 1) * k + (2 * (lv - 1) + p + 1)

        def level_y(k, lv, p, which):
            return (4 * LEVELS - 6) * k + (4 * (lv - 1) + (2 * p + which + 1 if lv < LEVELS - 1 else p + 1))

        def pairs(e, body, tail):
            body(0, 0, first=True)
            with e.Fori(0, TILES // 4 - 1) as i:
                body(2 * i + 1, 1)
                body(2 * i + 2, 0)
            body(TILES // 2 - 1, 1, last=True)
            tail()
        A = {n: counter("a_" + n) for n in (
            "dist", "score", "top", "negtop", "exp", "mix", "scaled",
            "probs", "turn")}
        a_pv = counters("a_pv", AHEAD)
        a_y = counters("a_y", 2)
        head_loaded = counters("head_loaded", 2)
        k_loaded = counters("k_loaded", 2)
        q_loaded = counters("q_loaded", 2)
        score_free = counter("score_free")
        turn_free = counters("turn_free", 2)
        M = {n: counter("m_" + n) for n in (
            "wo_loaded", "wo_hi", "wo_lo", "post", "y_hi", "y_lo", "wb_hi",
            "sum1", "sum2", "hi", "lo", "out_mm", "sq", "ss", "root", "inv", "normed", "done")}
        wb_free = counters("m_wb_free", 2)
        y_loaded = counters("m_y_loaded", 3)
        mm_done = counters("m_mm_done", 3)
        gated_done = counters("m_gated_done", 6)
        wb_loaded = counters("m_wb_loaded", 2)
        gate_loaded = counters("m_gate_loaded", 3)
        x_res_loaded = counters("m_x_loaded", 2)
        out_stored = counters("m_out_stored", 2)

        block = ctx.enter_context(nc.Block())

        @block.sync
        def _(sp):
            for s in counted:
                sp.sem_inc(s, 1)
            sp.dma_start(vec_rows[VEC_CONV:VEC_SC, :],
                         gdn_conv_w.rearrange("l k (t c) -> (l k t) c", c=P)).then_inc(vec_loaded, 16)
            sp.dma_start(vec_rows[VEC_SC:VEC_GDN, :],
                         sc_conv_w.rearrange("l k (t c) -> (l k t) c", c=P)).then_inc(vec_loaded, 16)
            sp.dma_start(vec_rows[VEC_GDN:VEC_DIFF, :], gdn_norm_w).then_inc(vec_loaded, 16)
            sp.dma_start(vec_rows[VEC_DIFF:VECS, :], diff_norm_w).then_inc(vec_loaded, 16)
            sp.dma_start(pre_w[:, :], norm_pre[0].partition_broadcast(P)).then_inc(vec_loaded, 16)
            sp.dma_start(lam_in[:, :, :], diff_lambda[0].partition_broadcast(P)).then_inc(vec_loaded, 16)
            sp.dma_start(head_in[:, 0, :], gdn_a_log[0].partition_broadcast(P)).then_inc(vec_loaded, 16)
            sp.dma_start(head_in[:, 1, :], gdn_dt_bias[0].partition_broadcast(P)).then_inc(vec_loaded, 16)
            with sp.Fori(0, TILES // 4) as i:
                for q in range(4):
                    sp.wait_ge(x_used[q], past(i))
                    sp.dma_start(x_in[q][:, :], x_rows[ds(4 * i + q, 1), :, :].rearrange("o p d -> p (o d)")
                                 ).then_inc(x_loaded[q], 16)

            def load_w(p, nth, col):
                sp.wait_ge(w_ready, past(nth))
                sp.dma_start(w_raw[p][:, :, :], w_cols[:, :, col]).then_inc(w_loaded[p], 16)

            load_w(0, 0, slice(0, P))
            load_w(1, 0, slice(P, 2 * P))
            with sp.Fori(1, U_Q // 2) as i:
                for p in range(2):
                    load_w(p, 2 * i + p - 1, ds(i * (2 * P) + p * P, P))
            with sp.Fori(U_Q // 2, U_SAVED // 2) as i:
                for p in range(2):
                    load_w(p, 2 * i + p - 1, ds(i * (2 * P) + (p * P + 2 * H), P))
            with sp.Fori(0, H) as j:
                for n, part in enumerate((1, 2, 0, 3)):
                    load_w(n % 2, 4 * j + (U_SAVED + n - 1), ds(j * P + (COL_SC + part * BW), P))
            with sp.Fori(0, 3 * KT // 2) as i:
                for p in range(2):
                    load_w(p, 2 * i + (U_SAVED + 4 * H + p - 1), ds(i * (2 * P) + (COL_MERGE + p * P), P))
            load_w(0, U_SAVED + 4 * H + 3 * KT - 1, slice(COL_B, COL_B + P))
            arrive(sp, 0)

            def chunk_loads(k, kp, first=False, last=False):
                for p in range(2):
                    rows = ds(k * (2 * P) + p * P, P)
                    sp.wait_ge(G["qkn"], past(4 * k))
                    sp.wait_ge(G["turn"], past(4 * k))
                    sp.dma_start(qkv_in[p][:, :, :], saved[U_GDN:U_ZA, :, rows].rearrange("u p r -> p u r")
                                 ).then_inc(qkv_loaded[p], 16)
                for p in range(2):
                    rows = ds(k * (2 * P) + p * P, P)
                    if not first:
                        sp.wait_ge(g_y[p], past(k - 1))
                    sp.dma_start(za_in[2 * kp + p][:, :, :], saved[U_ZA:U_Q, :, rows].rearrange("u p r -> p u r")
                                 ).then_inc(za_loaded[kp], 16)

            pairs(sp, chunk_loads, lambda: None)

            def load_k(i, p):
                for part in range(2):
                    sp.dma_start(k_in[p][part * QK_DIM:(part + 1) * QK_DIM, :, :],
                                 qk_parts[part, ds(2 * i + (H + p), 1), :, :].rearrange(
                                     "o (m c) r -> c (o m) r", m=MAPS)).then_inc(k_loaded[p], 16)

            def load_q(i, p, n):
                g = GROUPS[n]
                done = scores_before(GROUP_END[n - 2] + 1) if n > 1 else 0
                sp.wait_ge(A["score"], past(SCORES * (2 * i + p) + done))
                for part in range(2):
                    for half in range(2):
                        sp.dma_start(q_in[n % 2][half * QK_DIM:(half + 1) * QK_DIM, :, part, :],
                                     qk_parts[part, ds(2 * i + p, 1), :, g * R:(g + 1) * R].rearrange(
                                         "o (m c) r -> c (o m) r", m=MAPS)).then_inc(q_loaded[n % 2], 16)

            def load_rows(t, u, i, p):
                sp.dma_start(t[p][:, :], saved[ds(2 * i + (u + p), 1), :, :].rearrange("o p r -> p (o r)")
                             ).then_inc(head_loaded[p], 16)

            load_k(0, 0)
            load_q(0, 0, 0)
            arrive(sp, 1)
            load_rows(v_in, U_V, 0, 0)
            load_rows(zb_in, U_ZB, 0, 0)
            for n in range(1, RB):
                load_q(0, 0, n)
            for h in range(1, H):
                i, p = h // 2, h % 2
                sp.wait_ge(a_y[p], past(RB * i))
                load_k(i, p)
                load_q(i, p, 0)
                load_rows(v_in, U_V, i, p)
                load_rows(zb_in, U_ZB, i, p)
                for n in range(1, RB):
                    load_q(i, p, n)
            arrive(sp, 2)

            def load_y(r, b, dst=y_in[:, :, :]):
                if dst is not y_first[b]:
                    sp.wait_ge(M["y_lo"], past(3 * r + b))
                sp.dma_start(dst, y_all[H * b:H * (b + 1), :, ds(r * R, R)].rearrange("u p r -> p u r")
                             ).then_inc(y_loaded[b], 16)

            def merge_loads(r, first=False, last=False):
                rows = ds(r * R, R)
                for d in range(KT):
                    if first and d == 1:
                        sp.dma_start(post_w[:, :], norm_post[0].partition_broadcast(P)).then_inc(M["post"], 16)
                    for b in range(3):
                        n = 3 * d + b
                        if first and d == 0:
                            load_y(0, b, y_first[b])
                        sp.wait_ge(wb_free[n % 2], past(12 * r + n // 2))
                        sp.dma_start(wb_in[n % 2][:, :, :], wb_rows[:, H * b:H * (b + 1), d * P:(d + 1) * P]
                                     ).then_inc(wb_loaded[n % 2], 16)
                        sp.wait_ge(gated_done[3 * ((d + 1) % 2) + b], past(RB * r + (d + 1) // 2))
                        sp.dma_start(gate_in[b][:, :], gates[b * KT + d, :, rows]).then_inc(gate_loaded[b], 16)
                    if first:
                        sp.wait_ge(M["wo_lo"], past(max(0, d - 1)))
                        sp.dma_start(x_res[d % 2][:, :], wo_rows[:, d, :]).then_inc(M["wo_loaded"], 16)
                if first:
                    sp.wait_ge(M["wo_lo"], past(KT))
                if not last:
                    load_y(r + 1, 0)
                for t in range(RB):
                    sp.wait_ge(out_stored[t % 2], past(32 * r + 16 * (t // 2)))
                    sp.dma_start(x_res[t % 2][:, :], x_rows[ds(RB * r + t, 1), :, :].rearrange("o p d -> p (o d)")
                                 ).then_inc(x_res_loaded[t % 2], 16)
                    if not last and t in (1, 2):
                        load_y(r + 1, t)

            merge_loads(0, first=True)
            with sp.Fori(1, RB - 1) as r:
                merge_loads(r)
            merge_loads(RB - 1, last=True)
            for p in range(2):
                sp.wait_ge(out_stored[p], past(16 * TILES // 2))

        @block.gpsimd
        def _(pool):
            def sum_last(pool, r, d):
                pool.wait_ge(M["sum1"], past(KT * r + d + 1))
                pool.wait_ge(gated_done[3 * (d % 2) + 2], past(KT // 2 * r + d // 2 + 1))
                pool.tensor_tensor(gated[0][:, :], gated[1][:, :], gated[2][:, :], ALU.add
                                   ).then_inc(M["sum2"], 1)

            n_const = [0]

            def const(ins):
                n_const[0] += 1
                ins.then_inc(const_step, 1)
                pool.wait_ge(const_step, n_const[0])

            def select(t, op, fill, base, cm, pattern):
                const(pool.affine_select(out=t, in_=t, compare_op=op, fill=fill, base=base,
                                         channel_multiplier=cm, pattern=pattern))

            const(pool.memset(ident[:, :], 0.0))
            select(ident[:, :], ALU.not_equal, 1.0, 0, 1, [[-1, P]])
            const(pool.memset(ones[:, :], 1.0))
            const(pool.memset(eps[:, :], EPS))
            const(pool.memset(triu[:, :], 1.0))
            select(triu[:, :], ALU.is_ge, 0.0, 0, -1, [[1, P]])
            const(pool.memset(mask_lo[:, :], 0.0))
            select(mask_lo[:, :], ALU.is_ge, NEG, -1, 1, [[-1, P]])
            const(pool.memset(mask_up[:, :], 0.0))
            select(mask_up[:, :], ALU.is_ge, NEG, 0, -1, [[1, P]])
            const(pool.memset(pair_t[:, :, :], 0.0))
            for lv in range(LEVELS):
                s = 1 << lv
                odd = pair_t[:, lv, :].rearrange("p (a two s) -> p a two s", two=2, s=s)[:, :, 1, :]
                const(pool.memset(odd, 1.0))
                select(odd, ALU.is_ge, 0.0, 0, 1, [[-2 * s, P // (2 * s)], [0, s]])
                select(odd, ALU.is_ge, 0.0, s - 1, -1, [[2 * s, P // (2 * s)], [0, s]])
            const(pool.memset(pair1[:, :], 0.0))
            even = pair1[:, :].rearrange("p (a two) -> p a two", two=2)[:, :, 0]
            select(even, ALU.not_equal, 1.0, -1, 1, [[-2, P // 2]])

            assert n_const[0] == CONSTS

            def split_w(u, k, p):
                pool.wait_ge(w_loaded[p], past(16 * k + 16))
                pool.wait_ge(block_done[p], past(RB * k))
                wait_apart(pool)
                pool.tensor_copy(w_hi[p][:, :, :], w_raw[p][:, :, :]).then_inc(w_hi_done, 1)
                pool.wait_ge(w_hi_done, past(u + 1))
                pool.tensor_tensor(w_lo[p][:, :, :], w_raw[p][:, :, :], w_hi[p][:, :, :].bitcast(F32),
                                   ALU.subtract).then_inc(w_ready, 1)

            with pool.Fori(0, UNITS // 2) as i:
                for p in range(2):
                    split_w(2 * i + p, i, p)
            split_w(UNITS, UNITS // 2, 0)
            arrive(pool, 0)

            def bc(t, c):
                return t[:, ds(H * c, H)].rearrange("p (h o) -> p h o", o=1).to_broadcast([P, H, P])

            def per_head(m):
                return m.rearrange("p (o c) -> p o c", o=1).to_broadcast([P, H, P])

            def chunk_pair(k, kp, first=False, last=False):
                if not first:
                    decay(2 * k - 2, 0)
                for p in range(2):
                    c = 2 * k + p
                    pool.wait_ge(G["cumb"], past(2 * k))
                    pool.tensor_tensor(g_tri[p][:, :, :], per_head(triu[:, :]), bc(tab["g"], c), ALU.mult
                                       ).then_inc(G["tri"], 1)
                for p in range(2):
                    c = 2 * k + p
                    pool.wait_ge(G["masked"], past(4 * k))
                    pool.tensor_tensor(dec[p][:, 0, :, :], per_head(mask_lo[:, :]), bc(tab["cum"], c), ALU.add
                                       ).then_inc(G["mask"], 1)
                    pool.tensor_tensor(dec[p][:, 1, :, :], per_head(mask_up[:, :]), bc(tab["cum"], c),
                                       ALU.subtract).then_inc(G["mask"], 1)
                for p in range(2):
                    c = 2 * k + p
                    pool.wait_ge(G["decay"], past(c + 1))
                    pool.tensor_tensor(dec[p][:, 0, :, :], dec[p][:, 0, :, :], bc(tab["beta"], c), ALU.mult
                                       ).then_inc(G["decay_b"], 1)
                for p in range(2):
                    pool.wait_ge(G["lowt_sb"], past(2 * k + p + 1))
                    pool.wait_ge(G["u_mm"], past(4 * k))
                    for lv in range(2):
                        pool.tensor_tensor(pairM[p][:, lv, :, :], lowT[p][:, :, :], per_head(pair_t[:, lv, :]),
                                           ALU.mult).then_inc(G["pair"], 1)
                        if lv == 0:
                            pool.wait_ge(G["pair"], past(2 * LEVELS * k + 2 * p + 1))
                            pool.tensor_tensor(Tt[p][:, :, :], per_head(ident[:, :]), pairM[p][:, 0, :, :],
                                               ALU.subtract).then_inc(G["T"], 1)
                for lv in range(2, LEVELS):
                    for p in range(2):
                        pool.tensor_tensor(pairM[p][:, lv, :, :], lowT[p][:, :, :], per_head(pair_t[:, lv, :]),
                                           ALU.mult).then_inc(G["pair"], 1)
                    if lv == 2 and not first:
                        decay(2 * k - 1, 1)
                for p in range(2):
                    q = 2 * kp + p
                    pool.wait_ge(G["ecum"], past(2 * k + p + 1))
                    pool.wait_ge(G["qkn"], past(4 * k + 2 * p + 2))
                    if not first:
                        pool.wait_ge(G["o_mm"], past(2 * k - 2))
                    pool.tensor_tensor(q_dec[q][:, :, :], qkn[p][:, 0:H, :], e_cum[p][:, :, :], ALU.mult
                                       ).then_inc(G["qdec"], 1)

            def decay(c, p):
                pool.wait_ge(G["state"], past(c))
                pool.tensor_tensor(state_d[:, :, :], state[p][:, :, :], bc(tab["e_last"], c), ALU.mult
                                   ).then_inc(G["sdec"], 1)

            pool.memset(state[0][:, :, :], 0.0).then_inc(G["zero"], 1)
            pool.wait_ge(G["zero"], past(1))
            pairs(pool, chunk_pair, lambda: (decay(TILES - 2, 0), decay(TILES - 1, 1)))

            pool.iota(dist[:, :], [[1, SEQ]], base=P - SEQ, channel_multiplier=-1,
                      allow_small_or_imprecise_dtypes=True).then_inc(A["dist"], 1)
            pool.wait_ge(A["dist"], past(1))
            pool.affine_select(out=dist[:, :], in_=dist[:, :], compare_op=ALU.is_ge, fill=NEG, base=SEQ - P,
                               channel_multiplier=1, pattern=[[-1, SEQ]]).then_inc(A["dist"], 1)
            arrive(pool, 1)
            with pool.Fori(0, H // MAPS) as i:
                for p in range(2):
                    h = 2 * i + p
                    pool.wait_ge(A["dist"], past(2 * h + 2))
                    wait_apart(pool)
                    pool.tensor_scalar(dist[:, :], dist[:, :], SLOPE, 1.0, ALU.mult, ALU.mult
                                       ).then_inc(A["dist"], 1)
                    pool.wait_ge(A["dist"], past(2 * h + 3))
                    pool.wait_ge(a_y[p], past(RB * i))
                    wait_apart(pool)
                    pool.tensor_scalar(bias[p][:, :], dist[:, :], 1.0, 1.0, ALU.mult, ALU.mult
                                       ).then_inc(A["dist"], 1)
                    for j, b in enumerate(ORDER):
                        s1 = s_buf[j % AHEAD][:, 1, 0:(b + 1) * P]
                        pool.wait_ge(A["mix"], past(2 * TILES * h + 2 * j + 2))
                        wait_apart(pool)
                        pool.tensor_scalar(s1, s1, sub_w[j % AHEAD][:, 0:1], 1.0, ALU.mult, ALU.mult
                                           ).then_inc(A["scaled"], 1)
            arrive(pool, 2)

            with pool.Fori(0, RB) as r:
                for d in range(KT):
                    for b in range(3):
                        n = 3 * d + b
                        pool.wait_ge(M["wb_hi"], past(24 * r + n + 1))
                        pool.tensor_tensor(wb_lo[n % 3][:, :, :], wb_in[n % 2][:, :, :],
                                           wb_hi[n % 3][:, :, :].bitcast(F32), ALU.subtract
                                           ).then_inc(wb_free[n % 2], 1)
                        if b == 1 and d:
                            sum_last(pool, r, d - 1)
                sum_last(pool, r, KT - 1)

        @block.tensor
        def _(pe):
            def mm3(dst, lhs, rhs, first, last):
                pe.matmul(dst, lhs[0], rhs[0], start=first, stop=False)
                pe.matmul(dst, lhs[0], rhs[1], start=False, stop=False)
                return pe.matmul(dst, lhs[1], rhs[0], start=False, stop=last)

            pe.wait_ge(const_step, CONSTS)
            pe.wait_ge(vec_loaded, 128)
            pe.transpose(bank[0][:, 0:VECS], vec_rows[:, :], ident[0:VECS, 0:VECS]).then_inc(vec_ready, 1)
            with pe.Fori(0, TILES // 4) as i:
                for q in range(4):
                    p = q % 2
                    pe.wait_ge(x_scaled, past(4 * i + q + 1))
                    pe.wait_ge(h_lo_done[p], past(2 * (2 * i + q // 2)))
                    for k in range(KT):
                        last = pe.transpose(bank[4 + 2 * p + k // 4][:, (k % 4) * P:(k % 4 + 1) * P],
                                            x_in[q][:, k * P:(k + 1) * P], ident[:, :])
                    last.then_inc(x_used[q], 1)
            pe.wait_ge(h_lo_done[0], past(TILES))
            pe.wait_ge(h_lo_done[1], past(TILES))
            pe.wait_ge(vec_ready, 2)

            def project(u, p):
                pe.wait_ge(w_ready, past(u + 1))
                for rb in range(RB):
                    pe.wait_ge(bank_free[rb], past(u))
                    for k in range(KT):
                        cols = slice(rb * R, (rb + 1) * R)
                        last = mm3(bank[rb][:, :], (w_hi[p][:, k, :], w_lo[p][:, k, :]),
                                   (hT_hi[:, k, cols], hT_lo[:, k, cols]), k == 0, k == KT - 1)
                    last.then_inc(block_done[p], 1)

            with pe.Fori(0, UNITS // 2) as i:
                for p in range(2):
                    project(2 * i + p, p)
            project(UNITS, 0)

            pe.wait_ge(bank_free[RB - 1], past(UNITS + 1))
            for c in range(TILES):
                last = pe.transpose(bank[4][:, 2 * H * c:2 * H * (c + 1)], abT[0:2 * H, c * P:(c + 1) * P],
                                    ident[0:2 * H, 0:2 * H])
            last.then_inc(ab_turned, 1)
            pe.wait_ge(tab_v, 3)
            pe.matmul(bank[5][:, 0:TILES * H], triu[:, :], tab["g"][:, :], start=True, stop=True)
            pe.matmul(bank[5][:, TILES * H:2 * TILES * H], ones[:, :], tab["g"][:, :], start=True, stop=True
                      ).then_inc(tab_mm, 1)
            arrive(pe, 0)

            def heads(dst, lhs, rhs):
                for h in range(H):
                    last = pe.matmul(dst[:, h * P:(h + 1) * P], lhs[:, h, :], rhs[:, h, :],
                                     start=True, stop=True)
                return last

            def against_state(c, q):
                pe.wait_ge(G["uw_sb"], past(2 * c + 2))
                pe.wait_ge(G["state"], past(c))
                pe.wait_ge(G["zero"], past(1))
                pe.wait_ge(N["on"], past(c))
                heads(bank[6], WT[q % 2], state[q % 2]).then_inc(G["ws"], 1)

            def new_state(c, q):
                pe.wait_ge(G["vnew"], past(c + 1))
                pe.wait_ge(N["rso_ln"], past(c))
                heads(bank[7], k_dec[q], v_new).then_inc(G["s_mm"], 1)
                pe.wait_ge(G["qdec"], past(c + 1))
                for h in range(H):
                    cols = slice(h * P, (h + 1) * P)
                    pe.matmul(bank[6][:, cols], state[q % 2][:, h, :], q_dec[q][:, h, :], start=True, stop=False)
                    last = pe.matmul(bank[6][:, cols], v_new[:, h, :], qk_m[q][:, h, :],
                                     start=False, stop=True)
                last.then_inc(G["o_mm"], 1)

            def out_squares(c):
                pe.wait_ge(N["sqo"], past(c + 1))
                pe.wait_ge(G["state"], past(c + 1))
                pe.matmul(bank[7][:, :], ones[:, :], sq_o[:, :, :], start=True, stop=True
                          ).then_inc(N["sso"], 1)

            def chunk_pair(k, kp, first=False, last=False):
                c0 = 2 * k
                old, old_q = c0 - 2, 2 * (1 - kp)
                pe.wait_ge(G["uw_sb"], past(4 * k))
                for p in range(2):
                    pe.wait_ge(G["sq"], past(c0 + p + 1))
                    pe.matmul(bank[3 * p][:, :], ones[:, :], sq_qk[p][:, 0:H, :], start=True, stop=True)
                    pe.matmul(bank[3 * p + 1][:, :], ones[:, :], sq_qk[p][:, H:2 * H, :], start=True, stop=True
                              ).then_inc(G["ss"], 1)
                if not first:
                    against_state(old, old_q)
                for p in range(2):
                    pe.wait_ge(G["tri"], past(c0 + p + 1))
                    pe.matmul(bank[3 * p + 2][:, :], ones[:, :], g_tri[p][:, :, :], start=True, stop=True
                              ).then_inc(G["cumb"], 1)
                for p in range(2):
                    pe.wait_ge(G["rs_ln"], past(2 * c0 + 2 * p + 1))
                    for h in range(H):
                        end = pe.transpose(bank[3 * p][:, h * P:(h + 1) * P], qkv_in[p][:, 2 * H + h, :],
                                           ident[:, :])
                    end.then_inc(G["turn"], 1)
                if not first:
                    new_state(old, old_q)
                for p in range(2):
                    kn = qkn[p][:, H:2 * H, :]
                    pe.wait_ge(G["qkn"], past(2 * c0 + 2 * p + 1))
                    for h in range(H):
                        end = pe.transpose(bank[3 * p + 1][:, h * P:(h + 1) * P], kn[:, h, :], ident[:, :])
                    end.then_inc(G["turn"], 1)
                    pe.wait_ge(G["diff"], past(2 * c0 + 2 * p + 2))
                    heads(bank[3 * p + 2], kn, kn).then_inc(G["kk"], 1)
                for p in range(2):
                    pe.wait_ge(G["qkn"], past(2 * c0 + 2 * p + 2))
                    pe.wait_ge(G["rows"], past(6 * k + p + 1))
                    heads(bank[3 * p], qkn[p][:, H:2 * H, :], qkn[p][:, 0:H, :]).then_inc(G["kk"], 1)
                for p in range(2):
                    pe.wait_ge(G["masked"], past(4 * k + p + 1))
                    for h in range(H):
                        end = pe.transpose(bank[3 * p + 2][:, h * P:(h + 1) * P], low[p][:, h, :], ident[:, :])
                    end.then_inc(G["lowt"], 1)
                if not first:
                    out_squares(old)
                for lv in range(1, LEVELS):
                    for p in range(2):
                        pe.wait_ge(G["pair"], past(2 * LEVELS * k + (2 * p + 2 if lv == 1 else 2 * lv + p + 1)))
                        if lv == 1:
                            pe.wait_ge(G["t0"], past(2 * c0 + 2 * p + 2))
                            pe.wait_ge(G["masked"], past(4 * k + p + 3))
                        else:
                            pe.wait_ge(G["t_new"], past(level(k, lv - 1, p)))
                        heads(bank[3 * p], pairM[p][:, lv, :, :], T[p]).then_inc(G["x_mm"], 1)
                    if not first and lv == 2:
                        against_state(old + 1, old_q + 1)
                    if not first and lv == 3:
                        new_state(old + 1, old_q + 1)
                    if not first and lv == 5:
                        out_squares(old + 1)
                    for p in range(2):
                        if lv == 1:
                            pe.wait_ge(G["T"], past(c0 + p + 1))
                            pe.wait_ge(G["rows"], past(6 * k + 2 * p + 4))
                        pe.wait_ge(G["x_sb"], past(level(k, lv, p)))
                        if lv < LEVELS - 1:
                            heads(bank[3 * p + 2], Tt[p], X[p]).then_inc(G["y_mm"], 1)
                        heads(bank[3 * p + 1], X[p], Tt[p]).then_inc(G["y_mm"], 1)
                for p in range(2):
                    pe.wait_ge(G["t_new"], past(level(k, LEVELS - 1, p)))
                    heads(bank[3 * p], Tt[p], v_beta[p]).then_inc(G["u_mm"], 1)
                    heads(bank[3 * p + 2], k_beta[p], Tt[p]).then_inc(G["u_mm"], 1)

            def last_states():
                for p in range(2):
                    c = TILES - 2 + p
                    against_state(c, 2 + p)
                    new_state(c, 2 + p)
                    out_squares(c)

            pairs(pe, chunk_pair, last_states)
            arrive(pe, 1)

            with pe.Fori(0, H // MAPS) as i:
                for p in range(2):
                    h = 2 * i + p
                    turns = [0]
                    scored = [0]

                    def turn_bank():
                        n = turns[0]
                        turns[0] += 1
                        pe.wait_ge(turn_free[n % 2], past(TURNS // 2 * h + n // 2))
                        return bank[4 + n % 2]

                    def scores(j, first, last):
                        b = ORDER[j]
                        nth = GROUPS.index(b // RB)
                        pe.wait_ge(q_loaded[nth % 2], past(64 * (2 * h + nth // 2 + 1)))
                        groups = b // RB + 1
                        for t in range(first, min(last, MAPS * groups)):
                            m, g = t // groups, t % groups
                            n = scored[0]
                            scored[0] += 1
                            w = max(min(R, (b + 1) * P - g * R), R // 2)
                            pe.wait_ge(score_free, past(SCORES * h + max(0, n - SCORE_BANKS + 1)))
                            for part in range(2):
                                end = pe.matmul(bank[n % SCORE_BANKS][:, 0:w],
                                                q_in[nth % 2][:, m, part, b % RB * P:(b % RB + 1) * P
                                                                  ].bitcast(F32R),
                                                k_in[p][:, m, g * R:g * R + w].bitcast(F32R),
                                                start=(part == 0), stop=(part == 1))
                            end.then_inc(A["score"], 1)

                    def square_sum(nth):
                        pe.wait_ge(N["sqo"], past(TILES + RB * h + nth + 1))
                        pe.matmul(turn_bank()[:, :], ones[:, :], sq_b[:, :], start=True, stop=True
                                  ).then_inc(A["turn"], 1)

                    pe.wait_ge(k_loaded[p], past(32 * i + 32))
                    scores(0, 0, SCORES)
                    scores(1, 0, 2)
                    pe.wait_ge(head_loaded[p], past(32 * i + 32))
                    for g in range(RB):
                        dst = turn_bank()
                        for k in range(RB):
                            last = pe.transpose(dst[:, k * P:(k + 1) * P],
                                                v_in[p][:, (g * RB + k) * P:(g * RB + k + 1) * P], ident[:, :])
                        last.then_inc(A["turn"], 1)
                    scores(1, 2, SCORES)

                    def turn_probs(j):
                        b = ORDER[j]
                        pe.wait_ge(A["probs"], past(TILES * h + j + 1))
                        for g in range(b // RB + 1):
                            dst = turn_bank()
                            for k in range(min(RB, b + 1 - g * RB)):
                                kb = g * RB + k
                                last = pe.transpose(dst[:, k * P:(k + 1) * P],
                                                    s_buf[j % AHEAD][:, 0, kb * P:(kb + 1) * P], ident[:, :])
                            last.then_inc(A["turn"], 1)
                        turned.append(turns[0])

                    def weigh(j):
                        b = ORDER[j]
                        nth = GROUPS.index(b // RB)
                        for n in (turned[j] - 1, turned[j] - 2):
                            pe.wait_ge(turn_free[n % 2], past(TURNS // 2 * h + n // 2 + 1))
                        if b % RB == 0:
                            pe.wait_ge(N["on"], past(TILES - 1 + RB * h + nth))
                        for kb in range(b + 1):
                            last = pe.matmul(bank[6 + nth % 2][:, (b % RB) * P:(b % RB + 1) * P],
                                             v_rows[:, kb, :], probsT[j % 2][:, kb, :],
                                             start=(kb == 0), stop=(kb == b))
                        last.then_inc(a_pv[j % AHEAD], 1)

                    turned = []
                    for j in range(TILES):
                        if j + 2 < TILES:
                            scores(j + 2, 0, SCORE_BANKS)
                        turn_probs(j)
                        if j - 1 in GROUP_END:
                            square_sum(GROUP_END.index(j - 1))
                        if j + 2 < TILES:
                            scores(j + 2, SCORE_BANKS, SCORES)
                        weigh(j)
                    square_sum(RB - 1)
                    assert turns[0] == TURNS and scored[0] == SCORES
            arrive(pe, 2)

            with pe.Fori(0, RB) as r:
                for d in range(KT):
                    for b in range(3):
                        n = 3 * d + b
                        if d == 0:
                            pe.wait_ge(M["y_lo"], past(3 * r + b + 1))
                        half = KT // 2
                        pe.wait_ge(wb_free[n % 2], past(12 * r + n // 2 + 1))
                        pe.wait_ge(gated_done[n % 6], past(half * r + n // 6))
                        if n == 4:
                            pe.wait_ge(M["normed"], past(RB * r))
                        for k in range(H):
                            last = mm3(bank[(n + 2) % 6][:, :], (wb_hi[n % 3][:, k, :], wb_lo[n % 3][:, k, :]),
                                       (y_hi[:, H * b + k, :], y_lo[:, H * b + k, :]), k == 0, k == H - 1)
                        last.then_inc(mm_done[n % 3], 1)
                pe.wait_ge(M["wo_lo"], past(KT))
                for t in range(RB):
                    pe.wait_ge(M["normed"], past(RB * r + max(0, t - 1)))
                    for nb in range(2):
                        dst = bank[(6, 0)[t % 2] + nb]
                        for d in range(KT):
                            if t == 0 and nb == 0:
                                pe.wait_ge(M["lo"], past(KT * r + d + 1))
                            rows = slice(t * P, (t + 1) * P)
                            cols = slice(nb * R, (nb + 1) * R)
                            last = mm3(dst[:, :], (m_hi[:, d, rows], m_lo[:, d, rows]),
                                       (wo_hi[:, d, cols], wo_lo[:, d, cols]), d == 0, d == KT - 1)
                        last.then_inc(M["out_mm"], 1)

        @block.scalar
        def _(act):
            def f(out_, in_, func, **kw):
                return act.activation(out_, in_, func, **kw)

            def row_scale(i, q):
                t = 4 * i + q
                act.wait_ge(x_loaded[q], past(16 * i + 16))
                f(x_junk[:, :], x_in[q][:, :], ACT.Square, accum_out=x_stat[:, q, 0:1]).then_inc(x_square, 1)
                act.wait_ge(x_square, past(t + 1))
                f(x_stat[:, q, 1:2], x_stat[:, q, 0:1], ACT.Sqrt, scale=1.0 / D, bias=eps[:, 0:1]
                  ).then_inc(x_root, 1)

            def take_hi(i, q):
                t = 4 * i + q
                act.wait_ge(x_used[q], past(i + 1))
                for n in range(2):
                    f(hT_hi[:, 4 * n:4 * n + 4, ds(t * P, P)], hp(bank[4 + 2 * (q % 2) + n]), ACT.Copy
                      ).then_inc(h_hi_done, 1)

            act.wait_ge(const_step, CONSTS)
            row_scale(0, 0)
            row_scale(0, 1)
            with act.Fori(0, TILES // 4 - 1) as i:
                for q in range(4):
                    take_hi(i, q)
                    row_scale(i + (q + 2) // 4, (q + 2) % 4)
            last_i = TILES // 4 - 1
            for q in range(4):
                take_hi(last_i, q)
                if q < 2:
                    row_scale(last_i, q + 2)
            act.wait_ge(vec_loaded, 128)
            act.wait_ge(lam_step, 2)
            f(lam_s[:, 2:4], lam_s[:, 0:2], ACT.Exp).then_inc(lam_step, 1)

            def store(dst, p, sp_sem, value):
                act.wait_ge(sp_sem, past(value))
                act.dma_start(dst, stage[p][:, :]).then_inc(stored[p], 16)

            def one(t, u):
                return t[ds(u, 1), :, :].rearrange("o p r -> p (o r)")

            act.wait_ge(h_lo_done[1], past(TILES))
            act.wait_ge(raw_zero, 1)
            with act.Fori(0, U_ZA // 2) as i:
                for p in range(2):
                    u = 2 * i + p
                    act.wait_ge(conv_done[p], past(i))
                    for rb in range(RB):
                        act.wait_ge(block_done[p], past(RB * i + rb + 1))
                        f(raw[p][:, GDN_CONV - 1 + rb * R:GDN_CONV - 1 + (rb + 1) * R], bank[rb][:, :], ACT.Copy
                          ).then_inc(bank_free[rb], 1)
                    act.wait_ge(conv_done[p], past(i + 1))
                    f(stage[p][:, :], stage[p][:, :], ACT.Silu).then_inc(staged, 1)
                    store(one(saved, u), p, staged, u + 1)

            def direct(first, count, func, dst, dst_first, stored_before, **kw):
                with act.Fori(0, count // 2) as i:
                    for p in range(2):
                        k = i + first // 2
                        act.wait_ge(stored[p], past(16 * (i + stored_before[p])))
                        for rb in range(RB):
                            act.wait_ge(block_done[p], past(RB * k + rb + 1))
                            f(stage[p][:, rb * R:(rb + 1) * R], bank[rb][:, :], func, **kw
                              ).then_inc(bank_free[rb], 1)
                        store(one(dst, 2 * i + (dst_first + p)), p, bank_free[RB - 1], 2 * i + (first + p + 1))

            direct(U_ZA, H, ACT.Silu, saved, U_ZA, (U_ZA // 2, U_ZA // 2))
            for unit, scale in ((U_Q, QK_DIM ** -0.5), (U_K, 1.0)):
                with act.Fori(0, H // 2) as i:
                    for p in range(2):
                        before = (unit - U_Q) // 2
                        u = 2 * i + (unit + p)
                        act.wait_ge(stored[p], past(32 * i + (16 * (U_Q // 2) + 32 * before)))
                        for rb in range(RB):
                            act.wait_ge(block_done[p], past(RB * i + (RB * unit // 2 + rb + 1)))
                            f(stage[p][:, rb * R:(rb + 1) * R].bitcast(F32R), bank[rb][:, :], ACT.Copy, scale=scale
                              ).then_inc(staged, 1)
                        act.wait_ge(bank_free[RB - 1], past(u + 1))
                        parts = (stage[p][:, :], raw[p][:, GDN_CONV - 1:GDN_CONV - 1 + SEQ])
                        for part in range(2):
                            act.dma_start(qk_parts[part, ds(2 * i + (unit - U_Q + p), 1), :, :].rearrange(
                                "o p r -> p (o r)"), parts[part]).then_inc(stored[p], 16)
            for first, func in ((U_V, ACT.Copy), (U_ZB, ACT.Silu)):
                direct(first, H, func, saved, first, (first // 2 + H, first // 2 + H))
            with act.Fori(0, H) as j:
                k = 2 * j + U_SAVED // 2
                act.wait_ge(sc_conv_done, past(j))
                for rb in range(RB):
                    act.wait_ge(block_done[0], past(RB * k + rb + 1))
                    f(raw[0][:, GDN_CONV - 1 + rb * R:GDN_CONV - 1 + (rb + 1) * R], bank[rb][:, :], ACT.Copy
                      ).then_inc(bank_free[rb], 1)
                act.wait_ge(yc_done, past(j))
                act.wait_ge(stored[1], past(16 * (U_SAVED // 2 + H)))
                for rb in range(RB):
                    act.wait_ge(block_done[1], past(RB * k + (RB + rb + 1)))
                    f(stage[1][:, rb * R:(rb + 1) * R], bank[rb][:, :], ACT.Silu).then_inc(bank_free[rb], 1)
                act.wait_ge(yc_done, past(j + 1))
                act.dma_start(one(y_all, j + 2 * H), stage[0][:, :]).then_inc(stored[0], 16)
            direct(U_SAVED + 4 * H, 3 * KT, ACT.Sigmoid, gates, 0, (U_SAVED // 2 + 2 * H, U_SAVED // 2 + H))
            for rb in range(RB):
                act.wait_ge(block_done[0], past(RB * (UNITS // 2) + rb + 1))
                f(abT[0:2 * H, rb * R:(rb + 1) * R], bank[rb][0:2 * H, :], ACT.Copy).then_inc(bank_free[rb], 1)

            ab = bank[4][:, 0:TILES * 2 * H].rearrange("p (c e) -> p c e", e=2 * H)
            act.wait_ge(tab_v, 1)
            f(tab["beta"][:, :].rearrange("p (c h) -> p c h", h=H), ab[:, :, 0:H], ACT.Sigmoid).then_inc(tab_a, 1)
            f(tab["t1"][:, :], tab["t0"][:, :], ACT.Abs).then_inc(tab_a, 1)
            act.add_instruction(mybir.InstLoadActFuncSet(
                name=nc.get_next_instruction_name(), act_func_set_id=EXP_LN_SET, engine=act.engine))
            act.wait_ge(tab_a, 2)
            f(tab["t1"][:, :], tab["t1"][:, :], ACT.Exp, scale=-1.0).then_inc(tab_a, 1)
            f(head_in[:, 0, :], head_in[:, 0, :], ACT.Exp).then_inc(tab_a, 1)
            act.wait_ge(tab_a, 4)
            f(tab["t1"][:, :], tab["t1"][:, :], ACT.Ln, bias=ones[:, 0:1]).then_inc(tab_a, 1)
            act.wait_ge(tab_v, 5)
            f(tab["k_decay"][:, :], tab["t0"][:, :], ACT.Exp).then_inc(tab_a, 1)
            f(tab["e_last"][:, :], bank[5][:, TILES * H:2 * TILES * H], ACT.Exp).then_inc(tab_a, 1)
            f(tab["t1"][:, :], tab["cum"][:, :], ACT.Exp).then_inc(tab_a, 1)
            act.wait_ge(stored[0], past(16 * (U_SAVED // 2 + 2 * H + 3 * KT // 2)))
            act.wait_ge(stored[1], past(16 * (U_SAVED // 2 + H + 3 * KT // 2)))
            arrive(act, 0)

            def squares(k):
                for p in range(2):
                    act.wait_ge(qkv_loaded[p], past(16 * k + 16))
                    act.wait_ge(G["ss"], past(2 * k))
                    f(sq_qk[p][:, :, :], qkv_in[p][:, 0:2 * H, :], ACT.Square).then_inc(G["sq"], 1)

            def out_squares(c):
                act.wait_ge(G["o_mm"], past(c + 1))
                act.wait_ge(N["sso"], past(c))
                f(sq_o[:, :, :], hp(bank[6]), ACT.Square).then_inc(N["sqo"], 1)

            def out_scale(c):
                act.wait_ge(N["sso"], past(c + 1))
                act.wait_ge(N["on"], past(c))
                f(rs_o[:, :, :], hp(bank[7]), ACT.Ln, scale=1.0 / P, bias=eps[:, 0:1]).then_inc(N["rso_ln"], 1)
                act.wait_ge(N["rso_ln"], past(c + 1))
                f(rs_o[:, :, :], rs_o[:, :, :], ACT.Exp, scale=-0.5).then_inc(N["rso"], 1)

            def save_out(c, k, p):
                act.wait_ge(g_y[p], past(k + 1))
                act.dma_start(y_all[0:H, :, ds(c * P, P)].rearrange("h p r -> p h r"), y_a[:, :, :]
                              ).then_inc(N["y_stored"], 16)

            def chunk_pair(k, kp, first=False, last=False):
                c0 = 2 * k
                for p in range(2):
                    act.wait_ge(G["ss"], past(c0 + p + 1))
                    act.wait_ge(G["qkn"], past(4 * k))
                    for n in range(2):
                        f(rs_qk[p][:, n * H:(n + 1) * H, :], hp(bank[3 * p + n]), ACT.Ln, bias=eps[:, 0:1]
                          ).then_inc(G["rs_ln"], 1)
                    act.wait_ge(G["rs_ln"], past(2 * c0 + 2 * p + 2))
                    f(rs_qk[p][:, :, :], rs_qk[p][:, :, :], ACT.Exp, scale=-0.5).then_inc(G["rs"], 1)
                for p in range(2):
                    act.wait_ge(G["cumb"], past(c0 + p + 1))
                    act.wait_ge(G["qdec"], past(c0))
                    f(e_cum[p][:, :, :], hp(bank[3 * p + 2]), ACT.Exp).then_inc(G["ecum"], 1)
                for p in range(2):
                    act.wait_ge(G["diff"], past(2 * c0 + 2 * p + 2))
                    f(dec[p][:, :, :, :], dec[p][:, :, :, :], ACT.Exp).then_inc(G["decay"], 1)
                if not first:
                    out_squares(c0 - 2)
                for p in range(2):
                    act.wait_ge(G["lowt"], past(c0 + p + 1))
                    act.wait_ge(G["pair"], past(2 * LEVELS * k))
                    f(lowT[p][:, :, :], hp(bank[3 * p + 2]), ACT.Copy).then_inc(G["lowt_sb"], 1)
                if not first:
                    out_scale(c0 - 2)
                for lv in range(1, LEVELS):
                    for p in range(2):
                        act.wait_ge(G["x_mm"], past(level(k, lv, p)))
                        f(X[p][:, :, :], hp(bank[3 * p]), ACT.Copy).then_inc(G["x_sb"], 1)
                    if not first and lv == 2:
                        save_out(c0 - 2, k - 1, 0)
                    if not first and lv == 4:
                        out_squares(c0 - 1)
                    if not first and lv == 5:
                        out_scale(c0 - 1)
                if not last:
                    squares(k + 1)
                if not first:
                    save_out(c0 - 1, k - 1, 1)
                for p in range(2):
                    act.wait_ge(G["vnew"], past(c0))
                    act.wait_ge(G["u_mm"], past(2 * c0 + 2 * p + 1))
                    f(U[p][:, :, :], hp(bank[3 * p]), ACT.Copy).then_inc(G["uw_sb"], 1)
                    act.wait_ge(G["u_mm"], past(2 * c0 + 2 * p + 2))
                    f(WT[p][:, :, :], hp(bank[3 * p + 2]), ACT.Copy).then_inc(G["uw_sb"], 1)

            def last_outs():
                for p in range(2):
                    out_squares(TILES - 2 + p)
                    out_scale(TILES - 2 + p)
                    save_out(TILES - 2 + p, TILES // 2 - 1, p)

            squares(0)
            pairs(act, chunk_pair, last_outs)
            act.wait_ge(N["y_stored"], past(16 * TILES))
            arrive(act, 1)

            with act.Fori(0, H // MAPS) as i:
                for p in range(2):
                    h = 2 * i + p
                    turns = [0]

                    def turned(dst):
                        n = turns[0]
                        turns[0] += 1
                        act.wait_ge(A["turn"], past(TURNS * h + n + 1))
                        w = dst.shape[1]
                        f(dst, bank[4 + n % 2][:, 0:w * P].rearrange("p (k c) -> p k c", c=P), ACT.Copy
                          ).then_inc(turn_free[n % 2], 1)

                    def exps(j):
                        b = ORDER[j]
                        for m in range(MAPS):
                            act.wait_ge(A["negtop"], past(MAPS * (TILES * h + j) + m + 1))
                            n = j % AHEAD
                            s = s_buf[n][:, m, 0:(b + 1) * P]
                            f(s, s, ACT.Exp, bias=neg_top[n][:, m:m + 1], accum_out=den[n][:, m:m + 1]
                              ).then_inc(A["exp"], 1)

                    def out_squares(nth):
                        n = RB * h + nth
                        end = GROUP_END[nth]
                        act.wait_ge(a_pv[end % AHEAD], past(RB * h + end // AHEAD + 1))
                        act.wait_ge(N["on"], past(TILES + n))
                        f(sq_b[:, :], bank[6 + nth % 2][:, :], ACT.Square).then_inc(N["sqo"], 1)

                    def out_scale(nth):
                        n = RB * h + nth
                        t = turns[0]
                        turns[0] += 1
                        act.wait_ge(A["turn"], past(TURNS * h + t + 1))
                        f(rs_b[:, :], bank[4 + t % 2][:, :], ACT.Ln, scale=1.0 / P, bias=eps[:, 0:1]
                          ).then_inc(turn_free[t % 2], 1)
                        act.wait_ge(turn_free[t % 2], past(TURNS // 2 * h + t // 2 + 1))
                        f(rs_b[:, :], rs_b[:, :], ACT.Exp, scale=-0.5).then_inc(N["rso"], 1)

                    def save(nth):
                        sb = GROUPS[nth]
                        act.wait_ge(a_y[p], past(RB * i + nth + 1))
                        act.dma_start(y_all[ds(h + H, 1), :, sb * R:(sb + 1) * R].rearrange("o p r -> p (o r)"),
                                      y_b[:, :]).then_inc(N["y_stored"], 16)

                    act.wait_ge(a_pv[AHEAD - 1], past(RB * h))
                    exps(0)
                    for g in range(RB):
                        turned(v_rows[:, g * RB:(g + 1) * RB, :])
                    exps(1)
                    for j, b in enumerate(ORDER):
                        if j - 1 in GROUP_END:
                            out_squares(GROUP_END.index(j - 1))
                        act.wait_ge(a_pv[(j - 2) % AHEAD], past(RB * h + (j + 2) // AHEAD))
                        for g in range(b // RB + 1):
                            turned(probsT[j % 2][:, g * RB:min((g + 1) * RB, b + 1), :])
                        if j - 1 in GROUP_END:
                            out_scale(GROUP_END.index(j - 1))
                        if j + 2 < TILES:
                            exps(j + 2)
                        if j - 1 in GROUP_END:
                            save(GROUP_END.index(j - 1))
                    out_squares(RB - 1)
                    out_scale(RB - 1)
                    save(RB - 1)
            act.wait_ge(N["y_stored"], past(16 * TILES + 16 * RB * H))
            arrive(act, 2)

            def wb_split(r, n):
                act.wait_ge(wb_loaded[n % 2], past(192 * r + 16 * (n // 2) + 16))
                act.wait_ge(mm_done[n % 3], past(KT * r + n // 3))
                f(wb_hi[n % 3][:, :, :], wb_in[n % 2][:, :, :], ACT.Copy).then_inc(M["wb_hi"], 1)

            def y_split(r, b, src=y_in[:, :, :]):
                act.wait_ge(y_loaded[b], past(16 * r + 16))
                act.wait_ge(mm_done[2], past(KT * r))
                f(y_hi[:, H * b:H * (b + 1), :], src, ACT.Copy).then_inc(M["y_hi"], 1)

            def m_split(r, d):
                act.wait_ge(M["sum2"], past(KT * r + d + 1))
                if d == 0:
                    act.wait_ge(M["out_mm"], past(2 * RB * r))
                f(m_hi[:, d, :], gated[0][:, :], ACT.Copy).then_inc(M["hi"], 1)

            def merge(r, first=False, last=False):
                for d in range(KT):
                    for b in range(3):
                        if first and d == 0:
                            y_split(0, b, y_first[b])
                        wb_split(r, 3 * d + b)
                        if b == 1 and d:
                            m_split(r, d - 1)
                    if first:
                        act.wait_ge(M["wo_loaded"], past(16 * d + 16))
                        f(wo_hi[:, d, :], x_res[d % 2][:, :], ACT.Copy).then_inc(M["wo_hi"], 1)
                m_split(r, KT - 1)
                for t in range(RB):
                    n = RB * r + t
                    if not last and t:
                        y_split(r + 1, t - 1)
                    act.wait_ge(M["done"], past(n))
                    for nb in range(2):
                        act.wait_ge(M["out_mm"], past(2 * n + nb + 1))
                        f(o_norm[:, nb * R:(nb + 1) * R], bank[(6, 0)[t % 2] + nb][:, :], ACT.Square,
                          accum_out=o_stat[:, nb:nb + 1]).then_inc(M["sq"], 1)
                    act.wait_ge(M["ss"], past(n + 1))
                    f(o_stat[:, 3:4], o_stat[:, 2:3], ACT.Sqrt, scale=1.0 / D, bias=eps[:, 0:1]
                      ).then_inc(M["root"], 1)
                    act.wait_ge(M["done"], past(n + 1))
                    act.dma_start(out_rows[ds(n, 1), :, :].rearrange("o p d -> p (o d)"), x_res[t % 2][:, :]
                                  ).then_inc(out_stored[t % 2], 16)

            merge(0, first=True)
            with act.Fori(1, RB - 1) as r:
                merge(r)
            merge(RB - 1, last=True)

        @block.vector
        def _(dve):
            def stt(out_, a, s, b, op0, op1):
                return dve.scalar_tensor_tensor(out_, a, s, b, op0, op1)

            def tt(out_, a, b, op):
                return dve.tensor_tensor(out_, a, b, op)

            dve.wait_ge(vec_ready, 1)
            dve.tensor_copy(vec[:, :], bank[0][:, 0:VECS]).then_inc(vec_ready, 1)
            dve.wait_ge(vec_ready, 2)
            dve.tensor_scalar(diff_w[:, :], vec[:, VEC_DIFF:VEC_DIFF + 1], 1.0 - LAM_INIT, None, ALU.mult
                              ).then_inc(vec_ready, 1)
            for m in range(2):
                dve.tensor_tensor_reduce(lam_in[:, 2 * m, :], lam_in[:, 2 * m, :], lam_in[:, 2 * m + 1, :], 1.0, 0.0,
                                         ALU.mult, ALU.add, lam_s[:, m:m + 1]).then_inc(lam_step, 1)

            def scale_rows(i, q):
                t = 4 * i + q
                dve.wait_ge(x_root, past(t + 1))
                dve.reciprocal(x_stat[:, q, 2:3], x_stat[:, q, 1:2]).then_inc(x_inv, 1)
                dve.wait_ge(x_inv, past(t + 1))
                stt(x_in[q][:, :], x_in[q][:, :], x_stat[:, q, 2:3], pre_w[:, :], ALU.mult, ALU.mult
                    ).then_inc(x_scaled, 1)

            def take_lo(i, q):
                t = 4 * i + q
                for n in range(2):
                    dve.wait_ge(h_hi_done, past(2 * t + n + 1))
                    part = slice(4 * n, 4 * n + 4)
                    tt(hT_lo[:, part, ds(t * P, P)], hp(bank[4 + 2 * (q % 2) + n]),
                       hT_hi[:, part, ds(t * P, P)].bitcast(F32), ALU.subtract).then_inc(h_lo_done[q % 2], 1)

            scale_rows(0, 0)
            scale_rows(0, 1)
            with dve.Fori(0, TILES // 4 - 1) as i:
                for q in range(4):
                    take_lo(i, q)
                    scale_rows(i + (q + 2) // 4, (q + 2) % 4)
            last_i = TILES // 4 - 1
            for q in range(4):
                take_lo(last_i, q)
                if q < 2:
                    scale_rows(last_i, q + 2)
            dve.wait_ge(x_scaled, past(TILES))
            for p in range(2):
                dve.memset(raw[p][:, 0:GDN_CONV - 1], 0.0).then_inc(raw_zero, 1)
            dve.wait_ge(lam_step, 3)
            tt(neg_lam[:, :], lam_s[:, 3:4], lam_s[:, 2:3], ALU.subtract).then_inc(lam_step, 1)
            dve.wait_ge(lam_step, 4)
            dve.tensor_scalar(neg_lam[:, :], neg_lam[:, :], -LAM_INIT, None, ALU.add).then_inc(lam_step, 1)

            dve.wait_ge(raw_zero, 2)
            dve.wait_ge(vec_ready, 3)
            with dve.Fori(0, U_ZA // 2) as i:
                for p in range(2):
                    u = 2 * i + p
                    dve.wait_ge(bank_free[RB - 1], past(u + 1))
                    dve.wait_ge(stored[p], past(16 * i))
                    dve.tensor_scalar(stage[p][:, :], raw[p][:, 0:SEQ], vec[:, ds(u, 1)], None, ALU.mult
                                      ).then_inc(conv_step, 1)
                    for tap in range(1, GDN_CONV):
                        dve.wait_ge(conv_step, past((GDN_CONV - 1) * u + tap))
                        last = stt(stage[p][:, :], raw[p][:, tap:tap + SEQ], vec[:, ds(u + 12 * tap, 1)],
                                   stage[p][:, :], ALU.mult, ALU.add)
                        if tap < GDN_CONV - 1:
                            last.then_inc(conv_step, 1)
                    last.then_inc(conv_done[p], 1)

            for unit, scale in ((U_Q, QK_DIM ** -0.5), (U_K, 1.0)):
                with dve.Fori(0, H // 2) as i:
                    for p in range(2):
                        before = (unit - U_Q) // 2
                        dve.wait_ge(conv_done[p], past(U_ZA // 2))
                        dve.wait_ge(stored[p], past(32 * i + (16 * (U_Q // 2) + 32 * before)))
                        for rb in range(RB):
                            cols = slice(rb * R, (rb + 1) * R)
                            dve.wait_ge(staged, past(RB * 2 * i + (U_ZA + RB * (unit - U_Q + p) + rb + 1)))
                            stt(raw[p][:, GDN_CONV - 1 + rb * R:GDN_CONV - 1 + (rb + 1) * R].bitcast(F32R),
                                bank[rb][:, :], scale, stage[p][:, cols], ALU.mult, ALU.subtract
                                ).then_inc(bank_free[rb], 1)

            with dve.Fori(0, H) as j:
                k = 2 * j + U_SAVED // 2
                u = 4 * j + U_SAVED
                for rb in range(RB):
                    dve.wait_ge(block_done[1], past(RB * k + rb + 1))
                    dve.wait_ge(bank_free[rb], past(u + 1))
                    part = raw[0][:, GDN_CONV - 1 + rb * R:GDN_CONV - 1 + (rb + 1) * R]
                    tt(part, part, bank[rb][:, :], ALU.mult).then_inc(bank_free[rb], 1)
                dve.wait_ge(bank_free[RB - 1], past(u + 2))
                for tap in range(SC_CONV):
                    src = raw[0][:, GDN_CONV - SC_CONV + tap:GDN_CONV - SC_CONV + tap + SEQ]
                    w = vec[:, ds(j + (VEC_SC + H * tap), 1)]
                    if tap == 0:
                        dve.tensor_scalar(conv[:, :], src, w, None, ALU.mult).then_inc(sc_step, 1)
                        continue
                    dve.wait_ge(sc_step, past((SC_CONV - 1) * j + tap))
                    last = stt(conv[:, :], src, w, conv[:, :], ALU.mult, ALU.add)
                    last.then_inc(sc_step if tap < SC_CONV - 1 else sc_conv_done, 1)
                dve.wait_ge(sc_conv_done, past(j + 1))
                for rb in range(RB):
                    dve.wait_ge(block_done[0], past(RB * k + (RB + rb + 1)))
                    part = conv[:, rb * R:(rb + 1) * R]
                    tt(part, part, bank[rb][:, :], ALU.mult).then_inc(bank_free[rb], 1)
                dve.wait_ge(bank_free[RB - 1], past(u + 4))
                dve.wait_ge(stored[0], past(16 * (j + (U_SAVED // 2 + H))))
                tt(stage[0][:, :], conv[:, :], stage[1][:, :], ALU.mult).then_inc(yc_done, 1)

            def by_chunk(t):
                return t[:, :].rearrange("p (c h) -> p c h", h=H)

            ab = bank[4][:, 0:TILES * 2 * H].rearrange("p (c e) -> p c e", e=2 * H)
            dve.wait_ge(ab_turned, 1)
            tt(by_chunk(tab["t0"]), ab[:, :, H:2 * H], head_in[:, 1:2, :].to_broadcast([P, TILES, H]), ALU.add
               ).then_inc(tab_v, 1)
            dve.wait_ge(tab_a, 5)
            stt(tab["t0"][:, :], tab["t0"][:, :], 0.0, tab["t1"][:, :], ALU.max, ALU.add).then_inc(tab_v, 1)
            dve.wait_ge(tab_v, 2)
            stt(by_chunk(tab["g"]), by_chunk(tab["t0"]), -1.0, head_in[:, 0:1, :].to_broadcast([P, TILES, H]),
                ALU.mult, ALU.mult).then_inc(tab_v, 1)
            dve.wait_ge(tab_mm, 1)
            dve.tensor_copy(tab["cum"][:, :], bank[5][:, 0:TILES * H]).then_inc(tab_v, 1)
            dve.wait_ge(tab_v, 4)
            tt(tab["t0"][:, :], bank[5][:, TILES * H:2 * TILES * H], tab["cum"][:, :], ALU.subtract
               ).then_inc(tab_v, 1)
            dve.wait_ge(tab_a, 8)
            tt(tab["beta_ecum"][:, :], tab["beta"][:, :], tab["t1"][:, :], ALU.mult).then_inc(tab_v, 1)
            arrive(dve, 0)

            def bc(t, c):
                return t[:, ds(H * c, H)].rearrange("p (h o) -> p h o", o=1).to_broadcast([P, H, P])

            def per_head(m):
                return m.rearrange("p (o c) -> p o c", o=1).to_broadcast([P, H, P])

            def new_v(c, p):
                dve.wait_ge(G["ws"], past(c + 1))
                dve.wait_ge(G["o_mm"], past(c))
                tt(v_new[:, :, :], U[p][:, :, :], hp(bank[6]), ALU.subtract).then_inc(G["vnew"], 1)

            def new_state(c, p):
                dve.wait_ge(G["s_mm"], past(c + 1))
                dve.wait_ge(G["sdec"], past(c + 1))
                tt(state[1 - p][:, :, :], state_d[:, :, :], hp(bank[7]), ALU.add).then_inc(G["state"], 1)

            def norm_out(c, q):
                dve.wait_ge(N["rso"], past(c + 1))
                dve.wait_ge(N["y_stored"], past(16 * c))
                tt(y_a[:, :, :], hp(bank[6]), rs_o[:, :, :], ALU.mult).then_inc(N["on"], 1)
                dve.wait_ge(N["on"], past(c + 1))
                stt(y_a[:, :, :], y_a[:, :, :], vec[:, VEC_GDN:VEC_GDN + 1], za_in[q][:, :, :],
                    ALU.mult, ALU.mult).then_inc(g_y[q % 2], 1)

            def chunk_pair(k, kp, first=False, last=False):
                c0 = 2 * k
                old, old_q = c0 - 2, 2 * (1 - kp)
                if not first:
                    new_v(old, 0)
                for p in range(2):
                    dve.wait_ge(G["rs"], past(c0 + p + 1))
                    dve.wait_ge(qkv_loaded[p], past(16 * k + 16))
                    dve.wait_ge(G["kk"], past(4 * k))
                    dve.wait_ge(G["qdec"], past(c0))
                    tt(qkn[p][:, H:2 * H, :], qkv_in[p][:, H:2 * H, :], rs_qk[p][:, H:2 * H, :], ALU.mult
                       ).then_inc(G["qkn"], 1)
                    stt(qkn[p][:, 0:H, :], qkv_in[p][:, 0:H, :], P ** -0.5, rs_qk[p][:, 0:H, :], ALU.mult,
                        ALU.mult).then_inc(G["qkn"], 1)
                for p in range(2):
                    dve.wait_ge(G["mask"], past(2 * c0 + 2 * p + 2))
                    dve.wait_ge(G["ecum"], past(c0 + p + 1))
                    cum = hp(bank[3 * p + 2])
                    tt(dec[p][:, 0, :, :], dec[p][:, 0, :, :], cum, ALU.subtract).then_inc(G["diff"], 1)
                    tt(dec[p][:, 1, :, :], dec[p][:, 1, :, :], cum, ALU.add).then_inc(G["diff"], 1)
                for p in range(2):
                    dve.wait_ge(G["turn"], past(4 * k + p + 1))
                    dve.wait_ge(G["u_mm"], past(4 * k))
                    tt(v_beta[p][:, :, :], hp(bank[3 * p]), bc(tab["beta"], c0 + p), ALU.mult
                       ).then_inc(G["rows"], 1)
                if not first:
                    new_state(old, 0)
                for p in range(2):
                    dve.wait_ge(G["kk"], past(4 * k + p + 1))
                    dve.wait_ge(G["decay_b"], past(c0 + p + 1))
                    dve.wait_ge(G["lowt"], past(c0))
                    tt(low[p][:, :, :], hp(bank[3 * p + 2]), dec[p][:, 0, :, :], ALU.mult
                       ).then_inc(G["masked"], 1)
                for p in range(2):
                    dve.wait_ge(G["kk"], past(4 * k + p + 3))
                    tt(qk_m[2 * kp + p][:, :, :], hp(bank[3 * p]), dec[p][:, 1, :, :], ALU.mult
                       ).then_inc(G["masked"], 1)
                for p in range(2):
                    dve.wait_ge(G["masked"], past(4 * k + p + 1))
                    tt(T[p][:, :, :], low[p][:, :, :], per_head(pair1[:, :]), ALU.mult).then_inc(G["t0"], 1)
                    dve.wait_ge(G["t0"], past(2 * c0 + 2 * p + 1))
                    tt(T[p][:, :, :], per_head(ident[:, :]), T[p][:, :, :], ALU.subtract).then_inc(G["t0"], 1)
                for p in range(2):
                    dve.wait_ge(G["turn"], past(4 * k + p + 3))
                    tt(k_beta[p][:, :, :], hp(bank[3 * p + 1]), bc(tab["beta_ecum"], c0 + p), ALU.mult
                       ).then_inc(G["rows"], 1)
                    tt(k_dec[2 * kp + p][:, :, :], hp(bank[3 * p + 1]), bc(tab["k_decay"], c0 + p), ALU.mult
                       ).then_inc(G["rows"], 1)
                for lv in range(1, LEVELS):
                    for p in range(2):
                        if lv < LEVELS - 1:
                            dve.wait_ge(G["y_mm"], past(level_y(k, lv, p, 0)))
                            tt(T[p][:, :, :], T[p][:, :, :], hp(bank[3 * p + 2]), ALU.subtract)
                        dve.wait_ge(G["y_mm"], past(level_y(k, lv, p, 1)))
                        tt(Tt[p][:, :, :], Tt[p][:, :, :], hp(bank[3 * p + 1]), ALU.subtract
                           ).then_inc(G["t_new"], 1)
                        if p == 0 and not first:
                            if lv == 1:
                                dve.wait_ge(za_loaded[1 - kp], past(16 * (k + kp)))
                                norm_out(old, old_q)
                            if lv == 6:
                                norm_out(old + 1, old_q + 1)
                    if not first and lv == 2:
                        new_v(old + 1, 1)
                    if not first and lv == 3:
                        new_state(old + 1, 1)

            def last_chunks():
                dve.wait_ge(za_loaded[1], past(8 * TILES))
                for p in range(2):
                    c = TILES - 2 + p
                    new_v(c, p)
                    new_state(c, p)
                    norm_out(c, 2 + p)

            pairs(dve, chunk_pair, last_chunks)
            arrive(dve, 1)

            with dve.Fori(0, H // MAPS) as i:
                for p in range(2):
                    h = 2 * i + p
                    scored = [0]

                    def biased(j, m):
                        b = ORDER[j]
                        bp = j % AHEAD
                        groups = b // RB + 1
                        if m == 0:
                            dve.wait_ge(a_pv[bp], past(RB * h + j // AHEAD))
                        for g in range(groups):
                            n = scored[0]
                            scored[0] += 1
                            w = min(R, (b + 1) * P - g * R)
                            at = SEQ - P - b * P + g * R
                            dve.wait_ge(A["score"], past(SCORES * h + n + 1))
                            wait_apart(dve)
                            dve.tensor_tensor_reduce(
                                s_buf[bp][:, m, g * R:g * R + w], bank[n % SCORE_BANKS][:, 0:w],
                                bias[p][:, at:at + w], 1.0, -3e38, ALU.add, ALU.max, top[bp][:, m, g:g + 1]
                            ).then_inc(score_free, 1)
                        dve.wait_ge(score_free, past(SCORES * h + scored[0]))
                        dve.tensor_reduce(top_all[bp][:, m:m + 1], top[bp][:, m, 0:groups], AX.X, ALU.max
                                          ).then_inc(A["top"], 1)
                        dve.wait_ge(A["top"], past(MAPS * (TILES * h + j) + m + 1))
                        dve.tensor_scalar(neg_top[bp][:, m:m + 1], top_all[bp][:, m:m + 1], -1.0, None, ALU.mult
                                          ).then_inc(A["negtop"], 1)

                    def invert(j):
                        bp = j % AHEAD
                        n = TILES * h + j
                        dve.wait_ge(A["exp"], past(2 * n + 2))
                        dve.reciprocal(inv[bp][:, :], den[bp][:, :]).then_inc(A["mix"], 1)
                        dve.wait_ge(A["mix"], past(2 * n + 1))
                        tt(sub_w[bp][:, 0:1], inv[bp][:, 1:2], neg_lam[:, :], ALU.mult).then_inc(A["mix"], 1)

                    def combine(j):
                        bp = j % AHEAD
                        n = TILES * h + j
                        w = (ORDER[j] + 1) * P
                        s0, s1 = s_buf[bp][:, 0, 0:w], s_buf[bp][:, 1, 0:w]
                        dve.wait_ge(A["scaled"], past(n + 1))
                        stt(s0, s0, inv[bp][:, 0:1], s1, ALU.mult, ALU.add).then_inc(A["probs"], 1)

                    def finish(nth):
                        n = RB * h + nth
                        sb = GROUPS[nth]
                        dve.wait_ge(N["rso"], past(TILES + n + 1))
                        dve.wait_ge(N["y_stored"], past(16 * TILES + 16 * n))
                        dve.wait_ge(head_loaded[p], past(32 * i + 32))
                        tt(y_b[:, :], bank[6 + nth % 2][:, :], rs_b[:, :], ALU.mult).then_inc(N["on"], 1)
                        dve.wait_ge(N["on"], past(TILES + n + 1))
                        stt(y_b[:, :], y_b[:, :], diff_w[:, 0:1], zb_in[p][:, sb * R:(sb + 1) * R],
                            ALU.mult, ALU.mult).then_inc(a_y[p], 1)

                    dve.wait_ge(A["dist"], past(2 * h + 4))
                    for j in range(2):
                        for m in range(MAPS):
                            biased(j, m)
                    invert(0)
                    for j in range(TILES):
                        combine(j)
                        if j + 2 < TILES:
                            biased(j + 2, 0)
                        if j + 1 < TILES:
                            invert(j + 1)
                        if j + 2 < TILES:
                            biased(j + 2, 1)
                        if j - 1 in GROUP_END:
                            finish(GROUP_END.index(j - 1))
                    finish(RB - 1)
            arrive(dve, 2)

            def y_split(r, b, src=y_in[:, :, :]):
                dve.wait_ge(M["y_hi"], past(3 * r + b + 1))
                tt(y_lo[:, H * b:H * (b + 1), :], src,
                   y_hi[:, H * b:H * (b + 1), :].bitcast(F32), ALU.subtract).then_inc(M["y_lo"], 1)

            def merge(r, first=False, last=False):
                for d in range(KT):
                    for b in range(3):
                        n = 3 * d + b
                        dve.wait_ge(mm_done[b], past(KT * r + d + 1))
                        dve.wait_ge(gate_loaded[b], past(128 * r + 16 * d + 16))
                        dve.wait_ge(M["lo"], past(KT * r + d))
                        tt(gated[b][:, :], bank[(n + 2) % 6][:, :], gate_in[b][:, :], ALU.mult
                           ).then_inc(gated_done[n % 6], 1)
                        if b == 1:
                            dve.wait_ge(gated_done[n % 6], past(KT // 2 * r + d // 2 + 1))
                            tt(gated[1][:, :], gated[0][:, :], gated[1][:, :], ALU.add).then_inc(M["sum1"], 1)
                    if first:
                        if d == 1:
                            dve.wait_ge(M["post"], past(16))
                        dve.wait_ge(M["wo_hi"], past(d + 1))
                        tt(wo_lo[:, d, :], x_res[d % 2][:, :], wo_hi[:, d, :].bitcast(F32), ALU.subtract
                           ).then_inc(M["wo_lo"], 1)
                    dve.wait_ge(M["hi"], past(KT * r + d + 1))
                    tt(m_lo[:, d, :], gated[0][:, :], m_hi[:, d, :].bitcast(F32), ALU.subtract).then_inc(M["lo"], 1)
                for t in range(RB):
                    n = RB * r + t
                    if not last and t:
                        y_split(r + 1, t - 1)
                    dve.wait_ge(M["sq"], past(2 * n + 2))
                    tt(o_stat[:, 2:3], o_stat[:, 0:1], o_stat[:, 1:2], ALU.add).then_inc(M["ss"], 1)
                    dve.wait_ge(M["root"], past(n + 1))
                    dve.reciprocal(o_stat[:, 4:5], o_stat[:, 3:4]).then_inc(M["inv"], 1)
                    dve.wait_ge(M["inv"], past(n + 1))
                    for nb in range(2):
                        cols = slice(nb * R, (nb + 1) * R)
                        last_op = stt(o_norm[:, cols], bank[(6, 0)[t % 2] + nb][:, :], o_stat[:, 4:5],
                                      post_w[:, cols], ALU.mult, ALU.mult)
                    last_op.then_inc(M["normed"], 1)
                    dve.wait_ge(M["normed"], past(n + 1))
                    dve.wait_ge(x_res_loaded[t % 2], past(32 * r + 16 * (t // 2) + 16))
                    tt(x_res[t % 2][:, :], x_res[t % 2][:, :], o_norm[:, :], ALU.add).then_inc(M["done"], 1)

            for b in range(3):
                y_split(0, b, y_first[b])
            merge(0, first=True)
            with dve.Fori(1, RB - 1) as r:
                merge(r)
            merge(RB - 1, last=True)


_INS = ["x", "norm_pre", "norm_post", "w_in", "gdn_conv_w", "gdn_a_log", "gdn_dt_bias", "gdn_norm_w",
        "diff_lambda", "diff_norm_w", "sc_conv_w", "w_branch", "w_out"]


def kernel(**inputs):
    import numpy as np
    import concourse.bacc as bacc
    from concourse.bass_utils import run_bass_kernel_spmd

    nc = bacc.Bacc("TRN2", target_bir_lowering=False, num_devices=1)
    arrays, args = {}, []
    for name in _INS:
        a = np.ascontiguousarray(inputs[name])
        arrays[f"in_{name}"] = a
        args.append(nc.dram_tensor(f"in_{name}", a.shape, mybir.dt.from_np(a.dtype), kind="ExternalInput").ap())
    out = nc.dram_tensor("out_x", (1, SEQ, D), F32, kind="ExternalOutput").ap()
    hybrid_block(nc, *args, out)
    r = run_bass_kernel_spmd(nc, [arrays], core_ids=[0])
    return r.results[0]["out_x"]
```
